# Optimizing a Trainium2 kernel written in Bass

```python
import math
import jax, jax.numpy as jnp
from jax import lax
import numpy as np

D_MODEL = 1024
BATCH = 1
SEQ = 512
DEPTH = 2

CTX_LEN = 256
GRID_W = 64
EPS = 1e-6
ROPE_BASE = 10000.0
D_FF = 4 * D_MODEL
GDN_HEADS = 4
GDN_DK = 128
GDN_DV = 128
GDN_CHUNK = 64
CONV_W = 5
MLA_HEADS = 4
MLA_Q_RANK = 256
MLA_KV_RANK = 128
MLA_NOPE = 64
MLA_ROPE = 32
MLA_DV = 64
Q_BLOCK = 128
HG_HEADS = 4
HG_DK = 128
HG_DV = 64
HG_CHUNK = 32
D_MIX = GDN_HEADS * GDN_DV + MLA_HEADS * MLA_DV + HG_HEADS * HG_DV
IN_SIZES = (GDN_HEADS * GDN_DK, GDN_HEADS * GDN_DK, GDN_HEADS * GDN_DV, GDN_HEADS * GDN_DV, 2 * GDN_HEADS, 2 * GDN_HEADS,
            MLA_Q_RANK, MLA_KV_RANK, MLA_ROPE,
            HG_HEADS * HG_DK, HG_HEADS * HG_DK, HG_HEADS * HG_DK, HG_HEADS * HG_DV, HG_HEADS * HG_DV)
D_IN = sum(IN_SIZES)

kernel_name = "hybrid_gdn_mla_hgrn2_dit_block"

F32 = jnp.float32

def split_cols(z, sizes):
    return jnp.split(z, np.cumsum(np.array(sizes))[:-1].tolist(), axis=-1)

def rms_norm(x, g):
    xf = x.astype(F32)
    y = xf * lax.rsqrt(jnp.mean(xf * xf, axis=-1, keepdims=True) + EPS)
    return (y * g.astype(F32)).astype(x.dtype)

def l2_norm(x):
    xf = x.astype(F32)
    return xf * lax.rsqrt(jnp.sum(xf * xf, axis=-1, keepdims=True) + EPS)

def modulate(h, shift, scale):
    return h * (1.0 + scale) + shift

def short_conv(u, w):
    y = lax.conv_general_dilated(u, w[:, None, :].astype(u.dtype), window_strides=(1,),
                                 padding=[(CONV_W // 2, CONV_W // 2)],
                                 dimension_numbers=("NWC", "WIO", "NWC"),
                                 feature_group_count=u.shape[-1])
    return jax.nn.silu(y)

def axial_rope(rows, dim):
    per_axis = dim // 2
    inv = ROPE_BASE ** (-jnp.arange(0, per_axis, 2, dtype=F32) / per_axis)
    row = jnp.repeat(jnp.arange(rows, dtype=F32), GRID_W)
    col = jnp.tile(jnp.arange(GRID_W, dtype=F32), rows)
    ang = jnp.concatenate([row[:, None] * inv, col[:, None] * inv], axis=-1)
    return jnp.cos(ang), jnp.sin(ang)

def apply_rope(t, cos, sin):
    half = t.shape[-1] // 2
    t1 = t[..., :half].astype(F32)
    t2 = t[..., half:].astype(F32)
    return jnp.concatenate([t1 * cos - t2 * sin, t1 * sin + t2 * cos], axis=-1).astype(t.dtype)

def to_chunks(t, chunk):
    b, l, h = t.shape[:3]
    t = t.reshape((b, l // chunk, chunk, h) + t.shape[3:])
    return jnp.swapaxes(jnp.moveaxis(t, 1, 0), 2, 3)

def from_chunks(t):
    n, b, h, c = t.shape[:4]
    t = jnp.moveaxis(jnp.swapaxes(t, 2, 3), 0, 1)
    return t.reshape((b, n * c, h) + t.shape[4:])

def gdn_scan(q, k, v, log_a, beta, s0, want_out):
    kc = to_chunks(k.astype(F32), GDN_CHUNK)
    vc = to_chunks(v.astype(F32), GDN_CHUNK)
    bc = to_chunks(beta.astype(F32), GDN_CHUNK)
    gcum = jnp.cumsum(to_chunks(log_a.astype(F32), GDN_CHUNK), axis=-1)
    idx = jnp.arange(GDN_CHUNK)
    incl = idx[:, None] >= idx[None, :]
    strict = idx[:, None] > idx[None, :]
    decay = jnp.exp(jnp.where(incl, gcum[..., :, None] - gcum[..., None, :], -jnp.inf))
    kb = kc * bc[..., None]
    lower = jnp.where(strict, jnp.einsum("nbhid,nbhjd->nbhij", kb, kc) * decay, 0.0)
    eye = jnp.eye(GDN_CHUNK, dtype=F32)
    t_inv = lax.linalg.triangular_solve(eye + lower, jnp.broadcast_to(eye, lower.shape),
                                        left_side=True, lower=True, unit_diagonal=True)
    u = jnp.einsum("nbhij,nbhjd->nbhid", t_inv, vc * bc[..., None])
    w = jnp.einsum("nbhij,nbhjd->nbhid", t_inv, kb * jnp.exp(gcum)[..., None])
    g_last = gcum[..., -1]
    k_end = kc * jnp.exp(g_last[..., None] - gcum)[..., None]
    if want_out:
        qc = to_chunks(q.astype(F32), GDN_CHUNK)
        q_att = jnp.einsum("nbhid,nbhjd->nbhij", qc, kc) * decay
        q_dec = qc * jnp.exp(gcum)[..., None]
        xs = (u, w, k_end, g_last, q_att, q_dec)
    else:
        xs = (u, w, k_end, g_last)

    def step(s, inp):
        v_new = inp[0] - jnp.einsum("bhcd,bhde->bhce", inp[1], s)
        s_next = s * jnp.exp(inp[3])[..., None, None] + jnp.einsum("bhcd,bhce->bhde", inp[2], v_new)
        if want_out:
            o = jnp.einsum("bhcd,bhde->bhce", inp[5], s) + jnp.einsum("bhij,bhje->bhie", inp[4], v_new)
            return s_next, o
        return s_next, None

    s_fin, o = lax.scan(step, s0, xs)
    return (from_chunks(o) if want_out else None), s_fin

def gdn_mixer(pc, px, conv_w, a_log, dt_bias, norm_g, want_ctx):
    def prep(q, k, v, b_raw, a_raw):
        b, l = q.shape[:2]
        qkv = short_conv(jnp.concatenate([q, k, v], axis=-1), conv_w)
        q, k, v = split_cols(qkv, (GDN_HEADS * GDN_DK, GDN_HEADS * GDN_DK, GDN_HEADS * GDN_DV))
        q = l2_norm(q.reshape(b, l, GDN_HEADS, GDN_DK)) * GDN_DK ** -0.5
        k = l2_norm(k.reshape(b, l, GDN_HEADS, GDN_DK))
        v = v.reshape(b, l, GDN_HEADS, GDN_DV)
        beta = jax.nn.sigmoid(b_raw.astype(F32)).reshape(b, l, 2, GDN_HEADS)
        log_a = -jnp.exp(a_log.astype(F32)) * jax.nn.softplus(
            a_raw.astype(F32).reshape(b, l, 2, GDN_HEADS) + dt_bias.astype(F32))
        return q, k, v, beta, log_a

    cq, ck, cv, cbeta, cla = prep(pc[0], pc[1], pc[2], pc[4], pc[5])
    xq, xk, xv, xbeta, xla = prep(px[0], px[1], px[2], px[4], px[5])
    bsz = xq.shape[0]
    outs_x, outs_c = [], []
    for d in range(2):
        fl = (lambda t: jnp.flip(t, axis=1)) if d == 1 else (lambda t: t)
        s0 = jnp.zeros((bsz, GDN_HEADS, GDN_DK, GDN_DV), F32)
        oc, s_ctx = gdn_scan(fl(cq), fl(ck), fl(cv), fl(cla[:, :, d]), fl(cbeta[:, :, d]), s0, want_ctx)
        ox, _ = gdn_scan(fl(xq), fl(xk), fl(xv), fl(xla[:, :, d]), fl(xbeta[:, :, d]), s_ctx, True)
        outs_x.append(fl(ox))
        if want_ctx:
            outs_c.append(fl(oc))

    def readout(o, gate):
        b, l = gate.shape[:2]
        y = rms_norm(o, norm_g) * jax.nn.silu(gate.astype(F32).reshape(b, l, GDN_HEADS, GDN_DV))
        return y.reshape(b, l, GDN_HEADS * GDN_DV).astype(gate.dtype)

    y_x = readout(outs_x[0] + outs_x[1], px[3])
    y_c = readout(outs_c[0] + outs_c[1], pc[3]) if want_ctx else None
    return y_x, y_c

def mla_kv(ckv, kr, kv_norm_g, w_ukv, cos, sin):
    b, l = ckv.shape[:2]
    kv = (rms_norm(ckv, kv_norm_g) @ w_ukv).reshape(b, l, MLA_HEADS, MLA_NOPE + MLA_DV)
    if cos is not None:
        kr = apply_rope(kr, cos, sin)
    k_rope = jnp.broadcast_to(kr[:, :, None, :], (b, l, MLA_HEADS, MLA_ROPE))
    return jnp.concatenate([kv[..., :MLA_NOPE], k_rope], axis=-1), kv[..., MLA_NOPE:]

def mla_q(cq, q_norm_g, w_uq, cos, sin):
    b, l = cq.shape[:2]
    q = (rms_norm(cq, q_norm_g) @ w_uq).reshape(b, l, MLA_HEADS, MLA_NOPE + MLA_ROPE)
    if cos is not None:
        q = jnp.concatenate([q[..., :MLA_NOPE], apply_rope(q[..., MLA_NOPE:], cos[:, None], sin[:, None])], axis=-1)
    return q

def block_attention(q, k, v):
    b, lq, h, dq = q.shape
    qb = jnp.moveaxis(q.reshape(b, lq // Q_BLOCK, Q_BLOCK, h, dq), 1, 0)
    scale = dq ** -0.5

    def one(qblk):
        s = jnp.einsum("bqhd,bkhd->bhqk", qblk, k).astype(F32) * scale
        p = jax.nn.softmax(s, axis=-1).astype(v.dtype)
        return jnp.einsum("bhqk,bkhd->bqhd", p, v)

    o = lax.map(one, qb)
    return jnp.moveaxis(o, 0, 1).reshape(b, lq, h * v.shape[-1])

def mla_mixer(pc, px, q_norm_g, kv_norm_g, w_uq, w_ukv, cos, sin, want_ctx):
    kc, vc = mla_kv(pc[1], pc[2], kv_norm_g, w_ukv, None, None)
    kx, vx = mla_kv(px[1], px[2], kv_norm_g, w_ukv, cos, sin)
    qx = mla_q(px[0], q_norm_g, w_uq, cos, sin)
    y_x = block_attention(qx, jnp.concatenate([kc, kx], axis=1), jnp.concatenate([vc, vx], axis=1))
    y_c = block_attention(mla_q(pc[0], q_norm_g, w_uq, None, None), kc, vc) if want_ctx else None
    return y_x, y_c

def hgrn_scan(q, k, v, log_f, s0, want_out):
    if want_out:
        xs = (to_chunks(k, HG_CHUNK), to_chunks(v, HG_CHUNK), to_chunks(log_f, HG_CHUNK), to_chunks(q, HG_CHUNK))
    else:
        xs = (to_chunks(k, HG_CHUNK), to_chunks(v, HG_CHUNK), to_chunks(log_f, HG_CHUNK))
    idx = jnp.arange(HG_CHUNK)
    incl = idx[:, None] >= idx[None, :]

    def step(s, inp):
        k_n, v_n, lf_n = inp[0], inp[1], inp[2]
        bcum = jnp.cumsum(lf_n, axis=2)
        b_last = bcum[:, :, -1]
        s_next = s * jnp.exp(b_last)[..., None] + jnp.einsum(
            "bhcd,bhce->bhde", k_n * jnp.exp(b_last[:, :, None] - bcum), v_n)
        if want_out:
            q_n = inp[3]
            dec = jnp.exp(jnp.where(incl[:, :, None], bcum[:, :, :, None, :] - bcum[:, :, None, :, :], -jnp.inf))
            att = jnp.einsum("bhid,bhjd,bhijd->bhij", q_n, k_n, dec)
            o = jnp.einsum("bhcd,bhde->bhce", q_n * jnp.exp(bcum), s) + jnp.einsum("bhij,bhje->bhie", att, v_n)
            return s_next, o
        return s_next, None

    s_fin, o = lax.scan(step, s0, xs)
    return (from_chunks(o) if want_out else None), s_fin

def hgrn_mixer(pc, px, lb, norm_g, want_ctx):
    lbf = lb.astype(F32).reshape(2, HG_HEADS, HG_DK)

    def prep(q, f_fwd, f_bwd, i):
        b, l = q.shape[:2]
        q = q.astype(F32).reshape(b, l, HG_HEADS, HG_DK) * HG_DK ** -0.5
        i = i.astype(F32).reshape(b, l, HG_HEADS, HG_DV)
        log_fs = [jnp.logaddexp(jnp.log(lbf[d]), jnp.log1p(-lbf[d]) +
                                jax.nn.log_sigmoid(fr.astype(F32).reshape(b, l, HG_HEADS, HG_DK)))
                  for d, fr in enumerate((f_fwd, f_bwd))]
        return q, i, log_fs

    cq, ci, clf = prep(pc[0], pc[1], pc[2], pc[3])
    xq, xi, xlf = prep(px[0], px[1], px[2], px[3])
    bsz = xq.shape[0]
    outs_x, outs_c = [], []
    for d in range(2):
        fl = (lambda t: jnp.flip(t, axis=1)) if d == 1 else (lambda t: t)
        s0 = jnp.zeros((bsz, HG_HEADS, HG_DK, HG_DV), F32)
        oc, s_ctx = hgrn_scan(fl(cq), fl(-jnp.expm1(clf[d])), fl(ci), fl(clf[d]), s0, want_ctx)
        ox, _ = hgrn_scan(fl(xq), fl(-jnp.expm1(xlf[d])), fl(xi), fl(xlf[d]), s_ctx, True)
        outs_x.append(fl(ox))
        if want_ctx:
            outs_c.append(fl(oc))

    def readout(o, gate):
        b, l = gate.shape[:2]
        y = rms_norm(o, norm_g) * jax.nn.silu(gate.astype(F32).reshape(b, l, HG_HEADS, HG_DV))
        return y.reshape(b, l, HG_HEADS * HG_DV).astype(gate.dtype)

    y_x = readout(outs_x[0] + outs_x[1], px[4])
    y_c = readout(outs_c[0] + outs_c[1], pc[4]) if want_ctx else None
    return y_x, y_c

def mixing_layer(hx, hc, w_in_l, w_out_l, gdn_conv_l, gdn_a_log_l, gdn_dt_bias_l, gdn_norm_l,
                 mla_q_norm_l, mla_kv_norm_l, mla_w_uq_l, mla_w_ukv_l, lb_l, hgrn_norm_l, cos, sin, want_ctx):
    zx = split_cols(hx @ w_in_l, IN_SIZES)
    zc = split_cols(hc @ w_in_l, IN_SIZES)
    gdn_x, gdn_c = gdn_mixer(zc[0:6], zx[0:6], gdn_conv_l, gdn_a_log_l, gdn_dt_bias_l, gdn_norm_l, want_ctx)
    mla_x, mla_c = mla_mixer(zc[6:9], zx[6:9], mla_q_norm_l, mla_kv_norm_l, mla_w_uq_l, mla_w_ukv_l, cos, sin, want_ctx)
    hg_x, hg_c = hgrn_mixer(zc[9:14], zx[9:14], lb_l, hgrn_norm_l, want_ctx)
    y_x = jnp.concatenate([gdn_x, mla_x, hg_x], axis=-1) @ w_out_l
    y_c = jnp.concatenate([gdn_c, mla_c, hg_c], axis=-1) @ w_out_l if want_ctx else None
    return y_x, y_c

def sq_relu_mlp(h, w1, w2):
    return jnp.square(jax.nn.relu(h @ w1)) @ w2

def setup_inputs(seed: int = 0) -> dict:
    key = jax.random.key(seed)
    ks = jax.random.split(key, 24)

    def nrm(k, shape, scale):
        return jax.random.normal(k, shape, F32) * scale

    def gain(k, shape):
        return 1.0 + 0.02 * jax.random.normal(k, shape, F32)

    dt = jnp.exp(jax.random.uniform(ks[13], (DEPTH, 2, GDN_HEADS), F32, math.log(1e-3), math.log(1e-1)))
    return {
        "x": nrm(ks[0], (BATCH, SEQ, D_MODEL), 1.0),
        "c": nrm(ks[1], (BATCH, D_MODEL), 1.0),
        "ctx": nrm(ks[2], (BATCH, CTX_LEN, D_MODEL), 1.0),
        "c_ctx": nrm(ks[3], (D_MODEL,), 1.0),
        "w_ada": nrm(ks[4], (DEPTH, D_MODEL, 6 * D_MODEL), 0.5 * D_MODEL ** -0.5),
        "b_ada": nrm(ks[5], (DEPTH, 6 * D_MODEL), 0.02),
        "norm_mix_pre": gain(ks[6], (DEPTH, D_MODEL)),
        "norm_mix_post": gain(ks[7], (DEPTH, D_MODEL)),
        "norm_mlp_pre": gain(ks[8], (DEPTH, D_MODEL)),
        "norm_mlp_post": gain(ks[9], (DEPTH, D_MODEL)),
        "w_in": nrm(ks[10], (DEPTH, D_MODEL, D_IN), D_MODEL ** -0.5),
        "w_out": nrm(ks[11], (DEPTH, D_MIX, D_MODEL), D_MIX ** -0.5),
        "gdn_conv": nrm(ks[12], (DEPTH, CONV_W, GDN_HEADS * (2 * GDN_DK + GDN_DV)), CONV_W ** -0.5),
        "gdn_a_log": jnp.log(jax.random.uniform(ks[14], (DEPTH, 2, GDN_HEADS), F32, 1.0, 16.0)),
        "gdn_dt_bias": dt + jnp.log(-jnp.expm1(-dt)),
        "gdn_norm": gain(ks[15], (DEPTH, GDN_DV)),
        "mla_q_norm": gain(ks[16], (DEPTH, MLA_Q_RANK)),
        "mla_kv_norm": gain(ks[17], (DEPTH, MLA_KV_RANK)),
        "mla_w_uq": nrm(ks[18], (DEPTH, MLA_Q_RANK, MLA_HEADS * (MLA_NOPE + MLA_ROPE)), MLA_Q_RANK ** -0.5),
        "mla_w_ukv": nrm(ks[19], (DEPTH, MLA_KV_RANK, MLA_HEADS * (MLA_NOPE + MLA_DV)), MLA_KV_RANK ** -0.5),
        "hgrn_lb_logits": nrm(ks[20], (DEPTH, 2, HG_HEADS * HG_DK), 0.1),
        "hgrn_norm": gain(ks[21], (DEPTH, HG_DV)),
        "w_mlp1": nrm(ks[22], (DEPTH, D_MODEL, D_FF), D_MODEL ** -0.5),
        "w_mlp2": nrm(ks[23], (DEPTH, D_FF, D_MODEL), D_FF ** -0.5),
    }

def reference(x, c, ctx, c_ctx, w_ada, b_ada, norm_mix_pre, norm_mix_post, norm_mlp_pre, norm_mlp_post,
              w_in, w_out, gdn_conv, gdn_a_log, gdn_dt_bias, gdn_norm, mla_q_norm, mla_kv_norm,
              mla_w_uq, mla_w_ukv, hgrn_lb_logits, hgrn_norm, w_mlp1, w_mlp2):
    rows = x.shape[1] // GRID_W
    cos, sin = axial_rope(rows, MLA_ROPE)
    lb_cum = jnp.cumsum(jax.nn.softmax(hgrn_lb_logits.astype(F32), axis=0), axis=0)
    lower_bounds = lb_cum - lb_cum[0]
    h_ctx = ctx
    for l in range(DEPTH):
        want_ctx = l < DEPTH - 1
        sh1x, sc1x, g1x, sh2x, sc2x, g2x = [m[:, None, :] for m in
                                            split_cols(jax.nn.silu(c) @ w_ada[l] + b_ada[l], (D_MODEL,) * 6)]
        sh1c, sc1c, g1c, sh2c, sc2c, g2c = split_cols(jax.nn.silu(c_ctx) @ w_ada[l] + b_ada[l], (D_MODEL,) * 6)
        hx = modulate(rms_norm(x, norm_mix_pre[l]), sh1x, sc1x)
        hc = modulate(rms_norm(h_ctx, norm_mix_pre[l]), sh1c, sc1c)
        y_x, y_c = mixing_layer(hx, hc, w_in[l], w_out[l], gdn_conv[l], gdn_a_log[l], gdn_dt_bias[l], gdn_norm[l],
                                mla_q_norm[l], mla_kv_norm[l], mla_w_uq[l], mla_w_ukv[l], lower_bounds[l],
                                hgrn_norm[l], cos, sin, want_ctx)
        x = x + g1x * rms_norm(y_x, norm_mix_post[l])
        hx = modulate(rms_norm(x, norm_mlp_pre[l]), sh2x, sc2x)
        x = x + g2x * rms_norm(sq_relu_mlp(hx, w_mlp1[l], w_mlp2[l]), norm_mlp_post[l])
        if want_ctx:
            h_ctx = h_ctx + g1c * rms_norm(y_c, norm_mix_post[l])
            hc = modulate(rms_norm(h_ctx, norm_mlp_pre[l]), sh2c, sc2c)
            h_ctx = h_ctx + g2c * rms_norm(sq_relu_mlp(hc, w_mlp1[l], w_mlp2[l]), norm_mlp_post[l])
    return x


_drawn_inputs = setup_inputs


def setup_inputs(seed=0):
    import zlib

    import numpy as np

    out = dict(_drawn_inputs(seed))
    spreads = {}
    factors = {'norm_mix_pre': 3.645,
     'norm_mix_post': 6.822,
     'norm_mlp_pre': 6.231,
     'norm_mlp_post': 6.692,
     'gdn_norm': 8.0,
     'mla_q_norm': 8.0,
     'mla_kv_norm': 8.0,
     'hgrn_lb_logits': 5.183,
     'hgrn_norm': 8.0}
    for name, (base, spread) in spreads.items():
        noise = np.random.default_rng([zlib.crc32(name.encode()), seed]).standard_normal(out[name].shape)
        drawn = base * np.exp(spread * noise) if base else spread * noise
        out[name] = __import__('jax').numpy.asarray(drawn.astype(out[name].dtype))
    for name, factor in factors.items():
        out[name] = (out[name] * factor).astype(out[name].dtype)
    return out
```

```python
import numpy as np
import concourse.bass as bass
from concourse import mybir
from contextlib import ExitStack

D, SEQ, CTX, DEPTH = 1024, 512, 256, 2
TOK = CTX + SEQ
KB = D // 128
FF = 4 * D
FB = FF // 128
CONV_W = 5
NC = TOK // 128
NCC = CTX // 128
H = 4
EPS = 1e-6
NEG = 1.0e30
C_BA, C_CQ, C_CKV, C_HQ = 2048, 2064, 2320, 2480
C_HF, C_HI, C_HG, D_IN = 2992, 4016, 4272, 4528
LEVELS = [1, 2, 4, 8, 16, 32, 64]
V_BADA, V_MIXPRE, V_MIXPOST, V_MLPPRE, V_MLPPOST = 0, 48, 56, 64, 72
V_CONV, V_QN, V_KVN, V_GN, V_HN, V_LB, V_C = 0, 60, 62, 63, 64, 65, 81

LOADS = ([("ada", i) for i in range(24)] + [("ba", 0)] + [("qkv", i) for i in range(6)]
         + [("gate", i) for i in range(2)] + [("hq", i) for i in range(2)] + [("hf", i) for i in range(4)]
         + [("hi", 0), ("hgate", 0), ("cq", 0), ("ckv", 0), ("uq", 0), ("ukv", 0)]
         + [("out", i) for i in range(4)] + [("mlp1", i) for i in range(16)] + [("mlp2", i) for i in range(16)])
NSLOT = 3
UNITS = ([("norm0", 0), ("ba", 0)] + [("qkv", i) for i in range(12)] + [("gcum", 0)]
         + [("l2", i) for i in range(8)] + [("ktr", i) for i in range(NC)] + [("vtr", i) for i in range(NC)]
         + [("gate", i) for i in range(4)] + [("grms", i) for i in range(4)]
         + [("hq", i) for i in range(4)] + [("hf", i) for i in range(8)] + [("hi", i) for i in range(NC)]
         + [("hgate", i) for i in range(2)] + [("hrms", i) for i in range(2)]
         + [("cq", i) for i in range(2)] + [("ckv", 0), ("kr", 0), ("cqsum", 0), ("ckvsum", 0), ("krrot", 0)]
         + [("uq", i) for i in range(4)] + [("qrot", i) for i in range(4)] + [("uk", i) for i in range(4)]
         + [("vt", i) for i in range(NC)] + [("out", i) for i in range(KB)] + [("norm1", 0), ("norm2", 0)]
         + [("mlp1", i) for i in range(FB)] + [("mlp2", i) for i in range(KB)] + [("norm3", 0)])
SQUARES = ([("norm0", i) for i in range(8)] + [("l2", i) for i in range(8)] + [("grms", i) for i in range(4)]
           + [("hrms", i) for i in range(2)] + [("cqsum", i) for i in range(2)] + [("ckvsum", 0)]
           + [(f"norm{n}", i) for n in (1, 2, 3) for i in range(8)])


def number(table, layer, what, i=0):
    return layer * len(table) + table.index((what, i))


SUMS = ("norm0", "l2", "grms", "hrms", "cqsum", "ckvsum", "norm1", "norm2", "norm3")
ROOTS = [u for u in UNITS if u[0] in SUMS]
NOT_SUMS = [u for u in UNITS if u[0] not in SUMS]


def out_number(layer, what, i=0):
    return number(NOT_SUMS, layer, what, i) + 1


def trunk_program(nc, x, ctx, c, c_ctx, w_ada, b_ada, norm_mix_pre, norm_mix_post, norm_mlp_pre, norm_mlp_post,
                  w_in, w_out, gdn_conv, gdn_a_log, gdn_dt_bias, gdn_norm, mla_q_norm, mla_kv_norm,
                  mla_w_uq, mla_w_ukv, hgrn_lb_logits, hgrn_norm, w_mlp1, w_mlp2,
                  k_f32, k_mask, k_rope, out):
    f32, u8 = mybir.dt.float32, mybir.dt.uint8
    ALU, ACT, AX = mybir.AluOpType, mybir.ActivationFunctionType, mybir.AxisListType
    stack = ExitStack()
    with stack:
        def sb(name, shape, dt=f32):
            return stack.enter_context(nc.sbuf_tensor(name, shape, dt))

        def sem(name):
            return stack.enter_context(nc.semaphore(name))

        X = sb("residual", [128, KB, TOK])
        Hm = sb("modulated", [128, KB, TOK])
        Y = sb("mixed", [128, KB, TOK])
        R = sb("region", [128, 8, 4 * TOK])
        ring = sb("weights", [128, NSLOT, 2048])
        kf = sb("k_f32_sb", [128, 8, 128])
        masks = sb("masks", [128, 15, 128], u8)
        vecs = sb("vecs", [128, 4, 128])
        mod = sb("mod", [128, 48, 2])
        A1, A2, G1, G2 = (sb(n, [128, KB, 2]) for n in ("pre_gain1", "pre_gain2", "post_gain1", "post_gain2"))
        cs = sb("silu_c", [128, KB, 2])
        S = sb("state", [128, 2, 512])
        ba = sb("ba", [128, NC, 16])
        gd = sb("gdn_small", [128, 10, 48])
        alog, dtb = sb("alog", [128, 8]), sb("dtb", [128, 8])
        cst = sb("cst", [128, 8])
        lb = sb("lower_bound", [128, DEPTH, 2, 8])
        lbt = sb("lb_tmp", [128, 4, 8])
        sm = sb("small", [128, 16])
        ebl = sb("decay_last", [128, H, NC])
        ps = stack.enter_context(nc.psum_tensor("ps", [128, 8, 512], f32))

        ident, ones, bd64, rotp = kf[:, 0, :], kf[:, 1, :], kf[:, 2, :], kf[:, 3, :]
        tri, madd = (kf[:, 4, :], kf[:, 5, :]), (kf[:, 6, :], kf[:, 7, :])
        eps_col, one_col, lnq_col, tiny_col, zero_col = (cst[:, i:i + 1] for i in range(5))

        def pair(n):
            return ps[:, 2 * (n % 4):2 * (n % 4) + 2, :].rearrange("p a b -> p (a b)")

        def tokens(ap, lo=0):
            return ap[:, CTX + lo:CTX + TOK]

        def blocks(area):
            return R[:, area, :].rearrange("p (h t) -> p h t", t=TOK)

        def chunks(area):
            return R[:, area, :].rearrange("p (c h d) -> p c h d", c=NC, h=H)

        qT, kT, ktok, vtok, vT = blocks(0), blocks(1), chunks(2), chunks(3), blocks(5)
        N_, T_, TT, att = chunks(4), chunks(5), chunks(6), chunks(7)
        Yf = Y[:, :, :].rearrange("p a b -> p (a b)")
        sqb = [R[:, 6, TOK * i:TOK * (i + 1)] for i in range(4)]
        lnb = [R[:, 7, TOK * i:TOK * (i + 1)] for i in range(2)]
        zpad = [R[:, 6, i * 776:i * 776 + 774] for i in range(2)]
        cacc = [R[:, 7, i * 776:i * 776 + 770] for i in range(2)]

        def piece(i):
            return Yf[:, 4 * TOK + 512 * i:4 * TOK + 512 * (i + 1)].rearrange("p (h d) -> p h d", h=H)
        Csb = vb = [piece(0), piece(1)]
        kbg = kend = [piece(2), piece(3)]
        VN = [piece(4), piece(5)]
        beta, la, g_, gl, eg, egl, kd, bg, nbeta, ng = (gd[:, i, :].rearrange("p (c d h) -> p c d h", c=NC, d=2) for i in range(10))

        def s_of(n):
            return S[:, n % 2, :].rearrange("p (h d) -> p h d", h=H)

        def order(d):
            return list(range(NC)) if d == 0 else list(range(NCC))[::-1] + list(range(NCC, NC))[::-1]

        mask_in = sem("mask_in")
        const_in, rows_in, x_in, vec_in, rope_in = sem("const_in"), sem("rows_in"), sem("x_in"), sem("vec_in"), sem("rope_in")
        w_in_s = [sem(f"w_loaded{i}") for i in range(NSLOT)]
        w_used = sem("w_used")
        gemm_out, gemm_evac = sem("gemm_out"), sem("gemm_evac")
        sq_ready, sq_used, rs_ready, rs_used = sem("sq_ready"), sem("sq_used"), sem("rs_ready"), sem("rs_used")
        xT_ready, xT_evac, vT_ready = sem("xT_ready"), sem("xT_evac"), sem("vecT_ready")
        consts_ready, vecs_ready, cs_ready, mods_ready = sem("consts_ready"), sem("vecs_ready"), sem("cs_ready"), sem("mods_ready")
        x_ready, xn_ready, h_ready = sem("x_ready"), sem("xn_ready"), sem("h_ready")
        pads_ready, conv_done, silu_done, l2_done = sem("pads_ready"), sem("conv_done"), sem("silu_done"), sem("l2_done")
        la_a, la_v, la_ready, gs_a, gs_v, gs_ready = (sem(n) for n in ("ba_exps", "ba_sums", "la_ready", "g_split", "g_diff", "g_ready"))
        p1_out, p1_exp_in, p1_exp, p1_done = (sem(n) for n in ("p1_out", "p1_exponents", "p1_decays", "p1_done"))
        c_out, c_evac, b_out, t_ready = (sem(n) for n in ("c_out", "c_evac", "b_out", "t_ready"))
        kbg_ready, w_out_s, wt_ready, eg_exp, qd_ready = (sem(n) for n in ("kbg_ready", "w_out_s", "wt_ready", "eg_exp", "qd_ready"))
        vb_ready, kend_ready, v_out, vn_ready, u_out, s_ready, o_out, o_evac = (
            sem(n) for n in ("vb_ready", "kend_ready", "v_out", "vn_ready", "u_out", "s_ready", "o_out", "o_evac"))
        f_exp, f_done, k_done, lf_done, b_done = (sem(n) for n in ("f_exp", "f_done", "k_done", "lf_done", "b_done"))
        md_ready, me_ready, m_ready, lv_out, lv_evac, eb_ready, hqd_ready = (
            sem(n) for n in ("md_ready", "me_ready", "m_ready", "lv_out", "lv_evac", "eb_ready", "hqd_ready"))
        hu_out, hs_ready, ho_out, ho_evac, lb_a, lb_v, lb_ready = (
            sem(n) for n in ("hu_out", "hs_ready", "ho_out", "ho_evac", "lb_exps", "lb_diff", "lb_ready"))
        y_ready, cn_ready, rope_done, kr_copied = sem("y_ready"), sem("cn_ready"), sem("rope_done"), sem("kr_copied")
        sc_out, mx_ready, pe_ready, p_ready, pt_out, pt_ready, pv_out, pv_evac = (
            sem(n) for n in ("sc_out", "mx_ready", "p_exp", "p_ready", "pt_out", "pt_ready", "pv_out", "pv_evac"))
        out_ready, out_tr, out_evac, hid_ready = sem("out_ready"), sem("out_tr"), sem("out_evac"), sem("hid_ready")
        dve_step, act_step, pool_step = sem("dve_step"), sem("act_step"), sem("pool_step")
        block = stack.enter_context(nc.Block())

        def lo_of(l):
            return 0 if l < DEPTH - 1 else CTX

        def chunks_out(l):
            return [ci for ci in range(NC) if ci * 128 >= lo_of(l)]

        def segments(lo):
            return ([(0, CTX, 1)] if lo == 0 else []) + [(CTX, TOK, 0)]

        NU, NSQ = len(UNITS), len(SQUARES)
        def att_steps(l):
            return [(qt, h) for qt in chunks_out(l) for h in range(H)]
        ATT0 = [0, len(att_steps(0)), len(att_steps(0)) + len(att_steps(1))]
        NLV = 9 * NC

        def o_count(l, d, n):
            full = 2 * NC * l
            outs = [ci in chunks_out(l) for ci in order(d)]
            return full + d * len(chunks_out(l)) + sum(outs[:n + 1])

        def slot(l, what, i=0):
            return number(LOADS, l, what, i) % NSLOT

        def weights_used(n):
            l, k = divmod(n, len(LOADS))
            what, i = LOADS[k]
            if what == "ada":
                return w_used, 36 * l + i + 1
            if what == "mlp2":
                g, kg = divmod(i, 4)
                return (w_used, 36 * l + 24 + 3 * g + kg + 1) if kg < 3 else (gemm_out, out_number(l, "mlp2", 2 * g + 1))
            last = {"ba": ("ba", 0), "qkv": ("qkv", 2 * i + 1), "gate": ("gate", 2 * i + 1), "hq": ("hq", 2 * i + 1),
                    "hf": ("hf", 2 * i + 1), "hi": ("hi", NC - 1), "hgate": ("hgate", 1), "cq": ("cq", 1), "ckv": ("kr", 0),
                    "uq": ("uq", 3), "ukv": ("vt", NC - 1), "out": ("out", 2 * i + 1), "mlp1": ("mlp1", 2 * i + 1)}[what]
            return gemm_out, out_number(l, *last)

        GT = blocks(5)
        CQ, CKV = blocks(0)[:, 0:2, :], blocks(0)[:, 2, :]
        KR, ROT = blocks(0)[:, 3, :], blocks(5)
        QH, KH, VT = blocks(1), blocks(2), R[:, 3, 0:NC * 256].rearrange("p (c e) -> p c e", c=NC)
        KR0, KROT = R[:, 3, 2 * TOK:3 * TOK], R[:, 3, 3 * TOK:3 * TOK + SEQ]
        COS, SIN = R[:, 7, 2 * TOK:2 * TOK + SEQ], R[:, 7, 2 * TOK + SEQ:2 * TOK + 2 * SEQ]
        P_ = [R[:, 4, 0:TOK], R[:, 4, TOK:2 * TOK]]
        PT = [R[:, 4, 2 * TOK:3 * TOK], R[:, 4, 3 * TOK:4 * TOK]]
        HQ, HV, HGT = blocks(0), R[:, 1, 0:NC * 256].rearrange("p (c e) -> p c e", c=NC), R[:, 1, 2 * TOK:4 * TOK].rearrange("p (b t) -> p b t", b=2)
        HK, HB = (blocks(2), blocks(4)), (blocks(3), blocks(5))
        HATT = chunks(7)

        def m_area(d, i):
            return (6, 5 if d == 0 else 3)[i % 2]

        @block.sync
        def _(sp):
            sp.dma_start(kf[:, :, :], k_f32.rearrange("p (a b) -> p a b", b=128)).then_inc(const_in, 16)
            sp.dma_start(R[:, 1, 0:15 * 128], k_mask).then_inc(mask_in, 16)
            xt = Hm[:, :, :].rearrange("p a b -> p (a b)").rearrange("p (c f) -> p c f", c=NC)
            sp.dma_start(xt[:, 0:NCC, :], ctx[0].rearrange("(c p) f -> p c f", p=128)).then_inc(x_in, 16)
            sp.dma_start(xt[:, NCC:NC, :], x[0].rearrange("(c p) f -> p c f", p=128)).then_inc(x_in, 16)
            for l in range(DEPTH):
                for what, i in LOADS:
                    n = number(LOADS, l, what, i)
                    if n >= NSLOT:
                        sp.wait_ge(*weights_used(n - NSLOT))
                    wide = 256
                    if what == "ada":
                        src = w_ada[l][:, 256 * i:256 * i + 256]
                    elif what == "ba":
                        src, wide = w_in[l][:, C_BA:C_CQ], 16
                    elif what == "ckv":
                        src, wide = w_in[l][:, C_CKV:C_HQ], C_HQ - C_CKV
                    elif what in ("qkv", "gate", "hq", "hf", "hi", "hgate", "cq"):
                        c0 = {"qkv": 0, "gate": 1536, "hq": C_HQ, "hf": C_HF, "hi": C_HI, "hgate": C_HG, "cq": C_CQ}[what] + 256 * i
                        src = w_in[l][:, c0:c0 + 256]
                    elif what == "uq":
                        src, wide = mla_w_uq[l], 384
                    elif what == "ukv":
                        src, wide = mla_w_ukv[l], 512
                    elif what == "out":
                        src = w_out[l][:, 256 * i:256 * i + 256]
                    elif what == "mlp1":
                        src = w_mlp1[l][:, 256 * i:256 * i + 256]
                    else:
                        src = w_mlp2[l][1024 * (i % 4):1024 * (i % 4) + 1024, 256 * (i // 4):256 * (i // 4) + 256]
                    ks = src.shape[0] // 128
                    sp.dma_start(ring[:, n % NSLOT, 0:ks * wide].rearrange("p (k n) -> p k n", k=ks),
                                 src.rearrange("(k p) n -> p k n", p=128)).then_inc(w_in_s[n % NSLOT], 16)
            ot = R[:, 0:2, :].rearrange("p a b -> p (a b)")
            for ci in range(SEQ // 128):
                sp.wait_ge(out_evac, 2 * ci + 2)
                sp.dma_start(out[0, 128 * ci:128 * ci + 128, :], ot[:, 1024 * ci:1024 * ci + 1024]).then_inc(out_ready, 16)
            sp.wait_ge(out_ready, 16 * (SEQ // 128))

        @block.gpsimd
        def _(pool):
            count = [0]

            def link(ins):
                count[0] += 1
                ins.then_inc(pool_step, 1)
                pool.wait_ge(pool_step, count[0])

            rows = R[:, 0, 0:512].rearrange("p (a b) -> p a b", b=128)
            link(nc.gpsimd.memset(rows, 0.0))
            nd = 0
            for l in range(DEPTH):
                for at, src in ((V_BADA, b_ada[l]), (V_MIXPRE, norm_mix_pre[l]), (V_MIXPOST, norm_mix_post[l]),
                                (V_MLPPRE, norm_mlp_pre[l]), (V_MLPPOST, norm_mlp_post[l])):
                    n = src.shape[0] // 128
                    pool.dma_start(rows[at:at + n, 2 * l, :], src.rearrange("(r f) -> r f", f=128)).then_inc(rows_in, 16)
                    nd += 1
                pool.dma_start(rows[V_CONV:V_CONV + 60, 2 * l + 1, :], gdn_conv[l].rearrange("w (r f) -> (w r) f", f=128)).then_inc(rows_in, 16)
                for at, src in ((V_QN, mla_q_norm[l]), (V_KVN, mla_kv_norm[l]), (V_GN, gdn_norm[l])):
                    n = src.shape[0] // 128
                    pool.dma_start(rows[at:at + n, 2 * l + 1, :], src.rearrange("(r f) -> r f", f=128)).then_inc(rows_in, 16)
                    nd += 1
                for half in range(2):
                    pool.dma_start(rows[V_HN:V_HN + 1, 2 * l + 1, 64 * half:64 * half + 64],
                                   hgrn_norm[l].rearrange("(r f) -> r f", r=1)).then_inc(rows_in, 16)
                pool.dma_start(rows[V_LB:V_LB + 16, 2 * l + 1, :],
                               hgrn_lb_logits.rearrange("l d (r f) -> (l d r) f", f=128)).then_inc(rows_in, 16)
                pool.dma_start(rows[V_C:V_C + 8, 2 * l + 1, :], c[0].rearrange("(r f) -> r f", f=128)).then_inc(rows_in, 16)
                pool.dma_start(rows[V_C + 8:V_C + 16, 2 * l + 1, :], c_ctx.rearrange("(r f) -> r f", f=128)).then_inc(rows_in, 16)
                nd += 6
            assert nd == 14 * DEPTH
            for l in range(DEPTH):
                if l:
                    pool.wait_ge(la_ready, l)
                pool.dma_start(alog[:, :], gdn_a_log[l].rearrange("d h -> (d h)").partition_broadcast(128)).then_inc(vec_in, 16)
                pool.dma_start(dtb[:, :], gdn_dt_bias[l].rearrange("d h -> (d h)").partition_broadcast(128)).then_inc(vec_in, 16)
                pool.wait_ge(gs_ready, l + 1)
                for d in range(2):
                    base = NC * (2 * l + d)
                    for ci in range(NC):
                        if ci == 0:
                            pool.wait_ge(gemm_evac, number(UNITS, l, "vtr", NC - 1) + 1)
                            pool.wait_ge(t_ready, 7 * NC * (2 * l + d) + 7 * NC)
                            if d == 1:
                                pool.wait_ge(u_out, (NC - 1) * (2 * l + 1))
                        if ci >= 2:
                            pool.wait_ge(w_out_s, base + ci - 1)
                        nc.gpsimd.tensor_tensor(kbg[ci % 2], ktok[:, ci], bg[:, ci, d, :].unsqueeze(2).to_broadcast([128, H, 128]),
                                                ALU.mult).then_inc(kbg_ready, 1)
                        pool.wait_ge(eg_exp, base + ci + 1)
                        nc.gpsimd.tensor_tensor(T_[:, ci], T_[:, ci], qT[:, :, 128 * ci:128 * ci + 128], ALU.mult).then_inc(qd_ready, 1)
                    for n, ci in enumerate(order(d)):
                        if n >= 2:
                            pool.wait_ge(v_out, base + n - 1)
                        nc.gpsimd.tensor_tensor(vb[n % 2], vtok[:, ci], beta[:, ci, d, :].unsqueeze(2).to_broadcast([128, H, 128]),
                                                ALU.mult).then_inc(vb_ready, 1)
                        if n < NC - 1:
                            if n < 2:
                                pool.wait_ge(w_out_s, base + NC - 1 + n)
                            else:
                                pool.wait_ge(u_out, (NC - 1) * (2 * l + d) + n - 1)
                            nc.gpsimd.tensor_tensor(kend[n % 2], ktok[:, ci], kd[:, ci, d, :].unsqueeze(2).to_broadcast([128, H, 128]),
                                                    ALU.mult).then_inc(kend_ready, 1)
                for d in range(2):
                    b = blocks(3 if d == 0 else 5)
                    pool.wait_ge(b_done, 2 * l + d + 1)
                    for i, s in enumerate(LEVELS + [0]):
                        Mb = R[:, (6, 5 if d == 0 else 3)[i % 2], :]
                        if i >= 2:
                            pool.wait_ge(lv_out, NLV * (2 * l + d) + NC * i)
                        elif d == 0 and i == 0:
                            pool.wait_ge(gemm_evac, number(UNITS, l, "hgate", 1) + 1)
                        elif d == 1:
                            pool.wait_ge(ho_out, o_count(l, 0, NC - 1))
                        if s:
                            bv = b.rearrange("p h t -> p (h t)").rearrange("p (n s) -> p n s", s=2 * s)
                            mid = s - 1 if d == 0 else s
                            o = Mb.rearrange("p (n s) -> p n s", s=2 * s)
                            nc.gpsimd.tensor_tensor(o, bv, bv[:, :, mid:mid + 1].to_broadcast([128, 4 * TOK // (2 * s), 2 * s]),
                                                    ALU.subtract).then_inc(md_ready, 1)
                        else:
                            bv = b.rearrange("p h t -> p (h t)").rearrange("p (n s) -> p n s", s=128)
                            last = 127 if d == 0 else 0
                            o = Mb.rearrange("p (n s) -> p n s", s=128)
                            nc.gpsimd.tensor_tensor(o, bv, bv[:, :, last:last + 1].to_broadcast([128, 4 * NC, 128]),
                                                    ALU.subtract).then_inc(md_ready, 1)
                pool.wait_ge(ho_evac, o_count(l, 1, NC - 1))
                pool.dma_start(R[64:96, 7, 2 * TOK:2 * TOK + 2 * SEQ], k_rope).then_inc(rope_in, 16)
                pool.wait_ge(rope_done, 5 * l + 1)
                for h in range(H):
                    ins = nc.gpsimd.tensor_copy(KH[64:96, h, :], KR[64:96, :])
                ins.then_inc(kr_copied, 1)

        @block.tensor
        def _(pe):
            mm, tr = nc.tensor.matmul, nc.tensor.transpose

            def arrived(l, what, i=0):
                n = number(LOADS, l, what, i)
                pe.wait_ge(w_in_s[n % NSLOT], 16 * (n // NSLOT + 1))
                return ring[:, n % NSLOT, :]

            def free_pair(l, what, i=0):
                n = number(UNITS, l, what, i)
                if n >= 4:
                    pe.wait_ge(gemm_evac, n - 3)
                return pair(n)

            def streams(lo):
                return ([(0, CTX)] if lo == 0 else []) + [(CTX, TOK)]

            def project(dst, w, rhs, ks, m0, m, lo=0, first=True, final=True):
                for k in range(ks):
                    for a, b in streams(lo):
                        last = mm(dst[0:m, CTX + a:CTX + b], w[:, k, m0:m0 + m], rhs[:, k, a:b],
                                  start=(first and k == 0), stop=(final and k == ks - 1))
                return last

            def gemm(l, what, load, units, rhs, lo=0, wide=256):
                w = arrived(l, what, load)[:, 0:KB * wide].rearrange("p (k n) -> p k n", k=KB)
                for j, u in enumerate(units):
                    dst = free_pair(l, what, u)
                    last = project(dst, w, rhs, KB, 128 * j, 128, lo)
                    last.then_inc(gemm_out, 1)

            def sum_squares(l, what, n0, n, mat, lo=0):
                dst = free_pair(l, what, n0)
                first = number(SQUARES, l, what, 0 if n > 1 else n0)
                for k in range(n):
                    pe.wait_ge(sq_ready, first + k + 1)
                    for a, b in streams(lo):
                        last = mm(dst[:, CTX + a:CTX + b], mat, sqb[(first + k) % 4][:, a:b], start=(k == 0), stop=(k == n - 1))
                    last.then_inc(sq_used, 1)

            pe.wait_ge(const_in, 16)
            pe.wait_ge(rows_in, 16 * 14 * DEPTH)
            rows = R[:, 0, 0:512].rearrange("p (a b) -> p a b", b=128)
            for i in range(4):
                last = tr(ps[:, 7, 128 * i:128 * i + 128], rows[:, i, :], ident)
            last.then_inc(vT_ready, 1)
            pe.wait_ge(x_in, 32)
            xt = Hm[:, :, :].rearrange("p a b -> p (a b)").rearrange("p (c f) -> p c f", c=NC)
            for i in range(2 * NC):
                if i >= 4:
                    pe.wait_ge(xT_evac, i - 3)
                for j in range(4):
                    f0 = 512 * (i % 2) + 128 * j
                    last = tr(ps[:, i % 4, 128 * j:128 * j + 128], xt[:, i // 2, f0:f0 + 128], ident)
                last.then_inc(xT_ready, 1)

            for l in range(DEPTH):
                lo = lo_of(l)
                if l == 0:
                    pe.wait_ge(cs_ready, 1)
                    pe.wait_ge(xT_evac, 2 * NC)
                else:
                    pe.wait_ge(gemm_evac, NU * l)
                for i in range(24):
                    w = arrived(l, "ada", i).rearrange("p (k n) -> p k n", k=KB)
                    for j in range(2):
                        col = 2 * (2 * i + j)
                        for k in range(KB):
                            last = mm(ps[:, 0, col:col + 2], w[:, k, 128 * j:128 * j + 128], cs[:, k, :], start=(k == 0), stop=(k == KB - 1))
                    last.then_inc(w_used, 1)
                pe.wait_ge(mods_ready, l + 1)
                sum_squares(l, "norm0", 0, KB, ones)
                pe.wait_ge(h_ready, 8 * (2 * l + 1))
                dst = free_pair(l, "ba")
                w = arrived(l, "ba")[:, 0:KB * 16].rearrange("p (k n) -> p k n", k=KB)
                for ci in range(NC):
                    for k in range(KB):
                        last = mm(dst[:, 512 + 16 * ci:512 + 16 * ci + 16], Hm[:, k, 128 * ci:128 * ci + 128], w[:, k, :],
                                  start=(k == 0), stop=(k == KB - 1))
                last.then_inc(gemm_out, 1)
                for i in range(6):
                    gemm(l, "qkv", i, [2 * i, 2 * i + 1], Hm)
                pe.wait_ge(la_ready, l + 1)
                dst = free_pair(l, "gcum")
                for i, m in enumerate((tri[0], tri[1], ones)):
                    last = mm(dst[:, 512 + 48 * i:512 + 48 * i + 48], m, gd[:, 1, :], start=True, stop=True)
                last.then_inc(gemm_out, 1)
                for u in range(8):
                    sum_squares(l, "l2", u, 1, ones)
                pe.wait_ge(l2_done, 8 * (l + 1))
                pe.wait_ge(silu_done, 12 * (l + 1))
                for what, src in (("ktr", kT), ("vtr", vT)):
                    for ci in range(NC):
                        dst = free_pair(l, what, ci)
                        for h in range(H):
                            last = tr(dst[:, 512 + 128 * h:512 + 128 * h + 128], src[:, h, 128 * ci:128 * ci + 128], ident)
                        last.then_inc(gemm_out, 1)
                pe.wait_ge(gs_ready, l + 1)
                pe.wait_ge(gemm_evac, number(UNITS, l, "vtr", NC - 1) + 1)

                for d in range(2):
                    base = NC * (2 * l + d)
                    for ci in range(NC):
                        if ci >= 2:
                            pe.wait_ge(p1_done, base + ci - 1)
                        elif d == 1:
                            pe.wait_ge(o_evac, o_count(l, 0, NC - 1))
                        G, KK, QK = (3 * (ci % 2) + j for j in range(3))
                        cc = slice(128 * ci, 128 * ci + 128)
                        for h in range(H):
                            mm(ps[:, G, 128 * h:128 * h + 128], la[:, ci, d, h:h + 1].to_broadcast([128, 128]), tri[d], start=True, stop=True)
                        for h in range(H):
                            mm(ps[:, KK, 128 * h:128 * h + 128], kT[:, h, cc], kT[:, h, cc], start=True, stop=True)
                        for h in range(H):
                            last = mm(ps[:, QK, 128 * h:128 * h + 128], kT[:, h, cc], qT[:, h, cc], start=True, stop=True)
                        last.then_inc(p1_out, 1)
                    tb = 7 * NC * (2 * l + d)
                    cb = 6 * NC * (2 * l + d)
                    steps = [(lv, ci) for lv in range(7) for ci in range(NC)]
                    pe.wait_ge(p1_done, base + NC)

                    def c_product(i):
                        lv, ci = steps[i]
                        j = i - NC
                        pe.wait_ge(t_ready, tb + i - NC + 1)
                        if j >= 2:
                            pe.wait_ge(c_evac, cb + j - 1)
                        for h in range(H):
                            last = mm(ps[:, j % 2, 128 * h:128 * h + 128], N_[:, ci, h, :], TT[:, ci, h, :], start=True, stop=True)
                        last.then_inc(c_out, 1)
                    for i, (lv, ci) in enumerate(steps):
                        if i == NC - 1:
                            c_product(NC)
                        elif i >= NC and i + 1 < len(steps):
                            c_product(i + 1)
                        B, BT = 2 + 2 * (i % 2), 3 + 2 * (i % 2)
                        if i >= 2:
                            pe.wait_ge(t_ready, tb + i - 1)
                        if lv == 0:
                            for h in range(H):
                                last = tr(ps[:, BT, 128 * h:128 * h + 128], N_[:, ci, h, :], ident)
                        else:
                            j = i - NC
                            pe.wait_ge(c_evac, cb + j + 1)
                            for h in range(H):
                                last = mm(ps[:, BT, 128 * h:128 * h + 128], T_[:, ci, h, :], Csb[j % 2][:, h, :], start=True, stop=True)
                            if lv < 6:
                                for h in range(H):
                                    last = mm(ps[:, B, 128 * h:128 * h + 128], Csb[j % 2][:, h, :], T_[:, ci, h, :], start=True, stop=True)
                        last.then_inc(b_out, 1)
                    pe.wait_ge(t_ready, tb + 7 * NC)
                    for ci in range(NC):
                        if ci >= 2:
                            pe.wait_ge(eg_exp, base + ci - 1)
                            pe.wait_ge(wt_ready, base + ci - 1)
                        G, W = 2 * (ci % 2), 2 * (ci % 2) + 1
                        for h in range(H):
                            mm(ps[:, G, 128 * h:128 * h + 128], la[:, ci, d, h:h + 1].to_broadcast([128, 128]), tri[d], start=True, stop=True)
                        pe.wait_ge(kbg_ready, base + ci + 1)
                        for h in range(H):
                            last = mm(ps[:, W, 128 * h:128 * h + 128], kbg[ci % 2][:, h, :], TT[:, ci, h, :], start=True, stop=True)
                        last.then_inc(w_out_s, 1)
                    pe.wait_ge(eg_exp, base + NC)
                    pe.wait_ge(wt_ready, base + NC)
                    pe.wait_ge(qd_ready, base + NC)
                    for n, ci in enumerate(order(d)):
                        V, U, O = n % 2, 2 + n % 2, 4 + n % 2
                        pe.wait_ge(vb_ready, base + n + 1)
                        if n:
                            pe.wait_ge(s_ready, (NC - 1) * (2 * l + d) + n)
                        for h in range(H):
                            o = ps[:, V, 128 * h:128 * h + 128]
                            last = mm(o, TT[:, ci, h, :], vb[n % 2][:, h, :], start=True, stop=(n == 0))
                            if n:
                                last = mm(o, N_[:, ci, h, :], s_of(n - 1)[:, h, :], start=False, stop=True)
                        last.then_inc(v_out, 1)
                        pe.wait_ge(vn_ready, base + n + 1)
                        if n < NC - 1:
                            pe.wait_ge(kend_ready, (NC - 1) * (2 * l + d) + n + 1)
                            for h in range(H):
                                last = mm(ps[:, U, 128 * h:128 * h + 128], kend[n % 2][:, h, :], VN[n % 2][:, h, :], start=True, stop=True)
                            last.then_inc(u_out, 1)
                        if ci in chunks_out(l):
                            k = o_count(l, d, n)
                            if k > o_count(l, d, -1) + 2:
                                pe.wait_ge(o_evac, k - 2)
                            for h in range(H):
                                o = ps[:, O, 128 * h:128 * h + 128]
                                if n:
                                    mm(o, s_of(n - 1)[:, h, :], T_[:, ci, h, :], start=True, stop=False)
                                last = mm(o, VN[n % 2][:, h, :], att[:, ci, h, :], start=(n == 0), stop=True)
                            last.then_inc(o_out, 1)
                pe.wait_ge(o_evac, o_count(l, 1, NC - 1))
                for i in range(2):
                    gemm(l, "gate", i, [2 * i, 2 * i + 1], Hm, lo)
                for u in range(4):
                    sum_squares(l, "grms", u, 1, ones, lo)
                for i in range(2):
                    gemm(l, "hq", i, [2 * i, 2 * i + 1], Hm)
                for i in range(4):
                    gemm(l, "hf", i, [2 * i, 2 * i + 1], Hm)
                w = arrived(l, "hi").rearrange("p (k n) -> p k n", k=KB)
                for ci in range(NC):
                    dst = free_pair(l, "hi", ci)
                    for k in range(KB):
                        last = mm(dst[:, 512:768], Hm[:, k, 128 * ci:128 * ci + 128], w[:, k, :], start=(k == 0), stop=(k == KB - 1))
                    last.then_inc(gemm_out, 1)
                gemm(l, "hgate", 0, [0, 1], Hm, lo)
                pe.wait_ge(gemm_evac, number(UNITS, l, "hgate", 1) + 1)

                for d in range(2):
                    lvb = NLV * (2 * l + d)
                    bank = 0
                    if d == 1:
                        pe.wait_ge(ho_evac, o_count(l, 0, NC - 1))
                    for i in range(-1, 8):
                        if i < 0:
                            pe.wait_ge(k_done, 2 * l + d + 1)
                        else:
                            pe.wait_ge(m_ready, 8 * (2 * l + d) + i + 1)
                        for ci in range(NC):
                            cc = slice(128 * ci, 128 * ci + 128)
                            if bank >= 8:
                                pe.wait_ge(lv_evac, lvb + bank - 7)
                            for h in range(H):
                                o = ps[:, bank % 8, 128 * h:128 * h + 128]
                                if i < 0:
                                    last = mm(o, HK[d][:, h, cc], HQ[:, h, cc], start=True, stop=True)
                                elif i < 7:
                                    M = blocks(m_area(d, i))
                                    last = mm(o, M[:, h, cc], M[:, h, cc], start=True, stop=True)
                                else:
                                    last = tr(o, blocks(m_area(d, i))[:, h, cc], ident)
                            last.then_inc(lv_out, 1)
                            bank += 1
                    KE = chunks(m_area(d, 0))
                    pe.wait_ge(lv_evac, lvb + NLV)
                    pe.wait_ge(hqd_ready, 2 * l + d + 1)
                    for n, ci in enumerate(order(d)):
                        U, O = n % 2, 2 + n % 2
                        sbase = (NC - 1) * (2 * l + d)
                        if n < NC - 1:
                            if n >= 2:
                                pe.wait_ge(hs_ready, sbase + n - 1)
                            for h in range(H):
                                last = mm(ps[:, U, 64 * h:64 * h + 64], KE[:, ci, h, :], HV[:, ci, 64 * h:64 * h + 64], start=True, stop=True)
                            last.then_inc(hu_out, 1)
                        if ci in chunks_out(l):
                            k = o_count(l, d, n)
                            if k > o_count(l, d, -1) + 2:
                                pe.wait_ge(ho_evac, k - 2)
                            if n:
                                pe.wait_ge(hs_ready, sbase + n)
                            for h in range(H):
                                p0, c0 = 64 * (h % 2), 128 * (h // 2)
                                o = ps[p0:p0 + 64, O, c0:c0 + 128]
                                if n:
                                    mm(o, S[:, (n - 1) % 2, 64 * h:64 * h + 64], HK[d][:, h, 128 * ci:128 * ci + 128], start=True, stop=False)
                                last = mm(o, HV[:, ci, 64 * h:64 * h + 64], HATT[:, ci, h, :], start=(n == 0), stop=True)
                            last.then_inc(ho_out, 1)
                pe.wait_ge(ho_evac, o_count(l, 1, NC - 1))
                for u in range(2):
                    sum_squares(l, "hrms", u, 1, bd64, lo)

                gemm(l, "cq", 0, [0, 1], Hm)
                w = arrived(l, "ckv")[:, 0:KB * 160].rearrange("p (k n) -> p k n", k=KB)
                project(free_pair(l, "ckv"), w, Hm, KB, 0, 128).then_inc(gemm_out, 1)
                project(free_pair(l, "kr"), w, Hm, KB, 64, 96).then_inc(gemm_out, 1)
                sum_squares(l, "cqsum", 0, 2, ones)
                sum_squares(l, "ckvsum", 0, 1, ones)
                dst = free_pair(l, "krrot")
                pe.wait_ge(gemm_evac, number(UNITS, l, "kr") + 1)
                mm(dst[0:96, 512:1024], rotp[0:96, 0:96], KR0[0:96, CTX:TOK], start=True, stop=True).then_inc(gemm_out, 1)
                pe.wait_ge(cn_ready, 3 * l + 3)
                w = arrived(l, "uq")[:, 0:768].rearrange("p (k n) -> p k n", k=2)
                for h in range(H):
                    last = project(free_pair(l, "uq", h), w, CQ, 2, 96 * h, 96)
                    last.then_inc(gemm_out, 1)
                for h in range(H):
                    dst = free_pair(l, "qrot", h)
                    pe.wait_ge(gemm_evac, number(UNITS, l, "uq", h) + 1)
                    mm(dst[0:96, 512:1024], rotp[0:96, 0:96], QH[0:96, h, CTX:TOK], start=True, stop=True).then_inc(gemm_out, 1)
                w = arrived(l, "ukv")[:, 0:512].rearrange("p (k n) -> p k n", k=1)
                for h in range(H):
                    project(free_pair(l, "uk", h), w, CKV.unsqueeze(1), 1, 128 * h, 64).then_inc(gemm_out, 1)
                wv = arrived(l, "ukv")[:, 0:512].rearrange("p (h n) -> p h n", h=H)
                for ci in range(NC):
                    dst = free_pair(l, "vt", ci)
                    mm(dst[:, 512:768].rearrange("p (h n) -> p h n", h=H), CKV[:, 128 * ci:128 * ci + 128], wv[:, :, 64:128],
                       start=True, stop=True).then_inc(gemm_out, 1)
                pe.wait_ge(gemm_evac, number(UNITS, l, "vt", NC - 1) + 1)
                pe.wait_ge(rope_done, 5 * (l + 1))
                pe.wait_ge(kr_copied, l + 1)
                steps = att_steps(l)

                def scores(i):
                    qt, h = steps[i]
                    a = ATT0[l] + i
                    if i >= 2:
                        pe.wait_ge(pe_ready, a - 1)
                    dst = ps[:, 2 * (i % 2):2 * (i % 2) + 2, :].rearrange("p a b -> p (a b)")
                    for s0, s1 in ([(0, CTX)] if qt < NCC else [(0, CTX), (CTX, TOK)]):
                        last = mm(dst[:, CTX + s0:CTX + s1], QH[0:96, h, 128 * qt:128 * qt + 128], KH[0:96, h, s0:s1], start=True, stop=True)
                    last.then_inc(sc_out, 1)

                scores(0)
                for i, (qt, h) in enumerate(steps):
                    if i + 1 < len(steps):
                        scores(i + 1)
                    a = ATT0[l] + i
                    nk = NCC if qt < NCC else NC
                    pe.wait_ge(p_ready, a + 1)
                    if i >= 1:
                        pe.wait_ge(pt_ready, a)
                    dst = ps[:, 4:6, :].rearrange("p a b -> p (a b)")
                    for ck in range(nk):
                        last = tr(dst[:, CTX + 128 * ck:CTX + 128 * ck + 128], P_[i % 2][:, 128 * ck:128 * ck + 128], ident)
                    last.then_inc(pt_out, 1)
                    pe.wait_ge(pt_ready, a + 1)
                    if i >= 2:
                        pe.wait_ge(pv_evac, a - 1)
                    p0 = 64 * (h % 2)
                    for ck in range(nk):
                        last = mm(ps[p0:p0 + 64, 6 + i % 2, 0:128], VT[:, ck, 64 * h:64 * h + 64], PT[i % 2][:, 128 * ck:128 * ck + 128],
                                  start=(ck == 0), stop=(ck == nk - 1))
                    last.then_inc(pv_out, 1)
                pe.wait_ge(pv_evac, ATT0[l + 1])
                pe.wait_ge(y_ready, 6 * (l + 1))
                for i in range(4):
                    gemm(l, "out", i, [2 * i, 2 * i + 1], Y, lo)
                sum_squares(l, "norm1", 0, KB, ones, lo)
                sum_squares(l, "norm2", 0, KB, ones, lo)
                pe.wait_ge(h_ready, 8 * (2 * l + 2))
                for i in range(16):
                    gemm(l, "mlp1", i, [2 * i, 2 * i + 1], Hm, lo)
                pe.wait_ge(gemm_evac, number(UNITS, l, "mlp1", FB - 1) + 1)
                hid = R[:, :, :].rearrange("p a b -> p (a b)").rearrange("p (k t) -> p k t", t=TOK)
                pe.wait_ge(hid_ready, FB * (l + 1))
                for g in range(4):
                    dsts = [free_pair(l, "mlp2", 2 * g + j) for j in range(2)]
                    for kg in range(4):
                        w = arrived(l, "mlp2", 4 * g + kg).rearrange("p (k n) -> p k n", k=KB)
                        for j in range(2):
                            last = project(dsts[j], w, hid[:, 8 * kg:8 * kg + 8, :], KB, 128 * j, 128, lo, kg == 0, kg == 3)
                            if kg == 3:
                                last.then_inc(gemm_out, 1)
                        if kg < 3:
                            last.then_inc(w_used, 1)
                sum_squares(l, "norm3", 0, KB, ones, lo)
            pe.wait_ge(x_ready, 2 * DEPTH)
            for i in range(2 * SEQ // 128):
                if i >= 4:
                    pe.wait_ge(out_evac, i - 3)
                t0 = CTX + 128 * (i // 2)
                for j in range(4):
                    last = tr(ps[:, i % 4, 128 * j:128 * j + 128], X[:, 4 * (i % 2) + j, t0:t0 + 128], ident)
                last.then_inc(out_tr, 1)

        @block.scalar
        def _(act):
            af = nc.scalar.activation
            count = [0]

            def link(ins):
                count[0] += 1
                ins.then_inc(act_step, 1)
                act.wait_ge(act_step, count[0])

            def finished(l, what, i=0):
                act.wait_ge(gemm_out, out_number(l, what, i))
                return pair(number(UNITS, l, what, i))

            def copied(l, what, i, ins):
                ins.then_inc(gemm_evac, 1)
                assert next_unit[0] == number(UNITS, l, what, i), (what, i)
                next_unit[0] += 1
            next_unit = [0]

            def square(l, what, i, src, lo=0):
                n = number(SQUARES, l, what, i)
                if n >= 4:
                    act.wait_ge(sq_used, n - 3)
                af(sqb[n % 4][:, lo:], src, ACT.Square).then_inc(sq_ready, 1)

            def roots_used(n):
                l, k = divmod(n, len(ROOTS))
                what, i = ROOTS[k]
                if what in ("norm0", "norm2"):
                    return xn_ready, 8 * (2 * l + (1 if what == "norm0" else 2))
                if what in ("norm1", "norm3"):
                    return x_ready, 2 * l + (1 if what == "norm1" else 2)
                if what == "l2":
                    return l2_done, 8 * l + i + 1
                if what in ("grms", "hrms"):
                    return y_ready, 6 * l + i + 1 + (4 if what == "hrms" else 0)
                return cn_ready, 3 * l + (2 if what == "cqsum" else 3)

            def inverse_root(l, what, i, width, n, lo=0, bias=None):
                first = number(SQUARES, l, what, i)
                act.wait_ge(sq_used, first + n)
                r, u = number(ROOTS, l, what, i), number(UNITS, l, what, i)
                if r >= 2:
                    act.wait_ge(*roots_used(r - 2))
                o = lnb[r % 2][:, lo:]
                copied(l, what, i, af(o, tokens(pair(u), lo), ACT.Ln, bias=eps_col, scale=1.0 / width))
                act.wait_ge(gemm_evac, u + 1)
                af(o, o, ACT.Exp, bias=zero_col if bias is None else bias, scale=-0.5).then_inc(rs_ready, 1)

            def modulate(l, w, A, B):
                for b in range(KB):
                    act.wait_ge(xn_ready, 8 * (2 * l + w) + b + 1)
                    for a, e, s in segments(0 if w == 0 else lo_of(l)):
                        last = af(Hm[:, b, a:e], Hm[:, b, a:e], ACT.Identity, bias=B[:, b, s:s + 1], scale=A[:, b, s:s + 1])
                    last.then_inc(h_ready, 1)

            for i in range(2 * NC):
                act.wait_ge(xT_ready, i + 1)
                af(X[:, 4 * (i % 2):4 * (i % 2) + 4, 128 * (i // 2):128 * (i // 2) + 128],
                   ps[:, i % 4, :].rearrange("p (b t) -> p b t", b=4), ACT.Copy).then_inc(xT_evac, 1)
            act.wait_ge(consts_ready, 1)
            act.wait_ge(lb_v, 1)
            af(lbt[:, 0:2, :], lbt[:, 0:2, :], ACT.Exp, bias=zero_col).then_inc(lb_a, 1)
            act.wait_ge(vecs_ready, 1)
            af(cs[:, :, :].rearrange("p k s -> p s k"), vecs[:, 1, V_C:V_C + 16].rearrange("p (s k) -> p s k", s=2),
               ACT.Silu, bias=zero_col).then_inc(cs_ready, 1)
            act.wait_ge(xT_evac, 2 * NC)

            for l in range(DEPTH):
                lo = lo_of(l)
                if l:
                    act.wait_ge(x_ready, 2 * l)
                for b in range(KB):
                    square(l, "norm0", b, X[:, b, :])
                inverse_root(l, "norm0", 0, D, KB)
                modulate(l, 0, A1, mod[:, 0:8, :])
                copied(l, "ba", 0, af(ba[:, :, :], finished(l, "ba")[:, 512:608].rearrange("p (c n) -> p c n", c=NC), ACT.Copy))
                act.wait_ge(la_v, l + 1)
                act.wait_ge(vec_in, 32 * (l + 1))
                af(gd[:, 0, :].rearrange("p (c n) -> p c n", c=NC), ba[:, :, 0:8], ACT.Exp, bias=zero_col, scale=-1.0)
                link(af(gd[:, 6, :], gd[:, 9, :], ACT.Abs, bias=zero_col))
                link(af(gd[:, 6, :], gd[:, 6, :], ACT.Exp, bias=zero_col, scale=-1.0))
                link(af(gd[:, 6, :], gd[:, 6, :], ACT.Ln, bias=one_col))
                af(alog[:, :], alog[:, :], ACT.Exp, bias=zero_col).then_inc(la_a, 1)
                act.wait_ge(pads_ready, l + 1)

                def silu(u):
                    act.wait_ge(conv_done, 12 * l + u + 1)
                    dst = (qT, kT, vT)[u // 4][:, u % 4, :]
                    af(dst[:, 0:CTX], cacc[u % 2][:, 0:CTX], ACT.Silu, bias=zero_col)
                    af(dst[:, CTX:TOK], cacc[u % 2][:, CTX + 2:TOK + 2], ACT.Silu, bias=zero_col).then_inc(silu_done, 1)
                for u in range(12):
                    z = finished(l, "qkv", u)
                    if u >= 2:
                        act.wait_ge(conv_done, 12 * l + u - 1)
                    af(zpad[u % 2][:, 2:2 + CTX], z[:, CTX:2 * CTX], ACT.Copy)
                    copied(l, "qkv", u, af(zpad[u % 2][:, CTX + 4:TOK + 4], z[:, 2 * CTX:CTX + TOK], ACT.Copy))
                    if u:
                        silu(u - 1)
                silu(11)
                copied(l, "gcum", 0, af(S[:, 0, 0:144], finished(l, "gcum")[:, 512:656], ACT.Copy))
                act.wait_ge(gs_v, l + 1)
                af(gd[:, 4, :], gd[:, 2, :], ACT.Exp, bias=zero_col)
                af(gd[:, 5, :], gd[:, 3, :], ACT.Exp, bias=zero_col)
                af(gd[:, 6, :], gd[:, 6, :], ACT.Exp, bias=zero_col).then_inc(gs_a, 1)
                act.wait_ge(silu_done, 12 * (l + 1))
                qk = [(qT, kT)[u // 4][:, u % 4, :] for u in range(8)]
                for u in range(4):
                    square(l, "l2", u, qk[u])
                for u in range(8):
                    inverse_root(l, "l2", u, 1, 1, bias=lnq_col if u < 4 else None)
                    if u < 4:
                        square(l, "l2", u + 4, qk[u + 4])
                for what, dst in (("ktr", ktok), ("vtr", vtok)):
                    for ci in range(NC):
                        src = finished(l, what, ci)[:, 512:1024].rearrange("p (h d) -> p h d", h=H)
                        copied(l, what, ci, af(dst[:, ci], src, ACT.Copy))
                for d in range(2):
                    base = NC * (2 * l + d)
                    for ci in range(NC):
                        act.wait_ge(p1_exp_in, base + ci + 1)
                        for h in range(H):
                            af(T_[:, ci % 2, h, :], T_[:, ci % 2, h, :], ACT.Exp, bias=g_[:, ci, d, h:h + 1])
                        for h in range(H):
                            last = af(TT[:, ci % 2, h, :], TT[:, ci % 2, h, :], ACT.Exp, bias=ng[:, ci, d, h:h + 1])
                        last.then_inc(p1_exp, 1)
                    bb, cb = 7 * NC * (2 * l + d), 6 * NC * (2 * l + d)
                    for j in range(6 * NC):
                        act.wait_ge(c_out, cb + j + 1)
                        if j >= 2:
                            act.wait_ge(b_out, bb + NC + j - 1)
                        af(Csb[j % 2], ps[:, j % 2, :].rearrange("p (h d) -> p h d", h=H), ACT.Copy).then_inc(c_evac, 1)
                    for ci in range(NC):
                        act.wait_ge(w_out_s, base + ci + 1)
                        G, W = 2 * (ci % 2), 2 * (ci % 2) + 1
                        af(T_[:, ci], ps[:, G, :].rearrange("p (h d) -> p h d", h=H), ACT.Exp, bias=zero_col).then_inc(eg_exp, 1)
                        af(N_[:, ci], ps[:, W, :].rearrange("p (h d) -> p h d", h=H), ACT.Copy, scale=-1.0).then_inc(wt_ready, 1)
                    for n in range(NC):
                        act.wait_ge(v_out, base + n + 1)
                        af(VN[n % 2], ps[:, n % 2, :].rearrange("p (h d) -> p h d", h=H), ACT.Copy).then_inc(vn_ready, 1)
                for u in range(4):
                    copied(l, "gate", u, af(GT[:, u, lo:], tokens(finished(l, "gate", u), lo), ACT.Silu, bias=zero_col))
                act.wait_ge(o_evac, o_count(l, 1, NC - 1))
                for u in range(4):
                    square(l, "grms", u, Y[:, u, lo:], lo)
                for u in range(4):
                    inverse_root(l, "grms", u, 128, 1, lo)
                for u in range(4):
                    copied(l, "hq", u, af(HQ[:, u, :], tokens(finished(l, "hq", u)), ACT.Copy, scale=128 ** -0.5))
                for u in range(8):
                    copied(l, "hf", u, af(HK[u // 4][:, u % 4, :], tokens(finished(l, "hf", u)), ACT.Copy))
                for ci in range(NC):
                    copied(l, "hi", ci, af(HV[:, ci, :], finished(l, "hi", ci)[:, 512:768], ACT.Copy))
                for u in range(2):
                    copied(l, "hgate", u, af(HGT[:, u, lo:], tokens(finished(l, "hgate", u), lo), ACT.Silu, bias=zero_col))
                act.wait_ge(gemm_evac, number(UNITS, l, "hgate", 1) + 1)
                act.wait_ge(y_ready, 6 * l + 4)
                for d in range(2):
                    if d == 1:
                        act.wait_ge(lv_out, NLV * (2 * l + 1))
                    af(HB[d], HK[d], ACT.Exp, bias=zero_col, scale=-1.0).then_inc(f_exp, 1)
                    act.wait_ge(k_done, 2 * l + d + 1)
                    af(HB[d], HB[d], ACT.Ln, bias=tiny_col).then_inc(lf_done, 1)
                    for i, s in enumerate(LEVELS + [0]):
                        act.wait_ge(md_ready, 8 * (2 * l + d) + i + 1)
                        M = R[:, m_area(d, i), :]
                        if s:
                            v = M.rearrange("p (n e s) -> p n e s", e=2, s=s)
                            low = -1.0 if d == 0 else 1.0
                            af(v[:, :, 0, :], v[:, :, 0, :], ACT.Exp, bias=zero_col, scale=low)
                            af(v[:, :, 1, :], v[:, :, 1, :], ACT.Exp, bias=zero_col, scale=-low).then_inc(me_ready, 1)
                        else:
                            af(M, M, ACT.Exp, bias=zero_col, scale=-1.0).then_inc(me_ready, 1)
                    b4 = HB[d].rearrange("p h (c t) -> p h c t", t=128)
                    link(af(ebl[:, :, :], b4[:, :, :, 127 if d == 0 else 0], ACT.Exp, bias=zero_col))
                    af(HB[d], HB[d], ACT.Exp, bias=zero_col).then_inc(eb_ready, 1)
                act.wait_ge(ho_evac, o_count(l, 1, NC - 1))
                for u in range(2):
                    square(l, "hrms", u, Y[:, 6 + u, lo:], lo)
                for u in range(2):
                    inverse_root(l, "hrms", u, 64, 1, lo)
                act.wait_ge(y_ready, 6 * l + 6)
                for u in range(2):
                    copied(l, "cq", u, af(CQ[:, u, :], tokens(finished(l, "cq", u)), ACT.Copy))
                copied(l, "ckv", 0, af(CKV, tokens(finished(l, "ckv")), ACT.Copy))
                copied(l, "kr", 0, af(KR0[0:96], tokens(finished(l, "kr"))[0:96], ACT.Copy))
                act.wait_ge(gemm_evac, number(UNITS, l, "kr") + 1)
                for u in range(2):
                    square(l, "cqsum", u, CQ[:, u, :])
                square(l, "ckvsum", 0, CKV)
                inverse_root(l, "cqsum", 0, 256, 2)
                inverse_root(l, "ckvsum", 0, 128, 1)
                copied(l, "krrot", 0, af(KROT[0:96], finished(l, "krrot")[0:96, 512:1024], ACT.Copy))
                for h in range(H):
                    copied(l, "uq", h, af(QH[0:96, h, :], tokens(finished(l, "uq", h))[0:96], ACT.Copy))
                for h in range(H):
                    copied(l, "qrot", h, af(ROT[0:96, h, 0:SEQ], finished(l, "qrot", h)[0:96, 512:1024], ACT.Copy))
                for h in range(H):
                    copied(l, "uk", h, af(KH[0:64, h, :], tokens(finished(l, "uk", h))[0:64], ACT.Copy))
                for ci in range(NC):
                    copied(l, "vt", ci, af(VT[:, ci, :], finished(l, "vt", ci)[:, 512:768], ACT.Copy))
                steps = att_steps(l)

                def keys_of(i):
                    return CTX if steps[i][0] < NCC else TOK

                def probabilities(i):
                    a = ATT0[l] + i
                    act.wait_ge(mx_ready, a + 1)
                    if i >= 2:
                        act.wait_ge(pt_out, a - 1)
                    s = ps[:, 2 * (i % 2):2 * (i % 2) + 2, :].rearrange("p a b -> p (a b)")
                    af(P_[i % 2][:, 0:keys_of(i)], s[:, CTX:CTX + keys_of(i)], ACT.Exp, bias=sm[:, i % 2:i % 2 + 1], scale=96 ** -0.5,
                       accum_out=sm[:, 2 + i % 2:3 + i % 2]).then_inc(pe_ready, 1)

                def take_output(i):
                    qt, h = steps[i]
                    a, p0 = ATT0[l] + i, 64 * (h % 2)
                    act.wait_ge(pv_out, a + 1)
                    af(Y[p0:p0 + 64, 4 + h // 2, 128 * qt:128 * qt + 128], ps[p0:p0 + 64, 6 + i % 2, 0:128], ACT.Copy).then_inc(pv_evac, 1)

                probabilities(0)
                for i in range(len(steps)):
                    a = ATT0[l] + i
                    if i + 1 < len(steps):
                        probabilities(i + 1)
                    if i:
                        take_output(i - 1)
                    act.wait_ge(pt_out, a + 1)
                    t = ps[:, 4:6, :].rearrange("p a b -> p (a b)")
                    af(PT[i % 2][:, 0:keys_of(i)], t[:, CTX:CTX + keys_of(i)], ACT.Copy).then_inc(pt_ready, 1)
                take_output(len(steps) - 1)
                for b in range(KB):
                    copied(l, "out", b, af(Hm[:, b, lo:], tokens(finished(l, "out", b), lo), ACT.Copy))
                act.wait_ge(gemm_evac, number(UNITS, l, "out", KB - 1) + 1)
                for b in range(KB):
                    square(l, "norm1", b, Hm[:, b, lo:], lo)
                inverse_root(l, "norm1", 0, D, KB, lo)
                act.wait_ge(x_ready, 2 * l + 1)
                for b in range(KB):
                    square(l, "norm2", b, X[:, b, lo:], lo)
                inverse_root(l, "norm2", 0, D, KB, lo)
                modulate(l, 1, A2, mod[:, 24:32, :])
                hid = R[:, :, :].rearrange("p a b -> p (a b)").rearrange("p (k t) -> p k t", t=TOK)
                for b in range(FB):
                    copied(l, "mlp1", b, af(hid[:, b, lo:], tokens(finished(l, "mlp1", b), lo), ACT.Relu, bias=zero_col))
                for b in range(KB):
                    copied(l, "mlp2", b, af(Hm[:, b, lo:], tokens(finished(l, "mlp2", b), lo), ACT.Copy))
                act.wait_ge(gemm_evac, number(UNITS, l, "mlp2", KB - 1) + 1)
                for b in range(KB):
                    square(l, "norm3", b, Hm[:, b, lo:], lo)
                inverse_root(l, "norm3", 0, D, KB, lo)

        @block.vector
        def _(dve):
            v = nc.vector
            count = [0]

            def link(ins):
                count[0] += 1
                ins.then_inc(dve_step, 1)
                dve.wait_ge(dve_step, count[0])

            def roots(l, what, i=0):
                r = number(ROOTS, l, what, i)
                dve.wait_ge(rs_ready, r + 1)
                return lnb[r % 2]

            def over_heads(ap):
                return ap.unsqueeze(1).to_broadcast([128, H, 128])

            def norm_input(l, what, lo):
                rs = roots(l, what)
                for b in range(KB):
                    v.tensor_tensor(Hm[:, b, lo:], X[:, b, lo:], rs[:, lo:], ALU.mult).then_inc(xn_ready, 1)

            def add_normed(l, what, lo, G):
                rs = roots(l, what)
                for b in range(KB):
                    link(v.tensor_tensor(Hm[:, b, lo:], Hm[:, b, lo:], rs[:, lo:], ALU.mult))
                    for a, e, s in segments(lo):
                        last = v.scalar_tensor_tensor(X[:, b, a:e], Hm[:, b, a:e], G[:, b, s:s + 1], X[:, b, a:e], ALU.mult, ALU.add)
                last.then_inc(x_ready, 1)

            for i, val in enumerate((EPS, 1.0, -0.5 * float(np.log(128.0)), 1e-19, 0.0)):
                last = v.memset(cst[:, i:i + 1], val)
            last.then_inc(consts_ready, 1)
            dve.wait_ge(mask_in, 16)
            v.tensor_copy(masks[:, :, :], R[:, 1, 0:15 * 128].rearrange("p (a b) -> p a b", b=128))
            dve.wait_ge(vT_ready, 1)
            v.tensor_copy(vecs[:, :, :], ps[:, 7, :].rearrange("p (a b) -> p a b", a=4)).then_inc(vecs_ready, 1)
            dve.wait_ge(vecs_ready, 1)
            l0, l1 = vecs[:, 1, V_LB:V_LB + 8], vecs[:, 1, V_LB + 8:V_LB + 16]
            link(v.tensor_tensor(lbt[:, 2, :], l0, l1, ALU.max))
            link(v.tensor_tensor(lbt[:, 0, :], l0, lbt[:, 2, :], ALU.subtract))
            v.tensor_tensor(lbt[:, 1, :], l1, lbt[:, 2, :], ALU.subtract).then_inc(lb_v, 1)
            v.memset(lb[:, 0, 0, :], 0.0)
            v.memset(lb[:, 0, 1, :], 1.0)
            dve.wait_ge(lb_a, 1)
            link(v.tensor_tensor(lbt[:, 2, :], lbt[:, 0, :], lbt[:, 1, :], ALU.add))
            link(v.reciprocal(lbt[:, 2, :], lbt[:, 2, :]))
            link(v.tensor_tensor(lb[:, 1, 0, :], lbt[:, 1, :], lbt[:, 2, :], ALU.mult))
            link(v.tensor_tensor(lb[:, 1, 1, :], lbt[:, 0, :], lbt[:, 2, :], ALU.mult))

            for l in range(DEPTH):
                lo = lo_of(l)
                dve.wait_ge(w_used, 36 * l + 24)
                link(v.tensor_tensor(mod[:, :, :], ps[:, 0, 0:96].rearrange("p (b s) -> p b s", s=2),
                                     vecs[:, 2 * l, 0:48].unsqueeze(2).to_broadcast([128, 48, 2]), ALU.add))

                def gains(at):
                    return vecs[:, 2 * l, at:at + 8].unsqueeze(2).to_broadcast([128, 8, 2])
                v.scalar_tensor_tensor(A1[:, :, :], mod[:, 8:16, :], 1.0, gains(V_MIXPRE), ALU.add, ALU.mult)
                v.scalar_tensor_tensor(A2[:, :, :], mod[:, 32:40, :], 1.0, gains(V_MLPPRE), ALU.add, ALU.mult)
                v.tensor_tensor(G1[:, :, :], mod[:, 16:24, :], gains(V_MIXPOST), ALU.mult)
                v.tensor_tensor(G2[:, :, :], mod[:, 40:48, :], gains(V_MLPPOST), ALU.mult).then_inc(mods_ready, 1)
                norm_input(l, "norm0", 0)
                dve.wait_ge(gemm_evac, number(UNITS, l, "ba") + 1)
                dve.wait_ge(vec_in, 32 * (l + 1))
                v.tensor_tensor(gd[:, 9, :].rearrange("p (c n) -> p c n", c=NC), ba[:, :, 8:16],
                                dtb[:, :].unsqueeze(1).to_broadcast([128, NC, 8]), ALU.add).then_inc(la_v, 1)
                for i in range(2):
                    v.memset(zpad[i][:, 0:2], 0.0)
                    v.memset(zpad[i][:, CTX + 2:CTX + 4], 0.0)
                    last = v.memset(zpad[i][:, TOK + 4:TOK + 6], 0.0)
                last.then_inc(pads_ready, 1)
                dve.wait_ge(la_a, l + 1)
                link(v.tensor_scalar(gd[:, 0, :], gd[:, 0, :], 1.0, None, ALU.add))
                link(v.reciprocal(gd[:, 0, :], gd[:, 0, :]))
                link(v.scalar_tensor_tensor(gd[:, 6, :], gd[:, 9, :], 0.0, gd[:, 6, :], ALU.max, ALU.add))
                v.scalar_tensor_tensor(gd[:, 1, :].rearrange("p (c n) -> p c n", c=NC), gd[:, 6, :].rearrange("p (c n) -> p c n", c=NC),
                                       -1.0, alog[:, :].unsqueeze(1).to_broadcast([128, NC, 8]), ALU.mult, ALU.mult).then_inc(la_ready, 1)
                for u in range(12):
                    dve.wait_ge(gemm_evac, number(UNITS, l, "qkv", u) + 1)
                    if u >= 2:
                        dve.wait_ge(silu_done, 12 * l + u - 1)
                    for j in range(CONV_W):
                        w = vecs[:, 2 * l + 1, V_CONV + 12 * j + u:V_CONV + 12 * j + u + 1]
                        z = zpad[u % 2][:, j:j + 770]
                        if j == 0:
                            link(v.tensor_scalar(cacc[u % 2], z, w, None, ALU.mult))
                        elif j < CONV_W - 1:
                            link(v.scalar_tensor_tensor(cacc[u % 2], z, w, cacc[u % 2], ALU.mult, ALU.add))
                        else:
                            v.scalar_tensor_tensor(cacc[u % 2], z, w, cacc[u % 2], ALU.mult, ALU.add).then_inc(conv_done, 1)
                dve.wait_ge(gemm_evac, number(UNITS, l, "gcum") + 1)
                raw = S[:, 0, 0:144].rearrange("p (k c d h) -> p k c d h", k=3, c=NC, d=2)
                v.tensor_copy(g_[:, :, 0, :], raw[:, 0, :, 0, :])
                v.tensor_copy(g_[:, :, 1, :], raw[:, 1, :, 1, :])
                link(v.tensor_copy(gd[:, 3, :], S[:, 0, 96:144]))
                v.tensor_scalar(gd[:, 8, :], gd[:, 0, :], -1.0, None, ALU.mult)
                v.tensor_scalar(gd[:, 9, :], gd[:, 2, :], -1.0, None, ALU.mult)
                v.tensor_tensor(gd[:, 6, :], gd[:, 3, :], gd[:, 2, :], ALU.subtract).then_inc(gs_v, 1)
                dve.wait_ge(gs_a, l + 1)
                v.tensor_tensor(gd[:, 7, :], gd[:, 0, :], gd[:, 4, :], ALU.mult).then_inc(gs_ready, 1)
                for u in range(8):
                    rs = roots(l, "l2", u)
                    t = (qT, kT)[u // 4][:, u % 4, :]
                    v.tensor_tensor(t, t, rs, ALU.mult).then_inc(l2_done, 1)
                for d in range(2):
                    base = NC * (2 * l + d)

                    def exponents(ci):
                        dve.wait_ge(p1_out, base + ci + 1)
                        G = ps[:, 3 * (ci % 2), :].rearrange("p (h d) -> p h d", h=H)
                        v.tensor_tensor(T_[:, ci % 2], over_heads(madd[1 - d]), G, ALU.subtract)
                        v.tensor_tensor(TT[:, ci % 2], G, over_heads(madd[d]), ALU.add).then_inc(p1_exp_in, 1)

                    def matrices(ci):
                        dve.wait_ge(p1_exp, base + ci + 1)
                        KK, QK = 3 * (ci % 2) + 1, 3 * (ci % 2) + 2
                        for h in range(H):
                            v.scalar_tensor_tensor(N_[:, ci, h, :], ps[:, KK, 128 * h:128 * h + 128], nbeta[:, ci, d, h:h + 1],
                                                   T_[:, ci % 2, h, :], ALU.mult, ALU.mult)
                        v.tensor_tensor(att[:, ci], ps[:, QK, :].rearrange("p (h d) -> p h d", h=H), TT[:, ci % 2], ALU.mult).then_inc(p1_done, 1)
                    for ci in range(NC):
                        exponents(ci)
                        if ci:
                            matrices(ci - 1)
                    matrices(NC - 1)
                    dve.wait_ge(p1_done, base + NC)
                    eye = ident.unsqueeze(1).to_broadcast([128, NC * H, 128])
                    v.tensor_copy(R[:, 5, :].rearrange("p (n d) -> p n d", d=128), eye)
                    link(v.tensor_copy(R[:, 6, :].rearrange("p (n d) -> p n d", d=128), eye))
                    bb = 7 * NC * (2 * l + d)
                    for i in range(7 * NC):
                        lv, ci = divmod(i, NC)
                        dve.wait_ge(b_out, bb + i + 1)
                        B, BT = 2 + 2 * (i % 2), 3 + 2 * (i % 2)
                        mT = over_heads(masks[:, lv + (0 if d == 0 else 7), :])
                        mTT = over_heads(masks[:, lv + (7 if d == 0 else 0), :])
                        if lv == 0:
                            v.copy_predicated(T_[:, ci], mT, N_[:, ci])
                        elif lv < 6:
                            v.copy_predicated(T_[:, ci], mT, ps[:, B, :].rearrange("p (h d) -> p h d", h=H))
                        v.copy_predicated(TT[:, ci], mTT, ps[:, BT, :].rearrange("p (h d) -> p h d", h=H)).then_inc(t_ready, 1)
                    for n, ci in enumerate(order(d)):
                        if n < NC - 1:
                            k = (NC - 1) * (2 * l + d) + n
                            dve.wait_ge(u_out, k + 1)
                            U = ps[:, 2 + n % 2, :].rearrange("p (h d) -> p h d", h=H)
                            if n == 0:
                                v.tensor_copy(s_of(0), U).then_inc(s_ready, 1)
                            else:
                                dve.wait_ge(s_ready, k)
                                for h in range(H):
                                    last = v.scalar_tensor_tensor(s_of(n)[:, h, :], s_of(n - 1)[:, h, :], egl[:, ci, d, h:h + 1], U[:, h, :], ALU.mult, ALU.add)
                                last.then_inc(s_ready, 1)
                        if ci in chunks_out(l):
                            dve.wait_ge(o_out, o_count(l, d, n))
                            O = ps[:, 4 + n % 2, :].rearrange("p (h d) -> p h d", h=H)
                            y = Y[:, 0:4, 128 * ci:128 * ci + 128]
                            if d == 0:
                                v.tensor_copy(y, O).then_inc(o_evac, 1)
                            else:
                                v.tensor_tensor(y, y, O, ALU.add).then_inc(o_evac, 1)

                def gated(what, u, y, gain, gate):
                    rs = roots(l, what, u)
                    link(v.tensor_tensor(y, y, rs[:, lo:], ALU.mult))
                    v.scalar_tensor_tensor(y, y, gain, gate, ALU.mult, ALU.mult).then_inc(y_ready, 1)
                dve.wait_ge(gemm_evac, number(UNITS, l, "gate", 3) + 1)
                for u in range(4):
                    gated("grms", u, Y[:, u, lo:], vecs[:, 2 * l + 1, V_GN:V_GN + 1], GT[:, u, lo:])
                for d in range(2):
                    dve.wait_ge(f_exp, 2 * l + d + 1)
                    link(v.tensor_scalar(HB[d], HB[d], 1.0, None, ALU.add))
                    link(v.reciprocal(HB[d], HB[d]))
                    for h in range(H):
                        q = 4 * d + h
                        link(v.tensor_scalar(HB[d][:, h, :], HB[d][:, h, :], lb[:, l, 1, q:q + 1], lb[:, l, 0, q:q + 1], ALU.mult, ALU.add))
                    v.tensor_scalar(HK[d], HB[d], -1.0, 1.0, ALU.mult, ALU.add).then_inc(k_done, 1)
                    dve.wait_ge(lf_done, 2 * l + d + 1)
                    for h in range(H):
                        for ci in range(NC):
                            a = HB[d][:, h, 128 * ci:128 * ci + 128]
                            if d == 1:
                                a = a[:, ::-1]
                            last = v.tensor_tensor_scan(a, ones, a, 0.0, ALU.mult, ALU.add)
                    last.then_inc(b_done, 1)
                    lvb = NLV * (2 * l + d)
                    bank = 0

                    def queries_keys(i):
                        s = (LEVELS + [0])[i]
                        dve.wait_ge(me_ready, 8 * (2 * l + d) + i + 1)
                        M = R[:, m_area(d, i), :]
                        kk, qq = (z.rearrange("p h t -> p (h t)") for z in (HK[d], HQ))
                        if s:
                            m4, k4, q4 = (z.rearrange("p (n e s) -> p n e s", e=2, s=s) for z in (M, kk, qq))
                            low, high = (k4, q4) if d == 0 else (q4, k4)
                            v.tensor_tensor(m4[:, :, 0, :], m4[:, :, 0, :], low[:, :, 0, :], ALU.mult)
                            v.tensor_tensor(m4[:, :, 1, :], m4[:, :, 1, :], high[:, :, 1, :], ALU.mult).then_inc(m_ready, 1)
                        else:
                            v.tensor_tensor(M, M, kk, ALU.mult).then_inc(m_ready, 1)

                    queries_keys(0)
                    KE = chunks(m_area(d, 0))
                    for i in range(-1, 8):
                        if 0 <= i < 7:
                            queries_keys(i + 1)
                        for ci in range(NC):
                            dve.wait_ge(lv_out, lvb + bank + 1)
                            o = ps[:, bank % 8, :].rearrange("p (h d) -> p h d", h=H)
                            if i < 0:
                                v.tensor_tensor(HATT[:, ci], o, over_heads(ident), ALU.mult).then_inc(lv_evac, 1)
                            elif i < 7:
                                dve.wait_ge(lv_evac, lvb + bank - NC + 1)
                                m = over_heads(masks[:, i + (7 if d == 0 else 0), :])
                                v.copy_predicated(HATT[:, ci], m, o).then_inc(lv_evac, 1)
                            else:
                                v.tensor_copy(KE[:, ci], o).then_inc(lv_evac, 1)
                            bank += 1
                    dve.wait_ge(eb_ready, 2 * l + d + 1)
                    v.tensor_tensor(HK[d], HQ, HB[d], ALU.mult).then_inc(hqd_ready, 1)
                    for n, ci in enumerate(order(d)):
                        if n < NC - 1:
                            k = (NC - 1) * (2 * l + d) + n
                            dve.wait_ge(hu_out, k + 1)
                            U = ps[:, n % 2, 0:256]
                            if n == 0:
                                v.tensor_copy(S[:, 0, 0:256], U).then_inc(hs_ready, 1)
                            else:
                                dve.wait_ge(hs_ready, k)
                                if n >= 2 and o_count(l, d, n - 1) > o_count(l, d, -1):
                                    dve.wait_ge(ho_out, o_count(l, d, n - 1))
                                for h in range(H):
                                    e = slice(64 * h, 64 * h + 64)
                                    last = v.scalar_tensor_tensor(S[:, n % 2, e], S[:, (n - 1) % 2, e], ebl[:, h, ci:ci + 1], U[:, e], ALU.mult, ALU.add)
                                last.then_inc(hs_ready, 1)
                        if ci in chunks_out(l):
                            dve.wait_ge(ho_out, o_count(l, d, n))
                            O = ps[:, 2 + n % 2, 0:256].rearrange("p (b t) -> p b t", b=2)
                            y = Y[:, 6:8, 128 * ci:128 * ci + 128]
                            if d == 0:
                                v.tensor_copy(y, O).then_inc(ho_evac, 1)
                            else:
                                v.tensor_tensor(y, y, O, ALU.add).then_inc(ho_evac, 1)
                for u in range(2):
                    gated("hrms", u, Y[:, 6 + u, lo:], vecs[:, 2 * l + 1, V_HN:V_HN + 1], HGT[:, u, lo:])
                rs = roots(l, "cqsum")
                for u in range(2):
                    v.scalar_tensor_tensor(CQ[:, u, :], CQ[:, u, :], vecs[:, 2 * l + 1, V_QN + u:V_QN + u + 1], rs, ALU.mult, ALU.mult).then_inc(cn_ready, 1)
                rs = roots(l, "ckvsum")
                v.scalar_tensor_tensor(CKV, CKV, vecs[:, 2 * l + 1, V_KVN:V_KVN + 1], rs, ALU.mult, ALU.mult).then_inc(cn_ready, 1)
                dve.wait_ge(rope_in, 16 * (l + 1))
                cos, sin = COS[64:96], SIN[64:96]

                def rotate(dst, src, rot):
                    link(v.tensor_tensor(rot, rot, sin, ALU.mult))
                    link(v.tensor_tensor(dst, src, cos, ALU.mult))
                    v.tensor_tensor(dst, dst, rot, ALU.add).then_inc(rope_done, 1)
                dve.wait_ge(gemm_evac, number(UNITS, l, "krrot") + 1)
                v.tensor_copy(KR[64:96, 0:CTX], KR0[64:96, 0:CTX])
                rotate(KR[64:96, CTX:TOK], KR0[64:96, CTX:TOK], KROT[64:96])
                for h in range(H):
                    dve.wait_ge(gemm_evac, number(UNITS, l, "qrot", h) + 1)
                    q = QH[64:96, h, CTX:TOK]
                    rotate(q, q, ROT[64:96, h, 0:SEQ])
                steps = att_steps(l)

                def maximum(i):
                    a = ATT0[l] + i
                    nk = CTX if steps[i][0] < NCC else TOK
                    dve.wait_ge(sc_out, a + 1)
                    s = ps[:, 2 * (i % 2):2 * (i % 2) + 2, :].rearrange("p a b -> p (a b)")
                    link(v.reduce_max(sm[:, 4 + i % 2:5 + i % 2], s[:, CTX:CTX + nk], axis=AX.X))
                    v.tensor_scalar(sm[:, i % 2:i % 2 + 1], sm[:, 4 + i % 2:5 + i % 2], -(96 ** -0.5), None, ALU.mult).then_inc(mx_ready, 1)
                maximum(0)
                for i in range(len(steps)):
                    a = ATT0[l] + i
                    nk = CTX if steps[i][0] < NCC else TOK
                    if i + 1 < len(steps):
                        maximum(i + 1)
                    dve.wait_ge(pe_ready, a + 1)
                    link(v.reciprocal(sm[:, 6 + i % 2:7 + i % 2], sm[:, 2 + i % 2:3 + i % 2]))
                    p = P_[i % 2][:, 0:nk]
                    v.tensor_scalar(p, p, sm[:, 6 + i % 2:7 + i % 2], None, ALU.mult).then_inc(p_ready, 1)
                add_normed(l, "norm1", lo, G1)
                dve.wait_ge(x_ready, 2 * l + 1)
                norm_input(l, "norm2", lo)
                hid = R[:, :, :].rearrange("p a b -> p (a b)").rearrange("p (k t) -> p k t", t=TOK)
                for b in range(FB):
                    dve.wait_ge(gemm_evac, number(UNITS, l, "mlp1", b) + 1)
                    v.tensor_tensor(hid[:, b, lo:], hid[:, b, lo:], hid[:, b, lo:], ALU.mult).then_inc(hid_ready, 1)
                add_normed(l, "norm3", lo, G2)
                dve.wait_ge(x_ready, 2 * l + 2)
            ot = R[:, 0:2, :].rearrange("p a b -> p (a b)")
            for i in range(2 * SEQ // 128):
                dve.wait_ge(out_tr, i + 1)
                v.tensor_copy(ot[:, 512 * i:512 * i + 512], ps[:, i % 4, :]).then_inc(out_evac, 1)


def constants():
    p, f = np.arange(128)[:, None], np.arange(128)[None, :]
    tri_f, tri_b = (p <= f).astype(np.float32), (p >= f).astype(np.float32)
    rot = np.zeros((128, 128), np.float32)
    for i in range(16):
        rot[64 + 16 + i, 64 + i] = -1.0
        rot[64 + i, 64 + 16 + i] = 1.0
    k_f32 = np.stack([np.eye(128), np.ones((128, 128)), (p // 64 == f // 64), rot, tri_f, tri_b,
                      NEG * (tri_f - 1), NEG * (tri_b - 1)], axis=1).astype(np.float32).reshape(128, -1)
    low = [((p // (2 * s) == f // (2 * s)) & ((p // s) % 2 == 1) & ((f // s) % 2 == 0)) for s in LEVELS]
    k_mask = np.stack(low + [m.T for m in low] + [p == f], axis=1).astype(np.float32).reshape(128, -1)
    inv = 10000.0 ** (-np.arange(0, 16, 2, dtype=np.float32) / np.float32(16))
    t = np.arange(SEQ)
    ang = np.concatenate([(t // 64)[:, None] * inv, (t % 64)[:, None] * inv], axis=1).astype(np.float32).T
    k_rope = np.concatenate([np.tile(np.cos(ang), (2, 1)), np.tile(np.sin(ang), (2, 1))], axis=1).astype(np.float32)
    return {"k_f32": k_f32, "k_mask": k_mask, "k_rope": k_rope}


_INS = ["x", "ctx", "c", "c_ctx", "w_ada", "b_ada", "norm_mix_pre", "norm_mix_post", "norm_mlp_pre", "norm_mlp_post",
        "w_in", "w_out", "gdn_conv", "gdn_a_log", "gdn_dt_bias", "gdn_norm", "mla_q_norm", "mla_kv_norm",
        "mla_w_uq", "mla_w_ukv", "hgrn_lb_logits", "hgrn_norm", "w_mlp1", "w_mlp2"]


def kernel(**inputs):
    import concourse.bacc as bacc
    from concourse.bass_utils import run_bass_kernel_spmd

    nc = bacc.Bacc("TRN2", target_bir_lowering=False, num_devices=1)
    arrays, args = {}, []
    for name, a in [(n, inputs[n]) for n in _INS] + list(constants().items()):
        a = np.ascontiguousarray(a)
        arrays[f"in_{name}"] = a
        args.append(nc.dram_tensor(f"in_{name}", a.shape, mybir.dt.from_np(a.dtype), kind="ExternalInput").ap())
    args.append(nc.dram_tensor("out_0", (1, SEQ, D), mybir.dt.float32, kind="ExternalOutput").ap())
    trunk_program(nc, *args)
    r = run_bass_kernel_spmd(nc, [arrays], core_ids=[0])
    return r.results[0]["out_0"]
```

```python
import numpy as np
import concourse.bass as bass
from concourse import mybir
from contextlib import ExitStack

D, SEQ, CTX, DEPTH = 1024, 512, 256, 2
TOK = CTX + SEQ
KB = D // 128
FF = 4 * D
FB = FF // 128
CONV_W = 5
NC = TOK // 128
NCC = CTX // 128
H = 4
EPS = 1e-6
NEG = 1.0e30
C_BA, C_CQ, C_CKV, C_HQ = 2048, 2064, 2320, 2480
C_HF, C_HI, C_HG, D_IN = 2992, 4016, 4272, 4528
LEVELS = [1, 2, 4, 8, 16, 32, 64]
V_BADA, V_MIXPRE, V_MIXPOST, V_MLPPRE, V_MLPPOST = 0, 48, 56, 64, 72
V_CONV, V_QN, V_KVN, V_GN, V_HN, V_LB, V_C = 0, 60, 62, 63, 64, 65, 81

GROUPS = DEPTH * 12
ADA_FIRST = 4
ADA_GDN, ADA_HGRN = 12, 8
LOADS = []
for _l in range(DEPTH):
    LOADS += [(_l, "ba", 0)] + [(_l, "qkv", _i) for _i in range(6)]
    LOADS += [(_l, "ada", _i) for _i in range(2 * ADA_GDN)] if _l == 0 else []
    LOADS += [(_l, "gate", _i) for _i in range(2)] + [(_l, "hq", _i) for _i in range(2)] + [(_l, "hf", _i) for _i in range(4)]
    LOADS += [(_l, "hi", 0), (_l, "hgate", 0)]
    LOADS += [(_l, "ada", 2 * ADA_GDN + _i) for _i in range(2 * ADA_HGRN)] if _l == 0 else []
    LOADS += [(_l, "cq", 0), (_l, "ckv", 0), (_l, "uq", 0), (_l, "ukv", 0)] + [(_l, "out", _i) for _i in range(4)]
    LOADS += [(_l, "mlp1", _i) for _i in range(16)] + [(_l, "mlp2", _i) for _i in range(16)]
NSLOT = 3
UNITS = ([("norm0", 0), ("ba", 0)] + [("qkv", i) for i in range(12)] + [("gcum", 0)]
         + [("l2", i) for i in range(8)] + [("ktr", i) for i in range(NC)] + [("vtr", i) for i in range(NC)]
         + [("gate", i) for i in range(4)] + [("grms", i) for i in range(4)]
         + [("hq", i) for i in range(4)] + [("hf", i) for i in range(8)] + [("hi", i) for i in range(NC)]
         + [("hgate", i) for i in range(2)] + [("hrms", i) for i in range(2)]
         + [("cq", i) for i in range(2)] + [("ckv", 0), ("kr", 0), ("cqsum", 0), ("ckvsum", 0), ("krrot", 0)]
         + [("uq", i) for i in range(4)] + [("qrot", i) for i in range(4)] + [("uk", i) for i in range(4)]
         + [("vt", i) for i in range(NC)] + [("out", i) for i in range(KB)] + [("norm1", 0), ("norm2", 0)]
         + [("mlp1", i) for i in range(FB)] + [("mlp2", i) for i in range(KB)] + [("norm3", 0)])
SQUARES = ([("norm0", i) for i in range(8)] + [("l2", i) for i in range(8)] + [("grms", i) for i in range(4)]
           + [("hrms", i) for i in range(2)] + [("cqsum", i) for i in range(2)] + [("ckvsum", 0)]
           + [(f"norm{n}", i) for n in (1, 2, 3) for i in range(8)])


def number(table, layer, what, i=0):
    return layer * len(table) + table.index((what, i))


SUMS = ("norm0", "l2", "grms", "hrms", "cqsum", "ckvsum", "norm1", "norm2", "norm3")
ROOTS = [u for u in UNITS if u[0] in SUMS]
NOT_SUMS = [u for u in UNITS if u[0] not in SUMS]


def out_number(layer, what, i=0):
    return number(NOT_SUMS, layer, what, i) + 1


def trunk_program(nc, x, ctx, c, c_ctx, w_ada, b_ada, norm_mix_pre, norm_mix_post, norm_mlp_pre, norm_mlp_post,
                  w_in, w_out, gdn_conv, gdn_a_log, gdn_dt_bias, gdn_norm, mla_q_norm, mla_kv_norm,
                  mla_w_uq, mla_w_ukv, hgrn_lb_logits, hgrn_norm, w_mlp1, w_mlp2,
                  k_f32, k_mask, k_rope, out):
    f32, u8 = mybir.dt.float32, mybir.dt.uint8
    ALU, ACT, AX = mybir.AluOpType, mybir.ActivationFunctionType, mybir.AxisListType
    stack = ExitStack()
    with stack:
        def sb(name, shape, dt=f32):
            return stack.enter_context(nc.sbuf_tensor(name, shape, dt))

        def sem(name):
            return stack.enter_context(nc.semaphore(name))

        X = sb("residual", [128, KB, TOK])
        Hm = sb("modulated", [128, KB, TOK])
        Y = sb("mixed", [128, KB, TOK])
        R = sb("region", [128, 8, 4 * TOK])
        ring = sb("weights", [128, NSLOT, 2048])
        kf = sb("k_f32_sb", [128, 8, 128])
        masks = sb("masks", [128, 15, 128], u8)
        vecs = sb("vecs", [128, 4, 128])
        mods = sb("modulation", [128, DEPTH, 48, 2])
        A1, A2, G1, G2 = (sb(n, [128, KB, 2]) for n in ("pre_gain1", "pre_gain2", "post_gain1", "post_gain2"))
        cs = sb("silu_c", [128, KB, 2])
        S = sb("state", [128, 2, 512])
        ba = sb("ba", [128, NC, 16])
        gd = sb("gdn_small", [128, 10, 48])
        alog, dtb = sb("alog", [128, 8]), sb("dtb", [128, 8])
        cst = sb("cst", [128, 8])
        lb = sb("lower_bound", [128, DEPTH, 2, 8])
        lbt = sb("lb_tmp", [128, 4, 8])
        sm = sb("small", [128, 16])
        ebl = sb("decay_last", [128, H, NC])
        ps = stack.enter_context(nc.psum_tensor("ps", [128, 8, 512], f32))

        ident, ones, bd64, rotp = kf[:, 0, :], kf[:, 1, :], kf[:, 2, :], kf[:, 3, :]
        tri, madd = (kf[:, 4, :], kf[:, 5, :]), (kf[:, 6, :], kf[:, 7, :])
        eps_col, one_col, lnq_col, tiny_col, zero_col = (cst[:, i:i + 1] for i in range(5))

        def pair(n):
            return ps[:, 2 * (n % 4):2 * (n % 4) + 2, :].rearrange("p a b -> p (a b)")

        def tokens(ap, lo=0):
            return ap[:, CTX + lo:CTX + TOK]

        def blocks(area):
            return R[:, area, :].rearrange("p (h t) -> p h t", t=TOK)

        def chunks(area):
            return R[:, area, :].rearrange("p (c h d) -> p c h d", c=NC, h=H)

        qT, kT, ktok, vtok, vT = blocks(0), blocks(1), chunks(2), chunks(3), blocks(5)
        N_, T_, TT, att = chunks(4), chunks(5), chunks(6), chunks(7)
        Yf = Y[:, :, :].rearrange("p a b -> p (a b)")

        def square_buffer(what, i, n):
            if what in ("norm0", "norm3"):
                return Y[:, i, :]
            if what in ("norm1", "norm2"):
                return blocks((5 if what == "norm1" else 3) + i // 4)[:, i % 4, :]
            return R[:, 6, TOK * (n % 4):TOK * (n % 4 + 1)]
        lnb = [R[:, 7, TOK * i:TOK * (i + 1)] for i in range(2)]
        zpad = [R[:, 6, i * 776:i * 776 + 774] for i in range(2)]
        cacc = [R[:, 7, i * 776:i * 776 + 770] for i in range(2)]

        def piece(i):
            return Yf[:, 4 * TOK + 512 * i:4 * TOK + 512 * (i + 1)].rearrange("p (h d) -> p h d", h=H)
        Csb = vb = [piece(0), piece(1)]
        kbg = kend = [piece(2), piece(3)]
        VN = [piece(4), piece(5)]
        beta, la, g_, gl, eg, egl, kd, bg, nbeta, ng = (gd[:, i, :].rearrange("p (c d h) -> p c d h", c=NC, d=2) for i in range(10))

        def s_of(n):
            return S[:, n % 2, :].rearrange("p (h d) -> p h d", h=H)

        def order(d):
            return list(range(NC)) if d == 0 else list(range(NCC))[::-1] + list(range(NCC, NC))[::-1]

        mask_in, ada_in = sem("mask_in"), sem("ada_in")
        ada_out, ada_row, ada_tr, ada_read = sem("ada_out"), sem("ada_row"), sem("ada_transposed"), sem("ada_read")
        rows_clear = sem("rows_clear")
        rows1_in, vT1_ready = sem("rows1_in"), sem("vecT1_ready")
        const_in, rows_in, x_in, vec_in, rope_in = sem("const_in"), sem("rows_in"), sem("x_in"), sem("vec_in"), sem("rope_in")
        w_in_s = [sem(f"w_loaded{i}") for i in range(NSLOT)]
        w_used = sem("w_used")
        gemm_out, gemm_evac = sem("gemm_out"), sem("gemm_evac")
        sq_ready, sq_used, rs_ready, rs_used = sem("sq_ready"), sem("sq_used"), sem("rs_ready"), sem("rs_used")
        xT_ready, xT_evac, vT_ready = sem("xT_ready"), sem("xT_evac"), sem("vecT_ready")
        consts_ready, vecs_ready, cs_ready, mods_ready = sem("consts_ready"), sem("vecs_ready"), sem("cs_ready"), sem("mods_ready")
        x_ready, xn_ready, h_ready = sem("x_ready"), sem("xn_ready"), sem("h_ready")
        pads_ready, conv_done, silu_done, l2_done = sem("pads_ready"), sem("conv_done"), sem("silu_done"), sem("l2_done")
        la_a, la_v, la_ready, gs_a, gs_v, gs_ready = (sem(n) for n in ("ba_exps", "ba_sums", "la_ready", "g_split", "g_diff", "g_ready"))
        p1_out, p1_exp_in, p1_exp, p1_done = (sem(n) for n in ("p1_out", "p1_exponents", "p1_decays", "p1_done"))
        c_out, c_evac, b_out, t_ready = (sem(n) for n in ("c_out", "c_evac", "b_out", "t_ready"))
        kbg_ready, w_out_s, wt_ready, eg_exp, qd_ready = (sem(n) for n in ("kbg_ready", "w_out_s", "wt_ready", "eg_exp", "qd_ready"))
        vb_ready, kend_ready, v_out, vn_ready, u_out, s_ready, o_out, o_evac = (
            sem(n) for n in ("vb_ready", "kend_ready", "v_out", "vn_ready", "u_out", "s_ready", "o_out", "o_evac"))
        f_exp, f_done, k_done, lf_done, b_done = (sem(n) for n in ("f_exp", "f_done", "k_done", "lf_done", "b_done"))
        md_ready, me_ready, m_ready, lv_out, lv_evac, eb_ready, hqd_ready = (
            sem(n) for n in ("md_ready", "me_ready", "m_ready", "lv_out", "lv_evac", "eb_ready", "hqd_ready"))
        hu_out, hs_ready, ho_out, ho_evac, lb_a, lb_v, lb_ready = (
            sem(n) for n in ("hu_out", "hs_ready", "ho_out", "ho_evac", "lb_exps", "lb_diff", "lb_ready"))
        y_ready, cn_ready, rope_done, kr_copied = sem("y_ready"), sem("cn_ready"), sem("rope_done"), sem("kr_copied")
        sc_out, mx_ready, pe_ready, p_ready, pt_out, pt_ready, pv_out, pv_evac = (
            sem(n) for n in ("sc_out", "mx_ready", "p_exp", "p_ready", "pt_out", "pt_ready", "pv_out", "pv_evac"))
        out_ready, out_tr, out_evac, hid_ready = sem("out_ready"), sem("out_tr"), sem("out_evac"), sem("hid_ready")
        dve_step, act_step, pool_step = sem("dve_step"), sem("act_step"), sem("pool_step")
        block = stack.enter_context(nc.Block())

        def lo_of(l):
            return 0 if l < DEPTH - 1 else CTX

        def chunks_out(l):
            return [ci for ci in range(NC) if ci * 128 >= lo_of(l)]

        def segments(lo):
            return ([(0, CTX, 1)] if lo == 0 else []) + [(CTX, TOK, 0)]

        NU, NSQ = len(UNITS), len(SQUARES)
        def att_steps(l):
            return [(qt, h) for qt in chunks_out(l) for h in range(H)]
        ATT0 = [0, len(att_steps(0)), len(att_steps(0)) + len(att_steps(1))]
        NLV = 9 * NC

        def o_count(l, d, n):
            full = 2 * NC * l
            outs = [ci in chunks_out(l) for ci in order(d)]
            return full + d * len(chunks_out(l)) + sum(outs[:n + 1])

        def slot(l, what, i=0):
            return LOADS.index((l, what, i)) % NSLOT

        def weights_used(n):
            l, what, i = LOADS[n]
            if what == "ada":
                return (w_used, i // 2 + 1) if i % 2 == 0 else (ada_tr, ADA_FIRST + i // 2 + 1)
            if what == "mlp2":
                g, kg = divmod(i, 4)
                return (w_used, ADA_GDN + ADA_HGRN + 12 * l + 3 * g + kg + 1) if kg < 3 else (gemm_out, out_number(l, "mlp2", 2 * g + 1))
            last = {"ba": ("ba", 0), "qkv": ("qkv", 2 * i + 1), "gate": ("gate", 2 * i + 1), "hq": ("hq", 2 * i + 1),
                    "hf": ("hf", 2 * i + 1), "hi": ("hi", NC - 1), "hgate": ("hgate", 1), "cq": ("cq", 1), "ckv": ("kr", 0),
                    "uq": ("uq", 3), "ukv": ("vt", NC - 1), "out": ("out", 2 * i + 1), "mlp1": ("mlp1", 2 * i + 1)}[what]
            return gemm_out, out_number(l, *last)

        GT = blocks(5)
        CQ, CKV = blocks(0)[:, 0:2, :], blocks(0)[:, 2, :]
        KR, ROT = blocks(0)[:, 3, :], blocks(5)
        QH, KH, VT = blocks(1), blocks(2), R[:, 3, 0:NC * 256].rearrange("p (c e) -> p c e", c=NC)
        KR0, KROT = R[:, 3, 2 * TOK:3 * TOK], R[:, 3, 3 * TOK:3 * TOK + SEQ]
        COS, SIN = R[:, 7, 2 * TOK:2 * TOK + SEQ], R[:, 7, 2 * TOK + SEQ:2 * TOK + 2 * SEQ]
        P_ = [R[:, 4, 0:TOK], R[:, 4, TOK:2 * TOK]]
        PT = [R[:, 4, 2 * TOK:3 * TOK], R[:, 4, 3 * TOK:4 * TOK]]
        HQ, HV, HGT = blocks(0), R[:, 1, 0:NC * 256].rearrange("p (c e) -> p c e", c=NC), R[:, 1, 2 * TOK:4 * TOK].rearrange("p (b t) -> p b t", b=2)
        HK, HB = (blocks(2), blocks(4)), (blocks(3), blocks(5))
        HATT = chunks(7)
        MB = [R[:, 6, 0:1536], R[:, 6, 1536:3072], Y[:, 4:6, :].rearrange("p a b -> p (a b)")]

        def m_piece(d, m):
            return MB[(16 * d + m) % 3]

        def level(d, m):
            i = m // 2
            if i == 7:
                return 128, (127 if d == 0 else 0)
            return 2 * LEVELS[i], (LEVELS[i] - 1 if d == 0 else LEVELS[i])

        def part(ap, m):
            return ap[:, :, 384 * (m % 2):384 * (m % 2) + 384]

        def ada_weights(g, half):
            l, g = divmod(g, 12)
            return w_ada[l][512 * half:512 * half + 512, 512 * g:512 * g + 512]
        ada_first = R[:, 2:8, :].rearrange("p a b -> p (a b)")[:, 0:2 * ADA_FIRST * 2048].rearrange("p (i n) -> p i n", n=2048)

        @block.sync
        def _(sp):
            sp.dma_start(kf[:, :, :], k_f32.rearrange("p (a b) -> p a b", b=128)).then_inc(const_in, 16)
            sp.dma_start(R[:, 1, 0:15 * 128], k_mask).then_inc(mask_in, 16)
            xt = Hm[:, :, :].rearrange("p a b -> p (a b)").rearrange("p (c f) -> p c f", c=NC)
            sp.dma_start(xt[:, 0:NCC, :], ctx[0].rearrange("(c p) f -> p c f", p=128)).then_inc(x_in, 16)
            sp.dma_start(xt[:, NCC:NC, :], x[0].rearrange("(c p) f -> p c f", p=128)).then_inc(x_in, 16)
            for i in range(2 * ADA_FIRST):
                sp.dma_start(ada_first[:, i, :].rearrange("p (k n) -> p k n", n=512),
                             ada_weights(i // 2, i % 2).rearrange("(k p) n -> p k n", p=128)).then_inc(ada_in, 16)
            for l in range(DEPTH):
                for n, (_, what, i) in [(n, load) for n, load in enumerate(LOADS) if load[0] == l]:
                    if n >= NSLOT:
                        sp.wait_ge(*weights_used(n - NSLOT))
                    wide = 256
                    if what == "ada":
                        src, wide = ada_weights(ADA_FIRST + i // 2, i % 2), 512
                    elif what == "ba":
                        src, wide = w_in[l][:, C_BA:C_CQ], 16
                    elif what == "ckv":
                        src, wide = w_in[l][:, C_CKV:C_HQ], C_HQ - C_CKV
                    elif what in ("qkv", "gate", "hq", "hf", "hi", "hgate", "cq"):
                        c0 = {"qkv": 0, "gate": 1536, "hq": C_HQ, "hf": C_HF, "hi": C_HI, "hgate": C_HG, "cq": C_CQ}[what] + 256 * i
                        src = w_in[l][:, c0:c0 + 256]
                    elif what == "uq":
                        src, wide = mla_w_uq[l], 384
                    elif what == "ukv":
                        src, wide = mla_w_ukv[l], 512
                    elif what == "out":
                        src = w_out[l][:, 256 * i:256 * i + 256]
                    elif what == "mlp1":
                        src = w_mlp1[l][:, 256 * i:256 * i + 256]
                    else:
                        src = w_mlp2[l][1024 * (i % 4):1024 * (i % 4) + 1024, 256 * (i // 4):256 * (i // 4) + 256]
                    ks = src.shape[0] // 128
                    sp.dma_start(ring[:, n % NSLOT, 0:ks * wide].rearrange("p (k n) -> p k n", k=ks),
                                 src.rearrange("(k p) n -> p k n", p=128)).then_inc(w_in_s[n % NSLOT], 16)
            ot = R[:, 0:2, :].rearrange("p a b -> p (a b)")
            for ci in range(SEQ // 128):
                sp.wait_ge(out_evac, 2 * ci + 2)
                sp.dma_start(out[0, 128 * ci:128 * ci + 128, :], ot[:, 1024 * ci:1024 * ci + 1024]).then_inc(out_ready, 16)
            sp.wait_ge(out_ready, 16 * (SEQ // 128))

        rows = R[:, 0, 0:512].rearrange("p (a b) -> p a b", b=128)

        def load_rows(eng, l, arrived_sem):
            for t, at, src in ((0, V_BADA, b_ada[l]), (0, V_MIXPRE, norm_mix_pre[l]), (0, V_MIXPOST, norm_mix_post[l]),
                               (0, V_MLPPRE, norm_mlp_pre[l]), (0, V_MLPPOST, norm_mlp_post[l]),
                               (1, V_QN, mla_q_norm[l]), (1, V_KVN, mla_kv_norm[l]), (1, V_GN, gdn_norm[l]), (1, V_C, c[0]), (1, V_C + 8, c_ctx)):
                n = src.shape[0] // 128
                eng.dma_start(rows[at:at + n, 2 * l + t, :], src.rearrange("(r f) -> r f", f=128)).then_inc(arrived_sem, 16)
            eng.dma_start(rows[V_CONV:V_CONV + 60, 2 * l + 1, :], gdn_conv[l].rearrange("w (r f) -> (w r) f", f=128)).then_inc(arrived_sem, 16)
            eng.dma_start(rows[V_LB:V_LB + 16, 2 * l + 1, :],
                          hgrn_lb_logits.rearrange("l d (r f) -> (l d r) f", f=128)).then_inc(arrived_sem, 16)
            for half in range(2):
                eng.dma_start(rows[V_HN:V_HN + 1, 2 * l + 1, 64 * half:64 * half + 64],
                              hgrn_norm[l].rearrange("(r f) -> r f", r=1)).then_inc(arrived_sem, 16)

        @block.gpsimd
        def _(pool):
            count = [0]

            def link(ins):
                count[0] += 1
                ins.then_inc(pool_step, 1)
                pool.wait_ge(pool_step, count[0])

            pool.wait_ge(rows_clear, 1)
            load_rows(pool, 1, rows1_in)
            for l in range(DEPTH):
                if l:
                    pool.wait_ge(la_ready, l)
                pool.dma_start(alog[:, :], gdn_a_log[l].rearrange("d h -> (d h)").partition_broadcast(128)).then_inc(vec_in, 16)
                pool.dma_start(dtb[:, :], gdn_dt_bias[l].rearrange("d h -> (d h)").partition_broadcast(128)).then_inc(vec_in, 16)
                pool.wait_ge(gs_ready, l + 1)
                for d in range(2):
                    base = NC * (2 * l + d)
                    for ci in range(NC):
                        if ci == 0:
                            pool.wait_ge(gemm_evac, number(UNITS, l, "vtr", NC - 1) + 1)
                            pool.wait_ge(t_ready, 7 * NC * (2 * l + d) + 7 * NC)
                            if d == 1:
                                pool.wait_ge(u_out, (NC - 1) * (2 * l + 1))
                        if ci >= 2:
                            pool.wait_ge(w_out_s, base + ci - 1)
                        nc.gpsimd.tensor_tensor(kbg[ci % 2], ktok[:, ci], bg[:, ci, d, :].unsqueeze(2).to_broadcast([128, H, 128]),
                                                ALU.mult).then_inc(kbg_ready, 1)
                        pool.wait_ge(eg_exp, base + ci + 1)
                        nc.gpsimd.tensor_tensor(T_[:, ci], T_[:, ci], qT[:, :, 128 * ci:128 * ci + 128], ALU.mult).then_inc(qd_ready, 1)
                    for n, ci in enumerate(order(d)):
                        if n >= 2:
                            pool.wait_ge(v_out, base + n - 1)
                        nc.gpsimd.tensor_tensor(vb[n % 2], vtok[:, ci], beta[:, ci, d, :].unsqueeze(2).to_broadcast([128, H, 128]),
                                                ALU.mult).then_inc(vb_ready, 1)
                        if n < NC - 1:
                            if n < 2:
                                pool.wait_ge(w_out_s, base + NC - 1 + n)
                            else:
                                pool.wait_ge(u_out, (NC - 1) * (2 * l + d) + n - 1)
                            nc.gpsimd.tensor_tensor(kend[n % 2], ktok[:, ci], kd[:, ci, d, :].unsqueeze(2).to_broadcast([128, H, 128]),
                                                    ALU.mult).then_inc(kend_ready, 1)
                pool.wait_ge(sq_used, number(SQUARES, l, "grms", 3) + 1)
                for d in range(2):
                    pool.wait_ge(b_done, 2 * l + d + 1)
                    for m in range(16):
                        d3, m3 = divmod(16 * d + m - 3, 16)
                        if d3 >= 0:
                            pool.wait_ge(lv_out, NLV * (2 * l + d3) + NC + 3 * (m3 + 1))
                        wide, at = level(d, m)
                        b = part(HB[d], m).rearrange("p h (n s) -> p h n s", s=wide)
                        nc.gpsimd.tensor_tensor(m_piece(d, m).rearrange("p (h n s) -> p h n s", h=H, s=wide), b,
                                                b[:, :, :, at:at + 1].to_broadcast([128, H, 384 // wide, wide]), ALU.subtract).then_inc(md_ready, 1)
                pool.wait_ge(ho_evac, o_count(l, 1, NC - 1))
                pool.dma_start(R[64:96, 7, 2 * TOK:2 * TOK + 2 * SEQ], k_rope).then_inc(rope_in, 16)
                pool.wait_ge(rope_done, 5 * l + 1)
                for h in range(H):
                    ins = nc.gpsimd.tensor_copy(KH[64:96, h, :], KR[64:96, :])
                ins.then_inc(kr_copied, 1)

        @block.tensor
        def _(pe):
            mm, tr = nc.tensor.matmul, nc.tensor.transpose

            def arrived(l, what, i=0):
                n = LOADS.index((l, what, i))
                pe.wait_ge(w_in_s[n % NSLOT], 16 * (n // NSLOT + 1))
                return ring[:, n % NSLOT, :]

            def free_pair(l, what, i=0):
                n = number(UNITS, l, what, i)
                if n >= 4:
                    pe.wait_ge(gemm_evac, n - 3)
                return pair(n)

            def streams(lo):
                return ([(0, CTX)] if lo == 0 else []) + [(CTX, TOK)]

            def project(dst, w, rhs, ks, m0, m, lo=0, first=True, final=True, h_before=None):
                for k in range(ks):
                    if h_before is not None:
                        pe.wait_ge(h_ready, h_before + k + 1)
                    for a, b in streams(lo):
                        last = mm(dst[0:m, CTX + a:CTX + b], w[:, k, m0:m0 + m], rhs[:, k, a:b],
                                  start=(first and k == 0), stop=(final and k == ks - 1))
                return last

            def gemm(l, what, load, units, rhs, lo=0, wide=256, h_before=None):
                w = arrived(l, what, load)[:, 0:KB * wide].rearrange("p (k n) -> p k n", k=KB)
                for j, u in enumerate(units):
                    dst = free_pair(l, what, u)
                    last = project(dst, w, rhs, KB, 128 * j, 128, lo, h_before=h_before)
                    last.then_inc(gemm_out, 1)

            def sum_squares(l, what, n0, n, mat, lo=0):
                dst = free_pair(l, what, n0)
                first = number(SQUARES, l, what, 0 if n > 1 else n0)
                for k in range(n):
                    pe.wait_ge(sq_ready, first + k + 1)
                    sq = square_buffer(what, k if n > 1 else n0, first + k)
                    for a, b in streams(lo):
                        last = mm(dst[:, CTX + a:CTX + b], mat, sq[:, a:b], start=(k == 0), stop=(k == n - 1))
                    last.then_inc(sq_used, 1)

            pe.wait_ge(const_in, 16)
            pe.wait_ge(x_in, 32)
            xt = Hm[:, :, :].rearrange("p a b -> p (a b)").rearrange("p (c f) -> p c f", c=NC)
            for i in range(2 * NC):
                if i >= 4:
                    pe.wait_ge(xT_evac, i - 3)
                for j in range(4):
                    f0 = 512 * (i % 2) + 128 * j
                    last = tr(ps[:, i % 4, 128 * j:128 * j + 128], xt[:, i // 2, f0:f0 + 128], ident)
                last.then_inc(xT_ready, 1)
            for l, s_in, s_out in ((0, rows_in, vT_ready), (1, rows1_in, vT1_ready)):
                pe.wait_ge(s_in, 16 * 14)
                for i in (2 * l, 2 * l + 1):
                    last = tr(ps[:, 5 + l, 128 * (i % 2):128 * (i % 2) + 128], rows[:, i, :], ident)
                last.then_inc(s_out, 1)

            def ada_half(g, half, w, dst):
                for k in range(4):
                    last = mm(dst, cs[:, 4 * half + k, :], w[:, k, :], start=(half == 0 and k == 0), stop=(half == 1 and k == 3))
                return last

            def ada_columns(g, row, q, col):
                pe.wait_ge(ada_row, g + 1)
                for j in range(4):
                    last = tr(ps[:, 7, col + 2 * j:col + 2 * j + 2], row[q:q + 2, 128 * j:128 * j + 128], ident[q:q + 2, q:q + 2])
                last.then_inc(ada_tr, 1)

            def ada_point(p, first):
                g = ADA_FIRST + p // 2
                if p % 2 == 1 and p > first + 1:
                    ada_finish(p - 3, first)
                q = 32 * (g % 2)
                w = arrived(0, "ada", p)
                if p % 2 == 0 and p >= first + 4:
                    pe.wait_ge(ada_row, g - 1)
                last = ada_half(g, p % 2, w.rearrange("p (k n) -> p k n", n=512), ps[q:q + 2, 6, :])
                last.then_inc(*((w_used, 1) if p % 2 == 0 else (ada_out, 1)))

            def ada_finish(p, first):
                g = ADA_FIRST + p // 2
                ada_columns(g, ring[:, LOADS.index((0, "ada", p + 1)) % NSLOT, :], 32 * (g % 2), 4 * (p - first))

            for l in range(DEPTH):
                lo = lo_of(l)
                if l == 0:
                    pe.wait_ge(cs_ready, 1)
                    pe.wait_ge(xT_evac, 2 * NC)
                    for g in range(ADA_FIRST):
                        pe.wait_ge(ada_in, 16 * 2 * ADA_FIRST)
                        for half in range(2):
                            last = ada_half(g, half, ada_first[:, 2 * g + half, :].rearrange("p (k n) -> p k n", n=512), ps[0:2, g, :])
                        last.then_inc(ada_out, 1)
                    for g in range(ADA_FIRST):
                        ada_columns(g, ada_first[:, 2 * g + 1, :], 0, 8 * g)
                pe.wait_ge(mods_ready, l + 1)
                sum_squares(l, "norm0", 0, KB, ones)
                dst = free_pair(l, "ba")
                w = arrived(l, "ba")[:, 0:KB * 16].rearrange("p (k n) -> p k n", k=KB)
                for ci in range(NC):
                    for k in range(KB):
                        if ci == 0:
                            pe.wait_ge(h_ready, 16 * l + k + 1)
                        last = mm(dst[:, 512 + 16 * ci:512 + 16 * ci + 16], Hm[:, k, 128 * ci:128 * ci + 128], w[:, k, :],
                                  start=(k == 0), stop=(k == KB - 1))
                last.then_inc(gemm_out, 1)
                for i in range(6):
                    gemm(l, "qkv", i, [2 * i, 2 * i + 1], Hm)
                pe.wait_ge(la_ready, l + 1)
                dst = free_pair(l, "gcum")
                for i, m in enumerate((tri[0], tri[1], ones)):
                    last = mm(dst[:, 512 + 48 * i:512 + 48 * i + 48], m, gd[:, 1, :], start=True, stop=True)
                last.then_inc(gemm_out, 1)
                for u in range(8):
                    sum_squares(l, "l2", u, 1, ones)
                pe.wait_ge(l2_done, 8 * (l + 1))
                pe.wait_ge(silu_done, 12 * (l + 1))
                for what, src in (("ktr", kT), ("vtr", vT)):
                    for ci in range(NC):
                        dst = free_pair(l, what, ci)
                        for h in range(H):
                            last = tr(dst[:, 512 + 128 * h:512 + 128 * h + 128], src[:, h, 128 * ci:128 * ci + 128], ident)
                        last.then_inc(gemm_out, 1)
                pe.wait_ge(gs_ready, l + 1)
                pe.wait_ge(gemm_evac, number(UNITS, l, "vtr", NC - 1) + 1)

                for d in range(2):
                    base = NC * (2 * l + d)
                    for ci in range(NC):
                        if ci >= 2:
                            pe.wait_ge(p1_done, base + ci - 1)
                        elif d == 1:
                            pe.wait_ge(o_evac, o_count(l, 0, NC - 1))
                        if l == 0:
                            ada_point(2 * NC * d + ci, 0)
                        G, KK, QK = (3 * (ci % 2) + j for j in range(3))
                        cc = slice(128 * ci, 128 * ci + 128)
                        for h in range(H):
                            mm(ps[:, G, 128 * h:128 * h + 128], la[:, ci, d, h:h + 1].to_broadcast([128, 128]), tri[d], start=True, stop=True)
                        for h in range(H):
                            mm(ps[:, KK, 128 * h:128 * h + 128], kT[:, h, cc], kT[:, h, cc], start=True, stop=True)
                        for h in range(H):
                            last = mm(ps[:, QK, 128 * h:128 * h + 128], kT[:, h, cc], qT[:, h, cc], start=True, stop=True)
                        last.then_inc(p1_out, 1)
                    tb = 7 * NC * (2 * l + d)
                    cb = 6 * NC * (2 * l + d)
                    steps = [(lv, ci) for lv in range(7) for ci in range(NC)]
                    pe.wait_ge(p1_done, base + NC)

                    def c_product(i):
                        lv, ci = steps[i]
                        j = i - NC
                        pe.wait_ge(t_ready, tb + i - NC + 1)
                        if j >= 2:
                            pe.wait_ge(c_evac, cb + j - 1)
                        for h in range(H):
                            last = mm(ps[:, j % 2, 128 * h:128 * h + 128], N_[:, ci, h, :], TT[:, ci, h, :], start=True, stop=True)
                        last.then_inc(c_out, 1)
                    for i, (lv, ci) in enumerate(steps):
                        if i == NC - 1:
                            c_product(NC)
                        elif i >= NC and i + 1 < len(steps):
                            c_product(i + 1)
                        B, BT = 2 + 2 * (i % 2), 3 + 2 * (i % 2)
                        if i >= 2:
                            pe.wait_ge(t_ready, tb + i - 1)
                        if lv == 0:
                            for h in range(H):
                                last = tr(ps[:, BT, 128 * h:128 * h + 128], N_[:, ci, h, :], ident)
                        else:
                            j = i - NC
                            pe.wait_ge(c_evac, cb + j + 1)
                            for h in range(H):
                                last = mm(ps[:, BT, 128 * h:128 * h + 128], T_[:, ci, h, :], Csb[j % 2][:, h, :], start=True, stop=True)
                            if lv < 6:
                                for h in range(H):
                                    last = mm(ps[:, B, 128 * h:128 * h + 128], Csb[j % 2][:, h, :], T_[:, ci, h, :], start=True, stop=True)
                        last.then_inc(b_out, 1)
                    pe.wait_ge(t_ready, tb + 7 * NC)
                    for ci in range(NC):
                        if ci >= 2:
                            pe.wait_ge(eg_exp, base + ci - 1)
                            pe.wait_ge(wt_ready, base + ci - 1)
                        G, W = 2 * (ci % 2), 2 * (ci % 2) + 1
                        for h in range(H):
                            mm(ps[:, G, 128 * h:128 * h + 128], la[:, ci, d, h:h + 1].to_broadcast([128, 128]), tri[d], start=True, stop=True)
                        pe.wait_ge(kbg_ready, base + ci + 1)
                        for h in range(H):
                            last = mm(ps[:, W, 128 * h:128 * h + 128], kbg[ci % 2][:, h, :], TT[:, ci, h, :], start=True, stop=True)
                        last.then_inc(w_out_s, 1)
                    pe.wait_ge(eg_exp, base + NC)
                    pe.wait_ge(wt_ready, base + NC)
                    pe.wait_ge(qd_ready, base + NC)
                    for n, ci in enumerate(order(d)):
                        if l == 0:
                            ada_point(2 * NC * d + NC + n, 0)
                        V, U, O = n % 2, 2 + n % 2, 4 + n % 2
                        pe.wait_ge(vb_ready, base + n + 1)
                        if n:
                            pe.wait_ge(s_ready, (NC - 1) * (2 * l + d) + n)
                        for h in range(H):
                            o = ps[:, V, 128 * h:128 * h + 128]
                            last = mm(o, TT[:, ci, h, :], vb[n % 2][:, h, :], start=True, stop=(n == 0))
                            if n:
                                last = mm(o, N_[:, ci, h, :], s_of(n - 1)[:, h, :], start=False, stop=True)
                        last.then_inc(v_out, 1)
                        pe.wait_ge(vn_ready, base + n + 1)
                        if n < NC - 1:
                            pe.wait_ge(kend_ready, (NC - 1) * (2 * l + d) + n + 1)
                            for h in range(H):
                                last = mm(ps[:, U, 128 * h:128 * h + 128], kend[n % 2][:, h, :], VN[n % 2][:, h, :], start=True, stop=True)
                            last.then_inc(u_out, 1)
                        if ci in chunks_out(l):
                            k = o_count(l, d, n)
                            if k > o_count(l, d, -1) + 2:
                                pe.wait_ge(o_evac, k - 2)
                            for h in range(H):
                                o = ps[:, O, 128 * h:128 * h + 128]
                                if n:
                                    mm(o, s_of(n - 1)[:, h, :], T_[:, ci, h, :], start=True, stop=False)
                                last = mm(o, VN[n % 2][:, h, :], att[:, ci, h, :], start=(n == 0), stop=True)
                            last.then_inc(o_out, 1)
                if l == 0:
                    ada_finish(2 * ADA_GDN - 2, 0)
                    pe.wait_ge(ada_read, 1)
                pe.wait_ge(o_evac, o_count(l, 1, NC - 1))
                for i in range(2):
                    gemm(l, "gate", i, [2 * i, 2 * i + 1], Hm, lo)
                for u in range(4):
                    sum_squares(l, "grms", u, 1, ones, lo)
                for i in range(2):
                    gemm(l, "hq", i, [2 * i, 2 * i + 1], Hm)
                for i in range(4):
                    gemm(l, "hf", i, [2 * i, 2 * i + 1], Hm)
                w = arrived(l, "hi").rearrange("p (k n) -> p k n", k=KB)
                for ci in range(NC):
                    dst = free_pair(l, "hi", ci)
                    for k in range(KB):
                        last = mm(dst[:, 512:768], Hm[:, k, 128 * ci:128 * ci + 128], w[:, k, :], start=(k == 0), stop=(k == KB - 1))
                    last.then_inc(gemm_out, 1)
                gemm(l, "hgate", 0, [0, 1], Hm, lo)
                pe.wait_ge(gemm_evac, number(UNITS, l, "hgate", 1) + 1)

                for d in range(2):
                    lvb = NLV * (2 * l + d)
                    bank = 0
                    if d == 1:
                        pe.wait_ge(ho_evac, o_count(l, 0, NC - 1))
                    pe.wait_ge(k_done, 2 * l + d + 1)
                    for m in range(-2, 16):
                        if m >= 0:
                            pe.wait_ge(m_ready, 16 * (2 * l + d) + m + 1)
                            M = m_piece(d, m).rearrange("p (h t) -> p h t", h=H)
                            if l == 0 and m % 2 == 0:
                                ada_point(2 * ADA_GDN + 8 * d + m // 2, 2 * ADA_GDN)
                        for ci in range(3 * (m % 2), 3 * (m % 2) + 3):
                            cc, mc = slice(128 * ci, 128 * ci + 128), slice(128 * (ci % 3), 128 * (ci % 3) + 128)
                            if bank >= 6:
                                pe.wait_ge(lv_evac, lvb + bank - 5)
                            for h in range(H):
                                o = ps[:, bank % 6, 128 * h:128 * h + 128]
                                if m < 0:
                                    last = mm(o, HK[d][:, h, cc], HQ[:, h, cc], start=True, stop=True)
                                elif m < 14:
                                    last = mm(o, M[:, h, mc], M[:, h, mc], start=True, stop=True)
                                else:
                                    last = tr(o, M[:, h, mc], ident)
                            last.then_inc(lv_out, 1)
                            bank += 1
                    KE = chunks(3 if d == 0 else 5)
                    pe.wait_ge(lv_evac, lvb + NLV)
                    for n, ci in enumerate(order(d)):
                        U, O = n % 2, 2 + n % 2
                        sbase = (NC - 1) * (2 * l + d)
                        if n < NC - 1:
                            if n >= 2:
                                pe.wait_ge(hs_ready, sbase + n - 1)
                            for h in range(H):
                                last = mm(ps[:, U, 64 * h:64 * h + 64], KE[:, ci, h, :], HV[:, ci, 64 * h:64 * h + 64], start=True, stop=True)
                            last.then_inc(hu_out, 1)
                        if ci in chunks_out(l):
                            k = o_count(l, d, n)
                            if k > o_count(l, d, -1) + 2:
                                pe.wait_ge(ho_evac, k - 2)
                            if n:
                                pe.wait_ge(hs_ready, sbase + n)
                            for h in range(H):
                                p0, c0 = 64 * (h % 2), 128 * (h // 2)
                                o = ps[p0:p0 + 64, O, c0:c0 + 128]
                                if n:
                                    mm(o, S[:, (n - 1) % 2, 64 * h:64 * h + 64], HK[d][:, h, 128 * ci:128 * ci + 128], start=True, stop=False)
                                last = mm(o, HV[:, ci, 64 * h:64 * h + 64], HATT[:, ci, h, :], start=(n == 0), stop=True)
                            last.then_inc(ho_out, 1)
                if l == 0:
                    ada_finish(2 * (ADA_GDN + ADA_HGRN) - 2, 2 * ADA_GDN)
                    pe.wait_ge(ada_read, 2)
                pe.wait_ge(ho_evac, o_count(l, 1, NC - 1))
                for u in range(2):
                    sum_squares(l, "hrms", u, 1, bd64, lo)

                gemm(l, "cq", 0, [0, 1], Hm)
                w = arrived(l, "ckv")[:, 0:KB * 160].rearrange("p (k n) -> p k n", k=KB)
                project(free_pair(l, "ckv"), w, Hm, KB, 0, 128).then_inc(gemm_out, 1)
                project(free_pair(l, "kr"), w, Hm, KB, 64, 96).then_inc(gemm_out, 1)
                sum_squares(l, "cqsum", 0, 2, ones)
                sum_squares(l, "ckvsum", 0, 1, ones)
                dst = free_pair(l, "krrot")
                pe.wait_ge(gemm_evac, number(UNITS, l, "kr") + 1)
                mm(dst[0:96, 512:1024], rotp[0:96, 0:96], KR0[0:96, CTX:TOK], start=True, stop=True).then_inc(gemm_out, 1)
                pe.wait_ge(cn_ready, 3 * l + 3)
                w = arrived(l, "uq")[:, 0:768].rearrange("p (k n) -> p k n", k=2)
                for h in range(H):
                    last = project(free_pair(l, "uq", h), w, CQ, 2, 96 * h, 96)
                    last.then_inc(gemm_out, 1)
                for h in range(H):
                    dst = free_pair(l, "qrot", h)
                    pe.wait_ge(gemm_evac, number(UNITS, l, "uq", h) + 1)
                    mm(dst[0:96, 512:1024], rotp[0:96, 0:96], QH[0:96, h, CTX:TOK], start=True, stop=True).then_inc(gemm_out, 1)
                w = arrived(l, "ukv")[:, 0:512].rearrange("p (k n) -> p k n", k=1)
                for h in range(H):
                    project(free_pair(l, "uk", h), w, CKV.unsqueeze(1), 1, 128 * h, 64).then_inc(gemm_out, 1)
                wv = arrived(l, "ukv")[:, 0:512].rearrange("p (h n) -> p h n", h=H)
                for ci in range(NC):
                    dst = free_pair(l, "vt", ci)
                    mm(dst[:, 512:768].rearrange("p (h n) -> p h n", h=H), CKV[:, 128 * ci:128 * ci + 128], wv[:, :, 64:128],
                       start=True, stop=True).then_inc(gemm_out, 1)
                pe.wait_ge(gemm_evac, number(UNITS, l, "vt", NC - 1) + 1)
                pe.wait_ge(rope_done, 5 * (l + 1))
                pe.wait_ge(kr_copied, l + 1)
                steps = att_steps(l)

                def scores(i):
                    qt, h = steps[i]
                    a = ATT0[l] + i
                    if i >= 2:
                        pe.wait_ge(pe_ready, a - 1)
                    dst = ps[:, 2 * (i % 2):2 * (i % 2) + 2, :].rearrange("p a b -> p (a b)")
                    for s0, s1 in ([(0, CTX)] if qt < NCC else [(0, CTX), (CTX, TOK)]):
                        last = mm(dst[:, CTX + s0:CTX + s1], QH[0:96, h, 128 * qt:128 * qt + 128], KH[0:96, h, s0:s1], start=True, stop=True)
                    last.then_inc(sc_out, 1)

                def output(i):
                    qt, h = steps[i]
                    a, nk, p0 = ATT0[l] + i, (NCC if qt < NCC else NC), 64 * (h % 2)
                    pe.wait_ge(pt_ready, a + 1)
                    if i >= 2:
                        pe.wait_ge(pv_evac, a - 1)
                    for ck in range(nk):
                        last = mm(ps[p0:p0 + 64, 6 + i % 2, 0:128], VT[:, ck, 64 * h:64 * h + 64], PT[i % 2][:, 128 * ck:128 * ck + 128],
                                  start=(ck == 0), stop=(ck == nk - 1))
                    last.then_inc(pv_out, 1)

                scores(0)
                scores(1)
                for i, (qt, h) in enumerate(steps):
                    a, nk = ATT0[l] + i, (NCC if qt < NCC else NC)
                    if i + 2 < len(steps):
                        scores(i + 2)
                    pe.wait_ge(p_ready, a + 1)
                    if i >= 1:
                        pe.wait_ge(pt_ready, a)
                    dst = ps[:, 4:6, :].rearrange("p a b -> p (a b)")
                    for ck in range(nk):
                        last = tr(dst[:, CTX + 128 * ck:CTX + 128 * ck + 128], P_[i % 2][:, 128 * ck:128 * ck + 128], ident)
                    last.then_inc(pt_out, 1)
                    if i >= 1:
                        output(i - 1)
                output(len(steps) - 1)
                pe.wait_ge(pv_evac, ATT0[l + 1])
                pe.wait_ge(y_ready, 6 * (l + 1))
                for i in range(4):
                    gemm(l, "out", i, [2 * i, 2 * i + 1], Y, lo)
                sum_squares(l, "norm1", 0, KB, ones, lo)
                sum_squares(l, "norm2", 0, KB, ones, lo)
                for i in range(16):
                    gemm(l, "mlp1", i, [2 * i, 2 * i + 1], Hm, lo, h_before=8 * (2 * l + 1) if i == 0 else None)
                pe.wait_ge(gemm_evac, number(UNITS, l, "mlp1", FB - 1) + 1)
                hid = R[:, :, :].rearrange("p a b -> p (a b)").rearrange("p (k t) -> p k t", t=TOK)
                pe.wait_ge(hid_ready, FB * (l + 1))
                for g in range(4):
                    dsts = [free_pair(l, "mlp2", 2 * g + j) for j in range(2)]
                    for kg in range(4):
                        w = arrived(l, "mlp2", 4 * g + kg).rearrange("p (k n) -> p k n", k=KB)
                        for j in range(2):
                            last = project(dsts[j], w, hid[:, 8 * kg:8 * kg + 8, :], KB, 128 * j, 128, lo, kg == 0, kg == 3)
                            if kg == 3:
                                last.then_inc(gemm_out, 1)
                        if kg < 3:
                            last.then_inc(w_used, 1)
                sum_squares(l, "norm3", 0, KB, ones, lo)
            pe.wait_ge(x_ready, 16 * DEPTH)
            for i in range(2 * SEQ // 128):
                if i >= 4:
                    pe.wait_ge(out_evac, i - 3)
                t0 = CTX + 128 * (i // 2)
                for j in range(4):
                    last = tr(ps[:, i % 4, 128 * j:128 * j + 128], X[:, 4 * (i % 2) + j, t0:t0 + 128], ident)
                last.then_inc(out_tr, 1)

        @block.scalar
        def _(act):
            af = nc.scalar.activation
            count = [0]

            def link(ins):
                count[0] += 1
                ins.then_inc(act_step, 1)
                act.wait_ge(act_step, count[0])

            def finished(l, what, i=0):
                act.wait_ge(gemm_out, out_number(l, what, i))
                return pair(number(UNITS, l, what, i))

            def copied(l, what, i, ins):
                ins.then_inc(gemm_evac, 1)
                assert next_unit[0] == number(UNITS, l, what, i), (what, i)
                next_unit[0] += 1
            next_unit = [0]

            def square(l, what, i, src, lo=0):
                n = number(SQUARES, l, what, i)
                if what[:4] != "norm":
                    act.wait_ge(sq_used, n - 3)
                af(square_buffer(what, i, n)[:, lo:], src, ACT.Square).then_inc(sq_ready, 1)

            def roots_used(n):
                l, k = divmod(n, len(ROOTS))
                what, i = ROOTS[k]
                if what in ("norm0", "norm2"):
                    return xn_ready, 8 * (2 * l + (1 if what == "norm0" else 2))
                if what in ("norm1", "norm3"):
                    return x_ready, 16 * l + (8 if what == "norm1" else 16)
                if what == "l2":
                    return l2_done, 8 * l + i + 1
                if what in ("grms", "hrms"):
                    return y_ready, 6 * l + i + 1 + (4 if what == "hrms" else 0)
                return cn_ready, 3 * l + (2 if what == "cqsum" else 3)

            def inverse_root(l, what, i, width, n, lo=0, bias=None):
                first = number(SQUARES, l, what, i)
                act.wait_ge(sq_used, first + n)
                r, u = number(ROOTS, l, what, i), number(UNITS, l, what, i)
                if r >= 2:
                    act.wait_ge(*roots_used(r - 2))
                o = lnb[r % 2][:, lo:]
                copied(l, what, i, af(o, tokens(pair(u), lo), ACT.Ln, bias=eps_col, scale=1.0 / width))
                act.wait_ge(gemm_evac, u + 1)
                af(o, o, ACT.Exp, bias=zero_col if bias is None else bias, scale=-0.5).then_inc(rs_ready, 1)

            def take_and_square(l, what, norm, lo):
                for b in range(KB + 1):
                    if b < KB:
                        copied(l, what, b, af(Hm[:, b, lo:], tokens(finished(l, what, b), lo), ACT.Copy))
                    if b:
                        act.wait_ge(gemm_evac, number(UNITS, l, what, b - 1) + 1)
                        square(l, norm, b - 1, Hm[:, b - 1, lo:], lo)

            def modulate(l, w, A, B):
                for b in range(KB):
                    act.wait_ge(xn_ready, 8 * (2 * l + w) + b + 1)
                    for a, e, s in segments(0 if w == 0 else lo_of(l)):
                        last = af(Hm[:, b, a:e], Hm[:, b, a:e], ACT.Identity, bias=B[:, b, s:s + 1], scale=A[:, b, s:s + 1])
                    last.then_inc(h_ready, 1)

            act.wait_ge(rows_clear, 1)
            load_rows(act, 0, rows_in)
            for i in range(2 * NC):
                act.wait_ge(xT_ready, i + 1)
                af(X[:, 4 * (i % 2):4 * (i % 2) + 4, 128 * (i // 2):128 * (i // 2) + 128],
                   ps[:, i % 4, :].rearrange("p (b t) -> p b t", b=4), ACT.Copy).then_inc(xT_evac, 1)
            act.wait_ge(consts_ready, 1)
            act.wait_ge(lb_v, 1)
            af(lbt[:, 0:2, :], lbt[:, 0:2, :], ACT.Exp, bias=zero_col).then_inc(lb_a, 1)
            act.wait_ge(vecs_ready, 1)
            af(cs[:, :, :].rearrange("p k s -> p s k"), vecs[:, 1, V_C:V_C + 16].rearrange("p (s k) -> p s k", s=2),
               ACT.Silu, bias=zero_col).then_inc(cs_ready, 1)
            def ada_rows(g, row, q, bank):
                act.wait_ge(ada_out, g + 1)
                af(row[q:q + 2, 0:512], ps[q:q + 2, bank, :], ACT.Copy).then_inc(ada_row, 1)

            def ada_point(p, first):
                if p % 2 == 0 and p > first:
                    g = ADA_FIRST + p // 2 - 1
                    ada_rows(g, ring[:, LOADS.index((0, "ada", p - 1)) % NSLOT, :], 32 * (g % 2), 6)
            for g in range(ADA_FIRST):
                ada_rows(g, ada_first[:, 2 * g + 1, :], 0, g)
            act.wait_ge(xT_evac, 2 * NC)

            for l in range(DEPTH):
                lo = lo_of(l)
                for b in range(KB):
                    if l:
                        act.wait_ge(x_ready, 16 * l - 8 + b + 1)
                    square(l, "norm0", b, X[:, b, :])
                inverse_root(l, "norm0", 0, D, KB)
                modulate(l, 0, A1, mods[:, l, 0:8, :])
                copied(l, "ba", 0, af(ba[:, :, :], finished(l, "ba")[:, 512:608].rearrange("p (c n) -> p c n", c=NC), ACT.Copy))
                act.wait_ge(la_v, l + 1)
                act.wait_ge(vec_in, 32 * (l + 1))
                af(gd[:, 0, :].rearrange("p (c n) -> p c n", c=NC), ba[:, :, 0:8], ACT.Exp, bias=zero_col, scale=-1.0)
                link(af(gd[:, 6, :], gd[:, 9, :], ACT.Abs, bias=zero_col))
                link(af(gd[:, 6, :], gd[:, 6, :], ACT.Exp, bias=zero_col, scale=-1.0))
                link(af(gd[:, 6, :], gd[:, 6, :], ACT.Ln, bias=one_col))
                af(alog[:, :], alog[:, :], ACT.Exp, bias=zero_col).then_inc(la_a, 1)
                act.wait_ge(pads_ready, l + 1)

                def silu(u):
                    act.wait_ge(conv_done, 12 * l + u + 1)
                    dst = (qT, kT, vT)[u // 4][:, u % 4, :]
                    af(dst[:, 0:CTX], cacc[u % 2][:, 0:CTX], ACT.Silu, bias=zero_col)
                    af(dst[:, CTX:TOK], cacc[u % 2][:, CTX + 2:TOK + 2], ACT.Silu, bias=zero_col).then_inc(silu_done, 1)
                for u in range(12):
                    z = finished(l, "qkv", u)
                    if u >= 2:
                        act.wait_ge(conv_done, 12 * l + u - 1)
                    af(zpad[u % 2][:, 2:2 + CTX], z[:, CTX:2 * CTX], ACT.Copy)
                    copied(l, "qkv", u, af(zpad[u % 2][:, CTX + 4:TOK + 4], z[:, 2 * CTX:CTX + TOK], ACT.Copy))
                    if u:
                        silu(u - 1)
                silu(11)
                copied(l, "gcum", 0, af(S[:, 0, 0:144], finished(l, "gcum")[:, 512:656], ACT.Copy))
                act.wait_ge(gs_v, l + 1)
                af(gd[:, 4, :], gd[:, 2, :], ACT.Exp, bias=zero_col)
                af(gd[:, 5, :], gd[:, 3, :], ACT.Exp, bias=zero_col)
                af(gd[:, 6, :], gd[:, 6, :], ACT.Exp, bias=zero_col).then_inc(gs_a, 1)
                act.wait_ge(silu_done, 12 * (l + 1))
                qk = [(qT, kT)[u // 4][:, u % 4, :] for u in range(8)]
                for u in range(4):
                    square(l, "l2", u, qk[u])
                for u in range(8):
                    inverse_root(l, "l2", u, 1, 1, bias=lnq_col if u < 4 else None)
                    if u < 4:
                        square(l, "l2", u + 4, qk[u + 4])
                for what, dst in (("ktr", ktok), ("vtr", vtok)):
                    for ci in range(NC):
                        src = finished(l, what, ci)[:, 512:1024].rearrange("p (h d) -> p h d", h=H)
                        copied(l, what, ci, af(dst[:, ci], src, ACT.Copy))
                for d in range(2):
                    base = NC * (2 * l + d)
                    for ci in range(NC):
                        if l == 0:
                            ada_point(2 * NC * d + ci, 0)
                        act.wait_ge(p1_exp_in, base + ci + 1)
                        for h in range(H):
                            af(T_[:, ci % 2, h, :], T_[:, ci % 2, h, :], ACT.Exp, bias=g_[:, ci, d, h:h + 1])
                        for h in range(H):
                            last = af(TT[:, ci % 2, h, :], TT[:, ci % 2, h, :], ACT.Exp, bias=ng[:, ci, d, h:h + 1])
                        last.then_inc(p1_exp, 1)
                    bb, cb = 7 * NC * (2 * l + d), 6 * NC * (2 * l + d)
                    for j in range(6 * NC):
                        act.wait_ge(c_out, cb + j + 1)
                        if j >= 2:
                            act.wait_ge(b_out, bb + NC + j - 1)
                        af(Csb[j % 2], ps[:, j % 2, :].rearrange("p (h d) -> p h d", h=H), ACT.Copy).then_inc(c_evac, 1)
                    for ci in range(NC):
                        act.wait_ge(w_out_s, base + ci + 1)
                        G, W = 2 * (ci % 2), 2 * (ci % 2) + 1
                        af(T_[:, ci], ps[:, G, :].rearrange("p (h d) -> p h d", h=H), ACT.Exp, bias=zero_col).then_inc(eg_exp, 1)
                        af(N_[:, ci], ps[:, W, :].rearrange("p (h d) -> p h d", h=H), ACT.Copy, scale=-1.0).then_inc(wt_ready, 1)
                    for n in range(NC):
                        if l == 0:
                            ada_point(2 * NC * d + NC + n, 0)
                        act.wait_ge(v_out, base + n + 1)
                        af(VN[n % 2], ps[:, n % 2, :].rearrange("p (h d) -> p h d", h=H), ACT.Copy).then_inc(vn_ready, 1)
                if l == 0:
                    ada_point(2 * ADA_GDN, 0)
                for u in range(4):
                    copied(l, "gate", u, af(GT[:, u, lo:], tokens(finished(l, "gate", u), lo), ACT.Silu, bias=zero_col))
                act.wait_ge(o_evac, o_count(l, 1, NC - 1))
                for u in range(4):
                    square(l, "grms", u, Y[:, u, lo:], lo)
                for u in range(4):
                    inverse_root(l, "grms", u, 128, 1, lo)
                for u in range(4):
                    copied(l, "hq", u, af(HQ[:, u, :], tokens(finished(l, "hq", u)), ACT.Copy, scale=128 ** -0.5))
                for u in range(4):
                    copied(l, "hf", u, af(HK[0][:, u, :], tokens(finished(l, "hf", u)), ACT.Copy))
                act.wait_ge(gemm_evac, number(UNITS, l, "hf", 3) + 1)
                af(HB[0], HK[0], ACT.Exp, bias=zero_col, scale=-1.0).then_inc(f_exp, 1)
                for u in range(4, 8):
                    copied(l, "hf", u, af(HK[1][:, u - 4, :], tokens(finished(l, "hf", u)), ACT.Copy))
                act.wait_ge(k_done, 2 * l + 1)
                af(HB[0], HB[0], ACT.Ln, bias=tiny_col).then_inc(lf_done, 1)
                act.wait_ge(gemm_evac, number(UNITS, l, "hf", 7) + 1)
                act.wait_ge(y_ready, 6 * l + 4)
                af(HB[1], HK[1], ACT.Exp, bias=zero_col, scale=-1.0).then_inc(f_exp, 1)
                for ci in range(NC):
                    copied(l, "hi", ci, af(HV[:, ci, :], finished(l, "hi", ci)[:, 512:768], ACT.Copy))
                for u in range(2):
                    copied(l, "hgate", u, af(HGT[:, u, lo:], tokens(finished(l, "hgate", u), lo), ACT.Silu, bias=zero_col))
                act.wait_ge(k_done, 2 * l + 2)
                af(HB[1], HB[1], ACT.Ln, bias=tiny_col).then_inc(lf_done, 1)
                for d in range(2):
                    for m in range(16):
                        act.wait_ge(md_ready, 16 * (2 * l + d) + m + 1)
                        M, wide = m_piece(d, m), level(d, m)[0]
                        if m < 14:
                            v = M.rearrange("p (n e s) -> p n e s", e=2, s=wide // 2)
                            low = -1.0 if d == 0 else 1.0
                            af(v[:, :, 0, :], v[:, :, 0, :], ACT.Exp, bias=zero_col, scale=low)
                            af(v[:, :, 1, :], v[:, :, 1, :], ACT.Exp, bias=zero_col, scale=-low).then_inc(me_ready, 1)
                        else:
                            af(M, M, ACT.Exp, bias=zero_col, scale=-1.0).then_inc(me_ready, 1)
                        if l == 0 and m % 2 == 1:
                            ada_point(2 * ADA_GDN + 8 * d + m // 2, 2 * ADA_GDN)
                    b4 = HB[d].rearrange("p h (c t) -> p h c t", t=128)
                    link(af(ebl[:, :, :], b4[:, :, :, 127 if d == 0 else 0], ACT.Exp, bias=zero_col))
                    af(HB[d], HB[d], ACT.Exp, bias=zero_col).then_inc(eb_ready, 1)
                if l == 0:
                    ada_point(2 * (ADA_GDN + ADA_HGRN), 2 * ADA_GDN)
                act.wait_ge(ho_evac, o_count(l, 1, NC - 1))
                for u in range(2):
                    square(l, "hrms", u, Y[:, 6 + u, lo:], lo)
                for u in range(2):
                    inverse_root(l, "hrms", u, 64, 1, lo)
                act.wait_ge(y_ready, 6 * l + 6)
                for u in range(2):
                    copied(l, "cq", u, af(CQ[:, u, :], tokens(finished(l, "cq", u)), ACT.Copy))
                copied(l, "ckv", 0, af(CKV, tokens(finished(l, "ckv")), ACT.Copy))
                copied(l, "kr", 0, af(KR0[0:96], tokens(finished(l, "kr"))[0:96], ACT.Copy))
                act.wait_ge(gemm_evac, number(UNITS, l, "kr") + 1)
                for u in range(2):
                    square(l, "cqsum", u, CQ[:, u, :])
                square(l, "ckvsum", 0, CKV)
                inverse_root(l, "cqsum", 0, 256, 2)
                inverse_root(l, "ckvsum", 0, 128, 1)
                copied(l, "krrot", 0, af(KROT[0:96], finished(l, "krrot")[0:96, 512:1024], ACT.Copy))
                for h in range(H):
                    copied(l, "uq", h, af(QH[0:96, h, :], tokens(finished(l, "uq", h))[0:96], ACT.Copy))
                for h in range(H):
                    copied(l, "qrot", h, af(ROT[0:96, h, 0:SEQ], finished(l, "qrot", h)[0:96, 512:1024], ACT.Copy))
                for h in range(H):
                    copied(l, "uk", h, af(KH[0:64, h, :], tokens(finished(l, "uk", h))[0:64], ACT.Copy))
                for ci in range(NC):
                    copied(l, "vt", ci, af(VT[:, ci, :], finished(l, "vt", ci)[:, 512:768], ACT.Copy))
                steps = att_steps(l)

                def keys_of(i):
                    return CTX if steps[i][0] < NCC else TOK

                def probabilities(i):
                    a = ATT0[l] + i
                    act.wait_ge(mx_ready, a + 1)
                    if i >= 2:
                        act.wait_ge(pt_out, a - 1)
                    s = ps[:, 2 * (i % 2):2 * (i % 2) + 2, :].rearrange("p a b -> p (a b)")
                    af(P_[i % 2][:, 0:keys_of(i)], s[:, CTX:CTX + keys_of(i)], ACT.Exp, bias=sm[:, i % 2:i % 2 + 1], scale=96 ** -0.5,
                       accum_out=sm[:, 2 + i % 2:3 + i % 2]).then_inc(pe_ready, 1)

                def take_output(i):
                    qt, h = steps[i]
                    a, p0 = ATT0[l] + i, 64 * (h % 2)
                    act.wait_ge(pv_out, a + 1)
                    af(Y[p0:p0 + 64, 4 + h // 2, 128 * qt:128 * qt + 128], ps[p0:p0 + 64, 6 + i % 2, 0:128], ACT.Copy).then_inc(pv_evac, 1)

                probabilities(0)
                for i in range(len(steps)):
                    a = ATT0[l] + i
                    if i + 1 < len(steps):
                        probabilities(i + 1)
                    act.wait_ge(pt_out, a + 1)
                    if i >= 2:
                        act.wait_ge(pv_out, a - 1)
                    t = ps[:, 4:6, :].rearrange("p a b -> p (a b)")
                    af(PT[i % 2][:, 0:keys_of(i)], t[:, CTX:CTX + keys_of(i)], ACT.Copy).then_inc(pt_ready, 1)
                    if i:
                        take_output(i - 1)
                take_output(len(steps) - 1)
                take_and_square(l, "out", "norm1", lo)
                inverse_root(l, "norm1", 0, D, KB, lo)
                for b in range(KB):
                    act.wait_ge(x_ready, 16 * l + b + 1)
                    square(l, "norm2", b, X[:, b, lo:], lo)
                inverse_root(l, "norm2", 0, D, KB, lo)
                modulate(l, 1, A2, mods[:, l, 24:32, :])
                hid = R[:, :, :].rearrange("p a b -> p (a b)").rearrange("p (k t) -> p k t", t=TOK)
                for b in range(FB):
                    copied(l, "mlp1", b, af(hid[:, b, lo:], tokens(finished(l, "mlp1", b), lo), ACT.Relu, bias=zero_col))
                take_and_square(l, "mlp2", "norm3", lo)
                inverse_root(l, "norm3", 0, D, KB, lo)

        @block.vector
        def _(dve):
            v = nc.vector
            count = [0]

            def link(ins):
                count[0] += 1
                ins.then_inc(dve_step, 1)
                dve.wait_ge(dve_step, count[0])

            def roots(l, what, i=0):
                r = number(ROOTS, l, what, i)
                dve.wait_ge(rs_ready, r + 1)
                return lnb[r % 2]

            def over_heads(ap):
                return ap.unsqueeze(1).to_broadcast([128, H, 128])

            def norm_input(l, what, lo):
                rs = roots(l, what)
                for b in range(KB):
                    v.tensor_tensor(Hm[:, b, lo:], X[:, b, lo:], rs[:, lo:], ALU.mult).then_inc(xn_ready, 1)

            def add_normed(l, what, lo, G):
                rs = roots(l, what)
                for b in range(KB):
                    link(v.tensor_tensor(Hm[:, b, lo:], Hm[:, b, lo:], rs[:, lo:], ALU.mult))
                    for a, e, s in segments(lo):
                        last = v.scalar_tensor_tensor(X[:, b, a:e], Hm[:, b, a:e], G[:, b, s:s + 1], X[:, b, a:e], ALU.mult, ALU.add)
                    last.then_inc(x_ready, 1)

            v.memset(rows, 0.0).then_inc(rows_clear, 1)
            for i, val in enumerate((EPS, 1.0, -0.5 * float(np.log(128.0)), 1e-19, 0.0)):
                last = v.memset(cst[:, i:i + 1], val)
            last.then_inc(consts_ready, 1)
            dve.wait_ge(mask_in, 16)
            v.tensor_copy(masks[:, :, :], R[:, 1, 0:15 * 128].rearrange("p (a b) -> p a b", b=128))
            dve.wait_ge(vT_ready, 1)
            v.tensor_copy(vecs[:, 0:2, :], ps[:, 5, 0:256].rearrange("p (a b) -> p a b", a=2)).then_inc(vecs_ready, 1)
            dve.wait_ge(vT1_ready, 1)
            v.tensor_copy(vecs[:, 2:4, :], ps[:, 6, 0:256].rearrange("p (a b) -> p a b", a=2)).then_inc(vecs_ready, 1)
            dve.wait_ge(vecs_ready, 2)
            l0, l1 = vecs[:, 1, V_LB:V_LB + 8], vecs[:, 1, V_LB + 8:V_LB + 16]
            link(v.tensor_tensor(lbt[:, 2, :], l0, l1, ALU.max))
            link(v.tensor_tensor(lbt[:, 0, :], l0, lbt[:, 2, :], ALU.subtract))
            v.tensor_tensor(lbt[:, 1, :], l1, lbt[:, 2, :], ALU.subtract).then_inc(lb_v, 1)
            v.memset(lb[:, 0, 0, :], 0.0)
            v.memset(lb[:, 0, 1, :], 1.0)
            dve.wait_ge(lb_a, 1)
            link(v.tensor_tensor(lbt[:, 2, :], lbt[:, 0, :], lbt[:, 1, :], ALU.add))
            link(v.reciprocal(lbt[:, 2, :], lbt[:, 2, :]))
            link(v.tensor_tensor(lb[:, 1, 0, :], lbt[:, 1, :], lbt[:, 2, :], ALU.mult))
            link(v.tensor_tensor(lb[:, 1, 1, :], lbt[:, 0, :], lbt[:, 2, :], ALU.mult))

            def add_bias(l, b0, b1, columns):
                link(v.tensor_tensor(mods[:, l, b0:b1, :], columns.rearrange("p (b s) -> p b s", s=2),
                                     vecs[:, 2 * l, b0:b1].unsqueeze(2).to_broadcast([128, b1 - b0, 2]), ALU.add))

            for l in range(DEPTH):
                lo = lo_of(l)

                def gain(dst, b0, at, plus_one):
                    g = vecs[:, 2 * l, at:at + 8].unsqueeze(2).to_broadcast([128, 8, 2])
                    m = mods[:, l, b0:b0 + 8, :]
                    return (v.scalar_tensor_tensor(dst[:, :, :], m, 1.0, g, ALU.add, ALU.mult) if plus_one
                            else v.tensor_tensor(dst[:, :, :], m, g, ALU.mult))
                if l == 0:
                    dve.wait_ge(ada_tr, ADA_FIRST)
                    add_bias(0, 0, 16, ps[:, 7, 0:32])
                gain(A1, 8, V_MIXPRE, True).then_inc(mods_ready, 1)
                norm_input(l, "norm0", 0)
                dve.wait_ge(gemm_evac, number(UNITS, l, "ba") + 1)
                dve.wait_ge(vec_in, 32 * (l + 1))
                v.tensor_tensor(gd[:, 9, :].rearrange("p (c n) -> p c n", c=NC), ba[:, :, 8:16],
                                dtb[:, :].unsqueeze(1).to_broadcast([128, NC, 8]), ALU.add).then_inc(la_v, 1)
                for i in range(2):
                    v.memset(zpad[i][:, 0:2], 0.0)
                    v.memset(zpad[i][:, CTX + 2:CTX + 4], 0.0)
                    last = v.memset(zpad[i][:, TOK + 4:TOK + 6], 0.0)
                last.then_inc(pads_ready, 1)
                dve.wait_ge(la_a, l + 1)
                link(v.tensor_scalar(gd[:, 0, :], gd[:, 0, :], 1.0, None, ALU.add))
                link(v.reciprocal(gd[:, 0, :], gd[:, 0, :]))
                link(v.scalar_tensor_tensor(gd[:, 6, :], gd[:, 9, :], 0.0, gd[:, 6, :], ALU.max, ALU.add))
                v.scalar_tensor_tensor(gd[:, 1, :].rearrange("p (c n) -> p c n", c=NC), gd[:, 6, :].rearrange("p (c n) -> p c n", c=NC),
                                       -1.0, alog[:, :].unsqueeze(1).to_broadcast([128, NC, 8]), ALU.mult, ALU.mult).then_inc(la_ready, 1)
                for u in range(12):
                    dve.wait_ge(gemm_evac, number(UNITS, l, "qkv", u) + 1)
                    if u >= 2:
                        dve.wait_ge(silu_done, 12 * l + u - 1)
                    for j in range(CONV_W):
                        w = vecs[:, 2 * l + 1, V_CONV + 12 * j + u:V_CONV + 12 * j + u + 1]
                        z = zpad[u % 2][:, j:j + 770]
                        if j == 0:
                            link(v.tensor_scalar(cacc[u % 2], z, w, None, ALU.mult))
                        elif j < CONV_W - 1:
                            link(v.scalar_tensor_tensor(cacc[u % 2], z, w, cacc[u % 2], ALU.mult, ALU.add))
                        else:
                            v.scalar_tensor_tensor(cacc[u % 2], z, w, cacc[u % 2], ALU.mult, ALU.add).then_inc(conv_done, 1)
                dve.wait_ge(gemm_evac, number(UNITS, l, "gcum") + 1)
                raw = S[:, 0, 0:144].rearrange("p (k c d h) -> p k c d h", k=3, c=NC, d=2)
                v.tensor_copy(g_[:, :, 0, :], raw[:, 0, :, 0, :])
                v.tensor_copy(g_[:, :, 1, :], raw[:, 1, :, 1, :])
                link(v.tensor_copy(gd[:, 3, :], S[:, 0, 96:144]))
                v.tensor_scalar(gd[:, 8, :], gd[:, 0, :], -1.0, None, ALU.mult)
                v.tensor_scalar(gd[:, 9, :], gd[:, 2, :], -1.0, None, ALU.mult)
                v.tensor_tensor(gd[:, 6, :], gd[:, 3, :], gd[:, 2, :], ALU.subtract).then_inc(gs_v, 1)
                dve.wait_ge(gs_a, l + 1)
                v.tensor_tensor(gd[:, 7, :], gd[:, 0, :], gd[:, 4, :], ALU.mult).then_inc(gs_ready, 1)
                for u in range(8):
                    rs = roots(l, "l2", u)
                    t = (qT, kT)[u // 4][:, u % 4, :]
                    v.tensor_tensor(t, t, rs, ALU.mult).then_inc(l2_done, 1)
                for d in range(2):
                    base = NC * (2 * l + d)

                    def exponents(ci):
                        dve.wait_ge(p1_out, base + ci + 1)
                        G = ps[:, 3 * (ci % 2), :].rearrange("p (h d) -> p h d", h=H)
                        v.tensor_tensor(T_[:, ci % 2], over_heads(madd[1 - d]), G, ALU.subtract)
                        v.tensor_tensor(TT[:, ci % 2], G, over_heads(madd[d]), ALU.add).then_inc(p1_exp_in, 1)

                    def matrices(ci):
                        dve.wait_ge(p1_exp, base + ci + 1)
                        KK, QK = 3 * (ci % 2) + 1, 3 * (ci % 2) + 2
                        for h in range(H):
                            v.scalar_tensor_tensor(N_[:, ci, h, :], ps[:, KK, 128 * h:128 * h + 128], nbeta[:, ci, d, h:h + 1],
                                                   T_[:, ci % 2, h, :], ALU.mult, ALU.mult)
                        v.tensor_tensor(att[:, ci], ps[:, QK, :].rearrange("p (h d) -> p h d", h=H), TT[:, ci % 2], ALU.mult).then_inc(p1_done, 1)
                    for ci in range(NC):
                        exponents(ci)
                        if ci:
                            matrices(ci - 1)
                    matrices(NC - 1)
                    dve.wait_ge(p1_done, base + NC)
                    eye = ident.unsqueeze(1).to_broadcast([128, NC * H, 128])
                    v.tensor_copy(R[:, 5, :].rearrange("p (n d) -> p n d", d=128), eye)
                    link(v.tensor_copy(R[:, 6, :].rearrange("p (n d) -> p n d", d=128), eye))
                    bb = 7 * NC * (2 * l + d)
                    for i in range(7 * NC):
                        lv, ci = divmod(i, NC)
                        dve.wait_ge(b_out, bb + i + 1)
                        B, BT = 2 + 2 * (i % 2), 3 + 2 * (i % 2)
                        mT = over_heads(masks[:, lv + (0 if d == 0 else 7), :])
                        mTT = over_heads(masks[:, lv + (7 if d == 0 else 0), :])
                        if lv == 0:
                            v.copy_predicated(T_[:, ci], mT, N_[:, ci])
                        elif lv < 6:
                            v.copy_predicated(T_[:, ci], mT, ps[:, B, :].rearrange("p (h d) -> p h d", h=H))
                        v.copy_predicated(TT[:, ci], mTT, ps[:, BT, :].rearrange("p (h d) -> p h d", h=H)).then_inc(t_ready, 1)
                    for n, ci in enumerate(order(d)):
                        if n < NC - 1:
                            k = (NC - 1) * (2 * l + d) + n
                            dve.wait_ge(u_out, k + 1)
                            U = ps[:, 2 + n % 2, :].rearrange("p (h d) -> p h d", h=H)
                            if n == 0:
                                v.tensor_copy(s_of(0), U).then_inc(s_ready, 1)
                            else:
                                dve.wait_ge(s_ready, k)
                                for h in range(H):
                                    last = v.scalar_tensor_tensor(s_of(n)[:, h, :], s_of(n - 1)[:, h, :], egl[:, ci, d, h:h + 1], U[:, h, :], ALU.mult, ALU.add)
                                last.then_inc(s_ready, 1)
                        if ci in chunks_out(l):
                            dve.wait_ge(o_out, o_count(l, d, n))
                            O = ps[:, 4 + n % 2, :].rearrange("p (h d) -> p h d", h=H)
                            y = Y[:, 0:4, 128 * ci:128 * ci + 128]
                            if d == 0:
                                v.tensor_copy(y, O).then_inc(o_evac, 1)
                            else:
                                v.tensor_tensor(y, y, O, ALU.add).then_inc(o_evac, 1)

                def gated(what, u, y, gain, gate):
                    rs = roots(l, what, u)
                    link(v.tensor_tensor(y, y, rs[:, lo:], ALU.mult))
                    v.scalar_tensor_tensor(y, y, gain, gate, ALU.mult, ALU.mult).then_inc(y_ready, 1)
                if l == 0:
                    dve.wait_ge(ada_tr, ADA_FIRST + ADA_GDN)
                    add_bias(0, 16, 48, ps[:, 7, 0:64])
                    add_bias(1, 0, 16, ps[:, 7, 64:96])
                    v.tensor_copy(cst[:, 5:6], mods[:, 1, 15, 0:1]).then_inc(ada_read, 1)
                gain(A2, 32, V_MLPPRE, True)
                gain(G1, 16, V_MIXPOST, False)
                link(gain(G2, 40, V_MLPPOST, False))
                dve.wait_ge(gemm_evac, number(UNITS, l, "gate", 3) + 1)
                for u in range(4):
                    gated("grms", u, Y[:, u, lo:], vecs[:, 2 * l + 1, V_GN:V_GN + 1], GT[:, u, lo:])
                for d in range(2):
                    dve.wait_ge(f_exp, 2 * l + d + 1)
                    link(v.tensor_scalar(HB[d], HB[d], 1.0, None, ALU.add))
                    link(v.reciprocal(HB[d], HB[d]))
                    for h in range(H):
                        q = 4 * d + h
                        last = v.tensor_scalar(HB[d][:, h, :], HB[d][:, h, :], lb[:, l, 1, q:q + 1], lb[:, l, 0, q:q + 1], ALU.mult, ALU.add)
                    link(last)
                    v.tensor_scalar(HK[d], HB[d], -1.0, 1.0, ALU.mult, ALU.add).then_inc(k_done, 1)
                    dve.wait_ge(lf_done, 2 * l + d + 1)
                    for h in range(H):
                        for ci in range(NC):
                            a = HB[d][:, h, 128 * ci:128 * ci + 128]
                            if d == 1:
                                a = a[:, ::-1]
                            last = v.tensor_tensor_scan(a, ones, a, 0.0, ALU.mult, ALU.add)
                    last.then_inc(b_done, 1)

                def queries_keys(d, m):
                    wide = level(d, m)[0]
                    dve.wait_ge(me_ready, 16 * (2 * l + d) + m + 1)
                    kk, qq = part(HK[d], m), part(HQ, m)
                    if m < 14:
                        m5 = m_piece(d, m).rearrange("p (h n e s) -> p h n e s", h=H, e=2, s=wide // 2)
                        k5, q5 = (z.rearrange("p h (n e s) -> p h n e s", e=2, s=wide // 2) for z in (kk, qq))
                        low, high = (k5, q5) if d == 0 else (q5, k5)
                        v.tensor_tensor(m5[:, :, :, 0, :], m5[:, :, :, 0, :], low[:, :, :, 0, :], ALU.mult)
                        v.tensor_tensor(m5[:, :, :, 1, :], m5[:, :, :, 1, :], high[:, :, :, 1, :], ALU.mult).then_inc(m_ready, 1)
                    else:
                        M = m_piece(d, m).rearrange("p (h t) -> p h t", h=H)
                        v.tensor_tensor(M, M, kk, ALU.mult).then_inc(m_ready, 1)

                queries_keys(0, 0)
                queries_keys(0, 1)
                for d in range(2):
                    lvb = NLV * (2 * l + d)
                    bank = 0
                    KE = chunks(3 if d == 0 else 5)
                    for m in range(-2, 16):
                        if 0 <= m < 14:
                            queries_keys(d, m + 2)
                        if m == 14:
                            dve.wait_ge(eb_ready, 2 * l + d + 1)
                            dve.wait_ge(m_ready, 16 * (2 * l + d) + 16)
                            v.tensor_tensor(HK[d], HQ, HB[d], ALU.mult).then_inc(hqd_ready, 1)
                            dve.wait_ge(hqd_ready, 2 * l + d + 1)
                        for ci in range(3 * (m % 2), 3 * (m % 2) + 3):
                            dve.wait_ge(lv_out, lvb + bank + 1)
                            o = ps[:, bank % 6, :].rearrange("p (h d) -> p h d", h=H)
                            if m < 0:
                                v.tensor_tensor(HATT[:, ci], o, over_heads(ident), ALU.mult).then_inc(lv_evac, 1)
                            elif m < 14:
                                dve.wait_ge(lv_evac, lvb + bank - NC + 1)
                                mask = over_heads(masks[:, m // 2 + (7 if d == 0 else 0), :])
                                v.copy_predicated(HATT[:, ci], mask, o).then_inc(lv_evac, 1)
                            else:
                                v.tensor_copy(KE[:, ci], o).then_inc(lv_evac, 1)
                            bank += 1
                    if d == 0:
                        queries_keys(1, 0)
                        queries_keys(1, 1)
                    for n, ci in enumerate(order(d)):
                        if n < NC - 1:
                            k = (NC - 1) * (2 * l + d) + n
                            dve.wait_ge(hu_out, k + 1)
                            U = ps[:, n % 2, 0:256]
                            if n == 0:
                                v.tensor_copy(S[:, 0, 0:256], U).then_inc(hs_ready, 1)
                            else:
                                dve.wait_ge(hs_ready, k)
                                if n >= 2 and o_count(l, d, n - 1) > o_count(l, d, -1):
                                    dve.wait_ge(ho_out, o_count(l, d, n - 1))
                                for h in range(H):
                                    e = slice(64 * h, 64 * h + 64)
                                    last = v.scalar_tensor_tensor(S[:, n % 2, e], S[:, (n - 1) % 2, e], ebl[:, h, ci:ci + 1], U[:, e], ALU.mult, ALU.add)
                                last.then_inc(hs_ready, 1)
                        if ci in chunks_out(l):
                            dve.wait_ge(ho_out, o_count(l, d, n))
                            O = ps[:, 2 + n % 2, 0:256].rearrange("p (b t) -> p b t", b=2)
                            y = Y[:, 6:8, 128 * ci:128 * ci + 128]
                            if d == 0:
                                v.tensor_copy(y, O).then_inc(ho_evac, 1)
                            else:
                                v.tensor_tensor(y, y, O, ALU.add).then_inc(ho_evac, 1)
                if l == 0:
                    dve.wait_ge(ada_tr, GROUPS)
                    add_bias(1, 16, 48, ps[:, 7, 0:64])
                    v.tensor_copy(cst[:, 5:6], mods[:, 1, 47, 0:1]).then_inc(ada_read, 1)
                for u in range(2):
                    gated("hrms", u, Y[:, 6 + u, lo:], vecs[:, 2 * l + 1, V_HN:V_HN + 1], HGT[:, u, lo:])
                rs = roots(l, "cqsum")
                for u in range(2):
                    v.scalar_tensor_tensor(CQ[:, u, :], CQ[:, u, :], vecs[:, 2 * l + 1, V_QN + u:V_QN + u + 1], rs, ALU.mult, ALU.mult).then_inc(cn_ready, 1)
                rs = roots(l, "ckvsum")
                v.scalar_tensor_tensor(CKV, CKV, vecs[:, 2 * l + 1, V_KVN:V_KVN + 1], rs, ALU.mult, ALU.mult).then_inc(cn_ready, 1)
                dve.wait_ge(rope_in, 16 * (l + 1))
                cos, sin = COS[64:96], SIN[64:96]

                def rotate(dst, src, rot):
                    link(v.tensor_tensor(rot, rot, sin, ALU.mult))
                    link(v.tensor_tensor(dst, src, cos, ALU.mult))
                    v.tensor_tensor(dst, dst, rot, ALU.add).then_inc(rope_done, 1)
                dve.wait_ge(gemm_evac, number(UNITS, l, "krrot") + 1)
                v.tensor_copy(KR[64:96, 0:CTX], KR0[64:96, 0:CTX])
                rotate(KR[64:96, CTX:TOK], KR0[64:96, CTX:TOK], KROT[64:96])
                for h in range(H):
                    dve.wait_ge(gemm_evac, number(UNITS, l, "qrot", h) + 1)
                    q = QH[64:96, h, CTX:TOK]
                    rotate(q, q, ROT[64:96, h, 0:SEQ])
                steps = att_steps(l)

                def maximum(i):
                    a = ATT0[l] + i
                    nk = CTX if steps[i][0] < NCC else TOK
                    dve.wait_ge(sc_out, a + 1)
                    s = ps[:, 2 * (i % 2):2 * (i % 2) + 2, :].rearrange("p a b -> p (a b)")
                    link(v.reduce_max(sm[:, 4 + i % 2:5 + i % 2], s[:, CTX:CTX + nk], axis=AX.X))
                    v.tensor_scalar(sm[:, i % 2:i % 2 + 1], sm[:, 4 + i % 2:5 + i % 2], -(96 ** -0.5), None, ALU.mult).then_inc(mx_ready, 1)
                maximum(0)
                for i in range(len(steps)):
                    a = ATT0[l] + i
                    nk = CTX if steps[i][0] < NCC else TOK
                    if i + 1 < len(steps):
                        maximum(i + 1)
                    dve.wait_ge(pe_ready, a + 1)
                    link(v.reciprocal(sm[:, 6 + i % 2:7 + i % 2], sm[:, 2 + i % 2:3 + i % 2]))
                    p = P_[i % 2][:, 0:nk]
                    v.tensor_scalar(p, p, sm[:, 6 + i % 2:7 + i % 2], None, ALU.mult).then_inc(p_ready, 1)
                add_normed(l, "norm1", lo, G1)
                dve.wait_ge(x_ready, 16 * l + 8)
                norm_input(l, "norm2", lo)
                hid = R[:, :, :].rearrange("p a b -> p (a b)").rearrange("p (k t) -> p k t", t=TOK)
                for b in range(FB):
                    dve.wait_ge(gemm_evac, number(UNITS, l, "mlp1", b) + 1)
                    v.tensor_tensor(hid[:, b, lo:], hid[:, b, lo:], hid[:, b, lo:], ALU.mult).then_inc(hid_ready, 1)
                add_normed(l, "norm3", lo, G2)
                dve.wait_ge(x_ready, 16 * l + 16)
            ot = R[:, 0:2, :].rearrange("p a b -> p (a b)")
            for i in range(2 * SEQ // 128):
                dve.wait_ge(out_tr, i + 1)
                v.tensor_copy(ot[:, 512 * i:512 * i + 512], ps[:, i % 4, :]).then_inc(out_evac, 1)


def constants():
    p, f = np.arange(128)[:, None], np.arange(128)[None, :]
    tri_f, tri_b = (p <= f).astype(np.float32), (p >= f).astype(np.float32)
    rot = np.zeros((128, 128), np.float32)
    for i in range(16):
        rot[64 + 16 + i, 64 + i] = -1.0
        rot[64 + i, 64 + 16 + i] = 1.0
    k_f32 = np.stack([np.eye(128), np.ones((128, 128)), (p // 64 == f // 64), rot, tri_f, tri_b,
                      NEG * (tri_f - 1), NEG * (tri_b - 1)], axis=1).astype(np.float32).reshape(128, -1)
    low = [((p // (2 * s) == f // (2 * s)) & ((p // s) % 2 == 1) & ((f // s) % 2 == 0)) for s in LEVELS]
    k_mask = np.stack(low + [m.T for m in low] + [p == f], axis=1).astype(np.float32).reshape(128, -1)
    inv = 10000.0 ** (-np.arange(0, 16, 2, dtype=np.float32) / np.float32(16))
    t = np.arange(SEQ)
    ang = np.concatenate([(t // 64)[:, None] * inv, (t % 64)[:, None] * inv], axis=1).astype(np.float32).T
    k_rope = np.concatenate([np.tile(np.cos(ang), (2, 1)), np.tile(np.sin(ang), (2, 1))], axis=1).astype(np.float32)
    return {"k_f32": k_f32, "k_mask": k_mask, "k_rope": k_rope}


_INS = ["x", "ctx", "c", "c_ctx", "w_ada", "b_ada", "norm_mix_pre", "norm_mix_post", "norm_mlp_pre", "norm_mlp_post",
        "w_in", "w_out", "gdn_conv", "gdn_a_log", "gdn_dt_bias", "gdn_norm", "mla_q_norm", "mla_kv_norm",
        "mla_w_uq", "mla_w_ukv", "hgrn_lb_logits", "hgrn_norm", "w_mlp1", "w_mlp2"]


def kernel(**inputs):
    import concourse.bacc as bacc
    from concourse.bass_utils import run_bass_kernel_spmd

    nc = bacc.Bacc("TRN2", target_bir_lowering=False, num_devices=1)
    arrays, args = {}, []
    for name, a in [(n, inputs[n]) for n in _INS] + list(constants().items()):
        a = np.ascontiguousarray(a)
        arrays[f"in_{name}"] = a
        args.append(nc.dram_tensor(f"in_{name}", a.shape, mybir.dt.from_np(a.dtype), kind="ExternalInput").ap())
    args.append(nc.dram_tensor("out_0", (1, SEQ, D), mybir.dt.float32, kind="ExternalOutput").ap())
    trunk_program(nc, *args)
    r = run_bass_kernel_spmd(nc, [arrays], core_ids=[0])
    return r.results[0]["out_0"]
```

```python
import numpy as np
import concourse.bass as bass
from concourse import mybir
from contextlib import ExitStack

D, SEQ, CTX, DEPTH = 1024, 512, 256, 2
TOK = CTX + SEQ
KB = D // 128
FF = 4 * D
FB = FF // 128
CONV_W = 5
NC = TOK // 128
NCC = CTX // 128
H = 4
EPS = 1e-6
NEG = 1.0e30
C_BA, C_CQ, C_CKV, C_HQ = 2048, 2064, 2320, 2480
C_HF, C_HI, C_HG, D_IN = 2992, 4016, 4272, 4528
LEVELS = [1, 2, 4, 8, 16, 32, 64]
V_BADA, V_MIXPRE, V_MIXPOST, V_MLPPRE, V_MLPPOST = 0, 48, 56, 64, 72
V_CONV, V_QN, V_KVN, V_GN, V_HN, V_LB, V_C = 0, 60, 62, 63, 64, 65, 81

GROUPS = DEPTH * 12
ADA_FIRST = 4
ADA_GDN, ADA_HGRN = 12, 8
LOADS = []
for _l in range(DEPTH):
    LOADS += [(_l, "qkv", _i) for _i in range(4)] + [(_l, "ba", 0), (_l, "qkv", 4), (_l, "qkv", 5)]
    LOADS += [(_l, "ada", _i) for _i in range(2 * ADA_GDN)] if _l == 0 else []
    LOADS += [(_l, "gate", _i) for _i in range(2)] + [(_l, "hq", _i) for _i in range(2)] + [(_l, "hf", _i) for _i in range(4)]
    LOADS += [(_l, "hi", 0), (_l, "hgate", 0)]
    LOADS += [(_l, "ada", 2 * ADA_GDN + _i) for _i in range(2 * ADA_HGRN)] if _l == 0 else []
    LOADS += [(_l, "cq", 0), (_l, "ckv", 0), (_l, "uq", 0), (_l, "ukv", 0)] + [(_l, "out", _i) for _i in range(4)]
    for _q in range(4):
        LOADS += [(_l, "mlp1", 4 * _q + _i) for _i in range(4)] + [(_l, "mlp2", 4 * _q + _i) for _i in range(4)]
NSLOT = 3
UNITS = ([("norm0", 0)] + [("qkv", i) for i in range(8)] + [("ba", 0), ("qkv", 8), ("qkv", 9), ("gcum", 0)]
         + [("l2", i) for i in range(4)] + [("qkv", 10), ("qkv", 11)] + [("l2", i) for i in range(4, 8)] + [("ktr", i) for i in range(NC)] + [("vtr", i) for i in range(NC)]
         + [("gate", i) for i in range(4)] + [("grms", i) for i in range(4)]
         + [("hq", i) for i in range(4)] + [("hf", i) for i in range(8)] + [("hi", i) for i in range(NC)]
         + [("hgate", i) for i in range(2)] + [("hrms", i) for i in range(2)]
         + [("cq", i) for i in range(2)] + [("ckv", 0), ("kr", 0), ("cqsum", 0), ("ckvsum", 0), ("krrot", 0)]
         + [("uq", i) for i in range(4)] + [("qrot", i) for i in range(4)] + [("uk", i) for i in range(4)]
         + [("vt", i) for i in range(NC)] + [("out", i) for i in range(KB)] + [("norm1", 0), ("norm2", 0)]
         + [(w, 8 * q + i) for q in range(4) for w in ("mlp1", "mlp2") for i in range(8)] + [("norm3", 0)])
SQUARES = ([("norm0", i) for i in range(8)] + [("l2", i) for i in range(8)] + [("grms", i) for i in range(4)]
           + [("hrms", i) for i in range(2)] + [("cqsum", i) for i in range(2)] + [("ckvsum", 0)]
           + [(f"norm{n}", i) for n in (1, 2, 3) for i in range(8)])


def number(table, layer, what, i=0):
    return layer * len(table) + table.index((what, i))


SUMS = ("norm0", "l2", "grms", "hrms", "cqsum", "ckvsum", "norm1", "norm2", "norm3")
ROOTS = [u for u in UNITS if u[0] in SUMS]
NOT_SUMS = [u for u in UNITS if u[0] not in SUMS]


def out_number(layer, what, i=0):
    return number(NOT_SUMS, layer, what, i) + 1


def trunk_program(nc, x, ctx, c, c_ctx, w_ada, b_ada, norm_mix_pre, norm_mix_post, norm_mlp_pre, norm_mlp_post,
                  w_in, w_out, gdn_conv, gdn_a_log, gdn_dt_bias, gdn_norm, mla_q_norm, mla_kv_norm,
                  mla_w_uq, mla_w_ukv, hgrn_lb_logits, hgrn_norm, w_mlp1, w_mlp2,
                  k_f32, k_mask, k_rope, out):
    f32, u8 = mybir.dt.float32, mybir.dt.uint8
    ALU, ACT, AX = mybir.AluOpType, mybir.ActivationFunctionType, mybir.AxisListType
    stack = ExitStack()
    with stack:
        def sb(name, shape, dt=f32):
            return stack.enter_context(nc.sbuf_tensor(name, shape, dt))

        def sem(name):
            return stack.enter_context(nc.semaphore(name))

        f32r = mybir.dt.float32r

        def both(name, shape):
            t = sb(name, shape)
            nbytes = 4 * int(np.prod(shape[1:]))
            return t, nc.alloc_sbuf_tensor_at(name + "_r", shape, f32r, offset=nc.sbuf_base - nbytes)
        X = sb("residual", [128, KB, TOK])
        Hm, Hm_r = both("modulated", [128, KB, TOK])
        Y, Y_r = both("mixed", [128, KB, TOK])
        R, R_r = both("region", [128, 8, 4 * TOK])
        ring, ring_r = both("weights", [128, NSLOT, 2048])
        kf = sb("k_f32_sb", [128, 8, 128])
        masks = sb("masks", [128, 15, 128], u8)
        vecs = sb("vecs", [128, 4, 128])
        mods = sb("modulation", [128, DEPTH, 48, 2])
        A1, A2, G1, G2 = (sb(n, [128, KB, 2]) for n in ("pre_gain1", "pre_gain2", "post_gain1", "post_gain2"))
        cs = sb("silu_c", [128, KB, 2])
        S = sb("state", [128, 2, 512])
        ba = sb("ba", [128, NC, 16])
        gd = sb("gdn_small", [128, 10, 48])
        alog, dtb = sb("alog", [128, 8]), sb("dtb", [128, 8])
        cst = sb("cst", [128, 8])
        lb = sb("lower_bound", [128, DEPTH, 2, 8])
        lbt = sb("lb_tmp", [128, 4, 8])
        sm = sb("small", [128, 16])
        ebl = sb("decay_last", [128, H, NC])
        ps = stack.enter_context(nc.psum_tensor("ps", [128, 8, 512], f32))

        ident, ones, bd64, rotp = kf[:, 0, :], kf[:, 1, :], kf[:, 2, :], kf[:, 3, :]
        tri, madd = (kf[:, 4, :], kf[:, 5, :]), (kf[:, 6, :], kf[:, 7, :])
        eps_col, one_col, lnq_col, tiny_col, zero_col = (cst[:, i:i + 1] for i in range(5))

        def pair(n):
            return ps[:, 2 * (n % 4):2 * (n % 4) + 2, :].rearrange("p a b -> p (a b)")

        def tokens(ap, lo=0):
            return ap[:, CTX + lo:CTX + TOK]

        def blocks(area):
            return R[:, area, :].rearrange("p (h t) -> p h t", t=TOK)

        def chunks(area):
            return R[:, area, :].rearrange("p (c h d) -> p c h d", c=NC, h=H)

        qT, kT, ktok, vtok, vT = blocks(0), blocks(1), chunks(2), chunks(3), blocks(5)
        N_, T_, TT, att = chunks(4), chunks(5), chunks(6), chunks(7)
        Yf = Y[:, :, :].rearrange("p a b -> p (a b)")

        def square_buffer(what, i, n):
            if what in ("norm0", "norm3"):
                return Y[:, i, :]
            if what in ("norm1", "norm2"):
                return blocks((2 if what == "norm1" else 0) + i // 4)[:, i % 4, :]
            if what == "l2":
                return Y[:, i % 4, :]
            return R[:, 6, TOK * (n % 4):TOK * (n % 4 + 1)]

        def root_buffer(what, r):
            return Y[:, 4 + r % 2, :] if what == "l2" else R[:, 7, TOK * (r % 2):TOK * (r % 2 + 1)]
        zpad = [R[:, 6, i * 776:i * 776 + 774] for i in range(2)]
        cacc = [R[:, 7, i * 776:i * 776 + 770] for i in range(2)]

        Rb = R[:, :, :].rearrange("p a b -> p (a b)").rearrange("p (k t) -> p k t", t=TOK)
        Rb_r = R_r[:, :, :].rearrange("p a b -> p (a b)").rearrange("p (k t) -> p k t", t=TOK)
        hid_high, hid, hid_low = Rb_r[:, 0:8, :], Rb[:, 8:16, :], Rb_r[:, 8:16, :]
        w_high = [R_r[:, :, :].rearrange("p a b -> p (a b)")[:, 16 * TOK + 2048 * i:16 * TOK + 2048 * (i + 1)] for i in range(2)]
        y_high = [Rb_r[:, b, :] for b in (24, 25, 26, 27, 0, 1, 22, 23)]
        out_w_high = [R_r[:, 7, 0:2048], w_high[1], w_high[0], w_high[1]]
        partial, total = Rb[:, 22:24, :], Rb[:, 24:32, :]

        def piece(i):
            return Yf[:, 4 * TOK + 512 * i:4 * TOK + 512 * (i + 1)].rearrange("p (h d) -> p h d", h=H)
        Csb = vb = [piece(0), piece(1)]
        kbg = kend = [piece(2), piece(3)]
        VN = [piece(4), piece(5)]
        beta, la, g_, gl, eg, egl, kd, bg, nbeta, ng = (gd[:, i, :].rearrange("p (c d h) -> p c d h", c=NC, d=2) for i in range(10))

        def s_of(n):
            return S[:, n % 2, :].rearrange("p (h d) -> p h d", h=H)

        def order(d):
            return list(range(NC)) if d == 0 else list(range(NCC))[::-1] + list(range(NCC, NC))[::-1]

        mask_in = sem("mask_in")
        ada_in = [sem(f"ada_in{i}") for i in range(2 * ADA_FIRST)]
        ada_out, ada_row, ada_tr, ada_read = sem("ada_out"), sem("ada_row"), sem("ada_transposed"), sem("ada_read")
        rows_clear = sem("rows_clear")
        rows1_in, vT1_ready = sem("rows1_in"), sem("vecT1_ready")
        const_in, rows_in, x_in, vec_in, rope_in = sem("const_in"), sem("rows_in"), sem("x_in"), sem("vec_in"), sem("rope_in")
        w_in_s = [sem(f"w_loaded{i}") for i in range(NSLOT)]
        w_used = sem("w_used")
        gemm_out, gemm_evac = sem("gemm_out"), sem("gemm_evac")
        sq_ready, sq_used, rs_ready, rs_used = sem("sq_ready"), sem("sq_used"), sem("rs_ready"), sem("rs_used")
        xT_ready, xT_evac, vT_ready = sem("xT_ready"), sem("xT_evac"), sem("vecT_ready")
        consts_ready, vecs_ready, cs_ready, mods_ready = sem("consts_ready"), sem("vecs_ready"), sem("cs_ready"), sem("mods_ready")
        x_ready, xn_ready, h_ready = sem("x_ready"), sem("xn_ready"), sem("h_ready")
        pads_ready, conv_done, silu_done, l2_done = sem("pads_ready"), sem("conv_done"), sem("silu_done"), sem("l2_done")
        la_a, la_v, la_ready, gs_a, gs_v, gs_ready = (sem(n) for n in ("ba_exps", "ba_sums", "la_ready", "g_split", "g_diff", "g_ready"))
        gmask_ready = sem("gmask_ready")
        p1_out, p1_exp_in, p1_exp, p1_done = (sem(n) for n in ("p1_out", "p1_exponents", "p1_decays", "p1_done"))
        c_out, c_evac, b_out, t_ready = (sem(n) for n in ("c_out", "c_evac", "b_out", "t_ready"))
        kbg_ready, w_out_s, wt_ready, eg_exp, qd_ready = (sem(n) for n in ("kbg_ready", "w_out_s", "wt_ready", "eg_exp", "qd_ready"))
        vb_ready, kend_ready, v_out, vn_ready, u_out, s_ready, o_out, o_evac = (
            sem(n) for n in ("vb_ready", "kend_ready", "v_out", "vn_ready", "u_out", "s_ready", "o_out", "o_evac"))
        f_exp, f_done, k_done, lf_done, b_done = (sem(n) for n in ("f_exp", "f_done", "k_done", "lf_done", "b_done"))
        md_ready, me_ready, m_ready, lv_out, lv_evac, eb_ready, hqd_ready = (
            sem(n) for n in ("md_ready", "me_ready", "m_ready", "lv_out", "lv_evac", "eb_ready", "hqd_ready"))
        hu_out, hs_ready, ho_out, ho_evac, lb_a, lb_v, lb_ready = (
            sem(n) for n in ("hu_out", "hs_ready", "ho_out", "ho_evac", "lb_exps", "lb_diff", "lb_ready"))
        y_ready, cn_ready, rope_done, kr_copied = sem("y_ready"), sem("cn_ready"), sem("rope_done"), sem("kr_copied")
        sc_out, mx_ready, pe_ready, p_ready, pt_out, pt_ready, pv_out, pv_evac = (
            sem(n) for n in ("sc_out", "mx_ready", "p_exp", "p_ready", "pt_out", "pt_ready", "pv_out", "pv_evac"))
        out_ready, out_tr, out_evac, hid_ready = sem("out_ready"), sem("out_tr"), sem("out_evac"), sem("hid_ready")
        out_high_ready, out_low_ready, y_parts_early, y_parts_late = (
            sem(n) for n in ("out_high_ready", "out_low_ready", "y_parts_early", "y_parts_late"))
        w_high_ready, w_low_ready, h_low_ready, sum_ready = (
            sem(n) for n in ("w_high_ready", "w_low_ready", "h_low_ready", "sum_ready"))
        dve_step, act_step, pool_step = sem("dve_step"), sem("act_step"), sem("pool_step")
        block = stack.enter_context(nc.Block())

        def lo_of(l):
            return 0 if l < DEPTH - 1 else CTX

        def chunks_out(l):
            return [ci for ci in range(NC) if ci * 128 >= lo_of(l)]

        def segments(lo):
            return ([(0, CTX, 1)] if lo == 0 else []) + [(CTX, TOK, 0)]

        NU, NSQ = len(UNITS), len(SQUARES)
        def att_steps(l):
            return [(qt, h) for qt in chunks_out(l) for h in range(H)]
        ATT0 = [0, len(att_steps(0)), len(att_steps(0)) + len(att_steps(1))]
        NLV = 9 * NC

        def o_count(l, d, n):
            full = 2 * NC * l
            outs = [ci in chunks_out(l) for ci in order(d)]
            return full + d * len(chunks_out(l)) + sum(outs[:n + 1])

        def mlp_load(j):
            q, r = divmod(j, 8)
            return ("mlp1", 4 * q + r) if r < 4 else ("mlp2", 4 * q + r - 4)

        def slot(l, what, i=0):
            return LOADS.index((l, what, i)) % NSLOT

        def weights_used(n):
            l, what, i = LOADS[n]
            if what == "ada":
                return (w_used, i // 2 + 1) if i % 2 == 0 else (ada_tr, ADA_FIRST + i // 2 + 1)
            last = {"ba": ("ba", 0), "qkv": ("qkv", 2 * i + 1), "gate": ("gate", 2 * i + 1), "hq": ("hq", 2 * i + 1),
                    "hf": ("hf", 2 * i + 1), "hi": ("hi", NC - 1), "hgate": ("hgate", 1), "cq": ("cq", 1), "ckv": ("kr", 0),
                    "uq": ("uq", 3), "ukv": ("vt", NC - 1), "out": ("out", 2 * i + 1), "mlp1": ("mlp1", 2 * i + 1),
                    "mlp2": ("mlp2", 2 * i + 1)}[what]
            return gemm_out, out_number(l, *last)

        GT = blocks(5)
        CQ, CKV = blocks(0)[:, 0:2, :], blocks(0)[:, 2, :]
        KR, ROT = blocks(0)[:, 3, :], blocks(5)
        QH, KH, VT = blocks(1), blocks(2), R[:, 3, 0:NC * 256].rearrange("p (c e) -> p c e", c=NC)
        KR0, KROT = R[:, 3, 2 * TOK:3 * TOK], R[:, 3, 3 * TOK:3 * TOK + SEQ]
        COS, SIN = R[:, 7, 2 * TOK:2 * TOK + SEQ], R[:, 7, 2 * TOK + SEQ:2 * TOK + 2 * SEQ]
        P_ = [R[:, 4, 0:TOK], R[:, 4, TOK:2 * TOK]]
        PT = [R[:, 4, 2 * TOK:3 * TOK], R[:, 4, 3 * TOK:4 * TOK]]
        HQ, HV, HGT = blocks(0), R[:, 1, 0:NC * 256].rearrange("p (c e) -> p c e", c=NC), R[:, 1, 2 * TOK:4 * TOK].rearrange("p (b t) -> p b t", b=2)
        HK, HB = (blocks(2), blocks(4)), (blocks(3), blocks(5))
        HATT = chunks(7)
        MB = [R[:, 6, 0:1536], R[:, 6, 1536:3072], Y[:, 4:6, :].rearrange("p a b -> p (a b)")]

        def m_piece(d, m):
            return MB[(16 * d + m) % 3]

        def level(d, m):
            i = m // 2
            if i == 7:
                return 128, (127 if d == 0 else 0)
            return 2 * LEVELS[i], (LEVELS[i] - 1 if d == 0 else LEVELS[i])

        def part(ap, m):
            return ap[:, :, 384 * (m % 2):384 * (m % 2) + 384]

        def ada_weights(g, half):
            l, g = divmod(g, 12)
            return w_ada[l][512 * half:512 * half + 512, 512 * g:512 * g + 512]
        ada_first = R[:, 2:8, :].rearrange("p a b -> p (a b)")[:, 0:2 * ADA_FIRST * 2048].rearrange("p (i n) -> p i n", n=2048)

        @block.sync
        def _(sp):
            sp.dma_start(kf[:, :, :], k_f32.rearrange("p (a b) -> p a b", b=128)).then_inc(const_in, 16)
            sp.dma_start(R[:, 1, 0:15 * 128], k_mask).then_inc(mask_in, 16)
            xt = Hm[:, :, :].rearrange("p a b -> p (a b)").rearrange("p (c f) -> p c f", c=NC)
            sp.dma_start(xt[:, 0:NCC, :], ctx[0].rearrange("(c p) f -> p c f", p=128)).then_inc(x_in, 16)
            sp.dma_start(xt[:, NCC:NC, :], x[0].rearrange("(c p) f -> p c f", p=128)).then_inc(x_in, 16)
            for i in range(2 * ADA_FIRST):
                sp.dma_start(ada_first[:, i, :].rearrange("p (k n) -> p k n", n=512),
                             ada_weights(i // 2, i % 2).rearrange("(k p) n -> p k n", p=128)).then_inc(ada_in[i], 16)
            for l in range(DEPTH):
                for n, (_, what, i) in [(n, load) for n, load in enumerate(LOADS) if load[0] == l]:
                    if n >= NSLOT:
                        sp.wait_ge(*weights_used(n - NSLOT))
                    wide = 256
                    if what == "ada":
                        src, wide = ada_weights(ADA_FIRST + i // 2, i % 2), 512
                    elif what == "ba":
                        src, wide = w_in[l][:, C_BA:C_CQ], 16
                    elif what == "ckv":
                        src, wide = w_in[l][:, C_CKV:C_HQ], C_HQ - C_CKV
                    elif what in ("qkv", "gate", "hq", "hf", "hi", "hgate", "cq"):
                        c0 = {"qkv": 0, "gate": 1536, "hq": C_HQ, "hf": C_HF, "hi": C_HI, "hgate": C_HG, "cq": C_CQ}[what] + 256 * i
                        src = w_in[l][:, c0:c0 + 256]
                    elif what == "uq":
                        src, wide = mla_w_uq[l], 384
                    elif what == "ukv":
                        src, wide = mla_w_ukv[l], 512
                    elif what == "out":
                        src = w_out[l][:, 256 * i:256 * i + 256]
                    elif what == "mlp1":
                        src = w_mlp1[l][:, 256 * i:256 * i + 256]
                    else:
                        src = w_mlp2[l][1024 * (i // 4):1024 * (i // 4) + 1024, 256 * (i % 4):256 * (i % 4) + 256]
                    ks = src.shape[0] // 128
                    sp.dma_start(ring[:, n % NSLOT, 0:ks * wide].rearrange("p (k n) -> p k n", k=ks),
                                 src.rearrange("(k p) n -> p k n", p=128)).then_inc(w_in_s[n % NSLOT], 16)
            ot = R[:, 0:2, :].rearrange("p a b -> p (a b)")
            for ci in range(SEQ // 128):
                sp.wait_ge(out_evac, 2 * ci + 2)
                sp.dma_start(out[0, 128 * ci:128 * ci + 128, :], ot[:, 1024 * ci:1024 * ci + 1024]).then_inc(out_ready, 16)
            sp.wait_ge(out_ready, 16 * (SEQ // 128))

        rows = R[:, 0, 0:512].rearrange("p (a b) -> p a b", b=128)

        def load_rows(eng, l, arrived_sem):
            for t, at, src in ((0, V_BADA, b_ada[l]), (0, V_MIXPRE, norm_mix_pre[l]), (0, V_MIXPOST, norm_mix_post[l]),
                               (0, V_MLPPRE, norm_mlp_pre[l]), (0, V_MLPPOST, norm_mlp_post[l]),
                               (1, V_QN, mla_q_norm[l]), (1, V_KVN, mla_kv_norm[l]), (1, V_GN, gdn_norm[l]), (1, V_C, c[0]), (1, V_C + 8, c_ctx)):
                n = src.shape[0] // 128
                eng.dma_start(rows[at:at + n, 2 * l + t, :], src.rearrange("(r f) -> r f", f=128)).then_inc(arrived_sem, 16)
            eng.dma_start(rows[V_CONV:V_CONV + 60, 2 * l + 1, :], gdn_conv[l].rearrange("w (r f) -> (w r) f", f=128)).then_inc(arrived_sem, 16)
            eng.dma_start(rows[V_LB:V_LB + 16, 2 * l + 1, :],
                          hgrn_lb_logits.rearrange("l d (r f) -> (l d r) f", f=128)).then_inc(arrived_sem, 16)
            for half in range(2):
                eng.dma_start(rows[V_HN:V_HN + 1, 2 * l + 1, 64 * half:64 * half + 64],
                              hgrn_norm[l].rearrange("(r f) -> r f", r=1)).then_inc(arrived_sem, 16)

        @block.gpsimd
        def _(pool):
            count = [0]

            def link(ins):
                count[0] += 1
                ins.then_inc(pool_step, 1)
                pool.wait_ge(pool_step, count[0])

            pool.wait_ge(rows_clear, 1)
            load_rows(pool, 1, rows1_in)
            for l in range(DEPTH):
                if l:
                    pool.wait_ge(la_ready, l)
                pool.dma_start(alog[:, :], gdn_a_log[l].rearrange("d h -> (d h)").partition_broadcast(128)).then_inc(vec_in, 16)
                pool.dma_start(dtb[:, :], gdn_dt_bias[l].rearrange("d h -> (d h)").partition_broadcast(128)).then_inc(vec_in, 16)
                pool.wait_ge(gs_ready, l + 1)
                for d in range(2):
                    base = NC * (2 * l + d)
                    for ci in range(NC):
                        if ci >= 2:
                            pool.wait_ge(p1_exp_in, base + ci - 1)
                        elif ci == 0 and d == 0:
                            pool.wait_ge(gemm_evac, number(UNITS, l, "vtr", NC - 1) + 1)
                            pool.wait_ge(l2_done, 8 * (l + 1))
                        elif ci == 0:
                            pool.wait_ge(o_out, o_count(l, 0, NC - 1))
                        def mask_and(out, mask, col):
                            return nc.gpsimd.tensor_tensor(out, mask.unsqueeze(1).to_broadcast([128, H, 128]),
                                                           col.unsqueeze(2).to_broadcast([128, H, 128]), ALU.add)
                        mask_and(T_[:, 2 + ci % 2], madd[1 - d], g_[:, ci, d, :])
                        mask_and(TT[:, 2 + ci % 2], madd[d], ng[:, ci, d, :]).then_inc(gmask_ready, 1)
                    for ci in range(NC):
                        if ci == 0:
                            pool.wait_ge(gemm_evac, number(UNITS, l, "vtr", NC - 1) + 1)
                            pool.wait_ge(t_ready, 7 * NC * (2 * l + d) + 7 * NC)
                            if d == 1:
                                pool.wait_ge(u_out, (NC - 1) * (2 * l + 1))
                        if ci >= 2:
                            pool.wait_ge(w_out_s, base + ci - 1)
                        nc.gpsimd.tensor_tensor(kbg[ci % 2], ktok[:, ci], bg[:, ci, d, :].unsqueeze(2).to_broadcast([128, H, 128]),
                                                ALU.mult).then_inc(kbg_ready, 1)
                        pool.wait_ge(eg_exp, base + ci + 1)
                        nc.gpsimd.tensor_tensor(T_[:, ci], T_[:, ci], qT[:, :, 128 * ci:128 * ci + 128], ALU.mult).then_inc(qd_ready, 1)
                    for n, ci in enumerate(order(d)):
                        if n >= 2:
                            pool.wait_ge(v_out, base + n - 1)
                        nc.gpsimd.tensor_tensor(vb[n % 2], vtok[:, ci], beta[:, ci, d, :].unsqueeze(2).to_broadcast([128, H, 128]),
                                                ALU.mult).then_inc(vb_ready, 1)
                        if n < NC - 1:
                            if n < 2:
                                pool.wait_ge(w_out_s, base + NC - 1 + n)
                            else:
                                pool.wait_ge(u_out, (NC - 1) * (2 * l + d) + n - 1)
                            nc.gpsimd.tensor_tensor(kend[n % 2], ktok[:, ci], kd[:, ci, d, :].unsqueeze(2).to_broadcast([128, H, 128]),
                                                    ALU.mult).then_inc(kend_ready, 1)
                pool.wait_ge(sq_used, number(SQUARES, l, "grms", 3) + 1)
                for d in range(2):
                    pool.wait_ge(b_done, 2 * l + d + 1)
                    for m in range(16):
                        d3, m3 = divmod(16 * d + m - 3, 16)
                        if d3 >= 0:
                            pool.wait_ge(lv_out, NLV * (2 * l + d3) + NC + 3 * (m3 + 1))
                        wide, at = level(d, m)
                        b = part(HB[d], m).rearrange("p h (n s) -> p h n s", s=wide)
                        nc.gpsimd.tensor_tensor(m_piece(d, m).rearrange("p (h n s) -> p h n s", h=H, s=wide), b,
                                                b[:, :, :, at:at + 1].to_broadcast([128, H, 384 // wide, wide]), ALU.subtract).then_inc(md_ready, 1)
                pool.wait_ge(ho_evac, o_count(l, 1, NC - 1))
                pool.dma_start(R[64:96, 7, 2 * TOK:2 * TOK + 2 * SEQ], k_rope).then_inc(rope_in, 16)
                pool.wait_ge(rope_done, 5 * l + 1)
                for h in range(H):
                    ins = nc.gpsimd.tensor_copy(KH[64:96, h, :], KR[64:96, :])
                ins.then_inc(kr_copied, 1)
                lo = lo_of(l)
                pool.wait_ge(kr_copied, l + 1)
                pool.wait_ge(rope_done, 5 * (l + 1))
                pool.wait_ge(y_ready, 6 * (l + 1))
                for b in (0, 1, 2, 3, 6, 7):
                    link(nc.gpsimd.tensor_copy(y_high[b][:, lo:], Y[:, b, lo:]))
                    nc.gpsimd.tensor_tensor(Y_r[:, b, lo:], Y[:, b, lo:], y_high[b][:, lo:], ALU.subtract).then_inc(y_parts_early, 1)
                    if b == 0:
                        pool.wait_ge(out_high_ready, 4 * l + 1)
                        at = slot(l, "out", 0)
                        nc.gpsimd.tensor_tensor(ring_r[:, at, :], ring[:, at, :], out_w_high[0], ALU.subtract).then_inc(y_parts_early, 1)

        @block.tensor
        def _(pe):
            mm, tr = nc.tensor.matmul, nc.tensor.transpose

            def arrived(l, what, i=0):
                n = LOADS.index((l, what, i))
                pe.wait_ge(w_in_s[n % NSLOT], 16 * (n // NSLOT + 1))
                return ring[:, n % NSLOT, :]

            def free_pair(l, what, i=0):
                n = number(UNITS, l, what, i)
                if n >= 4:
                    pe.wait_ge(gemm_evac, n - 3)
                return pair(n)

            def streams(lo):
                return ([(0, CTX)] if lo == 0 else []) + [(CTX, TOK)]

            def project(dst, w, rhs, ks, m0, m, lo=0, first=True, final=True, h_before=None):
                for k in range(ks):
                    if h_before is not None:
                        pe.wait_ge(h_ready, h_before + k + 1)
                    for a, b in streams(lo):
                        last = mm(dst[0:m, CTX + a:CTX + b], w[:, k, m0:m0 + m], rhs[:, k, a:b],
                                  start=(first and k == 0), stop=(final and k == ks - 1))
                return last

            def gemm(l, what, load, units, rhs, lo=0, wide=256, h_before=None):
                w = arrived(l, what, load)[:, 0:KB * wide].rearrange("p (k n) -> p k n", k=KB)
                for j, u in enumerate(units):
                    dst = free_pair(l, what, u)
                    last = project(dst, w, rhs, KB, 128 * j, 128, lo, h_before=h_before)
                    last.then_inc(gemm_out, 1)

            def sum_squares(l, what, n0, n, mat, lo=0):
                dst = free_pair(l, what, n0)
                first = number(SQUARES, l, what, 0 if n > 1 else n0)
                for k in range(n):
                    pe.wait_ge(sq_ready, first + k + 1)
                    sq = square_buffer(what, k if n > 1 else n0, first + k)
                    for a, b in streams(lo):
                        last = mm(dst[:, CTX + a:CTX + b], mat, sq[:, a:b], start=(k == 0), stop=(k == n - 1))
                    last.then_inc(sq_used, 1)

            pe.wait_ge(const_in, 16)
            pe.wait_ge(x_in, 32)
            xt = Hm[:, :, :].rearrange("p a b -> p (a b)").rearrange("p (c f) -> p c f", c=NC)
            for i in range(2 * NC):
                if i >= 4:
                    pe.wait_ge(xT_evac, i - 3)
                for j in range(4):
                    f0 = 512 * (i % 2) + 128 * j
                    last = tr(ps[:, i % 4, 128 * j:128 * j + 128], xt[:, i // 2, f0:f0 + 128], ident)
                last.then_inc(xT_ready, 1)
            for l, s_in, s_out in ((0, rows_in, vT_ready), (1, rows1_in, vT1_ready)):
                pe.wait_ge(s_in, 16 * 14)
                for i in (2 * l, 2 * l + 1):
                    last = tr(ps[:, 5 + l, 128 * (i % 2):128 * (i % 2) + 128], rows[:, i, :], ident)
                last.then_inc(s_out, 1)

            def ada_half(g, half, w, dst):
                for k in range(4):
                    last = mm(dst, cs[:, 4 * half + k, :], w[:, k, :], start=(half == 0 and k == 0), stop=(half == 1 and k == 3))
                return last

            def ada_columns(g, row, q, col):
                pe.wait_ge(ada_row, g + 1)
                for j in range(4):
                    last = tr(ps[:, 7, col + 2 * j:col + 2 * j + 2], row[q:q + 2, 128 * j:128 * j + 128], ident[q:q + 2, q:q + 2])
                last.then_inc(ada_tr, 1)

            def ada_point(p, first):
                g = ADA_FIRST + p // 2
                if p % 2 == 1 and p > first + 1:
                    ada_finish(p - 3, first)
                q = 32 * (g % 2)
                w = arrived(0, "ada", p)
                if p % 2 == 0 and p >= first + 4:
                    pe.wait_ge(ada_row, g - 1)
                last = ada_half(g, p % 2, w.rearrange("p (k n) -> p k n", n=512), ps[q:q + 2, 6, :])
                last.then_inc(*((w_used, 1) if p % 2 == 0 else (ada_out, 1)))

            def ada_finish(p, first):
                g = ADA_FIRST + p // 2
                ada_columns(g, ring[:, LOADS.index((0, "ada", p + 1)) % NSLOT, :], 32 * (g % 2), 4 * (p - first))

            for l in range(DEPTH):
                lo = lo_of(l)
                if l == 0:
                    pe.wait_ge(cs_ready, 1)
                    pe.wait_ge(xT_evac, 2 * NC)
                    for g in range(ADA_FIRST):
                        for half in range(2):
                            pe.wait_ge(ada_in[2 * g + half], 16)
                            last = ada_half(g, half, ada_first[:, 2 * g + half, :].rearrange("p (k n) -> p k n", n=512), ps[0:2, g, :])
                        last.then_inc(ada_out, 1)
                    for g in range(ADA_FIRST):
                        ada_columns(g, ada_first[:, 2 * g + 1, :], 0, 8 * g)
                pe.wait_ge(mods_ready, l + 1)
                sum_squares(l, "norm0", 0, KB, ones)
                for i in range(4):
                    gemm(l, "qkv", i, [2 * i, 2 * i + 1], Hm, h_before=16 * l if i == 0 else None)
                dst = free_pair(l, "ba")
                w = arrived(l, "ba")[:, 0:KB * 16].rearrange("p (k n) -> p k n", k=KB)
                for ci in range(NC):
                    for k in range(KB):
                        last = mm(dst[:, 512 + 16 * ci:512 + 16 * ci + 16], Hm[:, k, 128 * ci:128 * ci + 128], w[:, k, :],
                                  start=(k == 0), stop=(k == KB - 1))
                last.then_inc(gemm_out, 1)
                gemm(l, "qkv", 4, [8, 9], Hm)
                pe.wait_ge(la_ready, l + 1)
                dst = free_pair(l, "gcum")
                for i, m in enumerate((tri[0], tri[1], ones)):
                    last = mm(dst[:, 512 + 48 * i:512 + 48 * i + 48], m, gd[:, 1, :], start=True, stop=True)
                last.then_inc(gemm_out, 1)
                for u in range(4):
                    sum_squares(l, "l2", u, 1, ones)
                gemm(l, "qkv", 5, [10, 11], Hm)
                for u in range(4, 8):
                    sum_squares(l, "l2", u, 1, ones)
                pe.wait_ge(l2_done, 8 * (l + 1))
                pe.wait_ge(silu_done, 12 * (l + 1))
                for what, src in (("ktr", kT), ("vtr", vT)):
                    for ci in range(NC):
                        dst = free_pair(l, what, ci)
                        for h in range(H):
                            last = tr(dst[:, 512 + 128 * h:512 + 128 * h + 128], src[:, h, 128 * ci:128 * ci + 128], ident)
                        last.then_inc(gemm_out, 1)
                pe.wait_ge(gs_ready, l + 1)
                pe.wait_ge(gemm_evac, number(UNITS, l, "vtr", NC - 1) + 1)

                for d in range(2):
                    base = NC * (2 * l + d)
                    for ci in range(NC):
                        if ci >= 2:
                            pe.wait_ge(p1_done, base + ci - 1)
                        elif d == 1:
                            pe.wait_ge(o_evac, o_count(l, 0, NC - 1))
                        if l == 0:
                            ada_point(2 * NC * d + ci, 0)
                        G, KK, QK = (3 * (ci % 2) + j for j in range(3))
                        cc = slice(128 * ci, 128 * ci + 128)
                        for h in range(H):
                            mm(ps[:, G, 128 * h:128 * h + 128], la[:, ci, d, h:h + 1].to_broadcast([128, 128]), tri[d], start=True, stop=True)
                        for h in range(H):
                            mm(ps[:, KK, 128 * h:128 * h + 128], kT[:, h, cc], kT[:, h, cc], start=True, stop=True)
                        for h in range(H):
                            last = mm(ps[:, QK, 128 * h:128 * h + 128], kT[:, h, cc], qT[:, h, cc], start=True, stop=True)
                        last.then_inc(p1_out, 1)
                    tb = 7 * NC * (2 * l + d)
                    cb = 6 * NC * (2 * l + d)
                    steps = [(lv, ci) for lv in range(7) for ci in range(NC)]
                    pe.wait_ge(p1_done, base + NC)

                    def c_product(i):
                        lv, ci = steps[i]
                        j = i - NC
                        pe.wait_ge(t_ready, tb + i - NC + 1)
                        if j >= 2:
                            pe.wait_ge(c_evac, cb + j - 1)
                        for h in range(H):
                            last = mm(ps[:, j % 2, 128 * h:128 * h + 128], N_[:, ci, h, :], TT[:, ci, h, :], start=True, stop=True)
                        last.then_inc(c_out, 1)
                    for i, (lv, ci) in enumerate(steps):
                        if i == NC - 1:
                            c_product(NC)
                        elif i >= NC and i + 1 < len(steps):
                            c_product(i + 1)
                        B, BT = 2 + 2 * (i % 2), 3 + 2 * (i % 2)
                        if i >= 2:
                            pe.wait_ge(t_ready, tb + i - 1)
                        if lv == 0:
                            for h in range(H):
                                last = tr(ps[:, BT, 128 * h:128 * h + 128], N_[:, ci, h, :], ident)
                        else:
                            j = i - NC
                            pe.wait_ge(c_evac, cb + j + 1)
                            for h in range(H):
                                last = mm(ps[:, BT, 128 * h:128 * h + 128], T_[:, ci, h, :], Csb[j % 2][:, h, :], start=True, stop=True)
                            if lv < 6:
                                for h in range(H):
                                    last = mm(ps[:, B, 128 * h:128 * h + 128], Csb[j % 2][:, h, :], T_[:, ci, h, :], start=True, stop=True)
                        last.then_inc(b_out, 1)
                    pe.wait_ge(t_ready, tb + 7 * NC)
                    for ci in range(NC):
                        if ci >= 2:
                            pe.wait_ge(eg_exp, base + ci - 1)
                            pe.wait_ge(wt_ready, base + ci - 1)
                        G, W = 2 * (ci % 2), 2 * (ci % 2) + 1
                        for h in range(H):
                            mm(ps[:, G, 128 * h:128 * h + 128], la[:, ci, d, h:h + 1].to_broadcast([128, 128]), tri[d], start=True, stop=True)
                        pe.wait_ge(kbg_ready, base + ci + 1)
                        for h in range(H):
                            last = mm(ps[:, W, 128 * h:128 * h + 128], kbg[ci % 2][:, h, :], TT[:, ci, h, :], start=True, stop=True)
                        last.then_inc(w_out_s, 1)
                    pe.wait_ge(eg_exp, base + NC)
                    pe.wait_ge(wt_ready, base + NC)
                    pe.wait_ge(qd_ready, base + NC)
                    for n, ci in enumerate(order(d)):
                        if l == 0:
                            ada_point(2 * NC * d + NC + n, 0)
                        V, U, O = n % 2, 2 + n % 2, 4 + n % 2
                        pe.wait_ge(vb_ready, base + n + 1)
                        if n:
                            pe.wait_ge(s_ready, (NC - 1) * (2 * l + d) + n)
                        for h in range(H):
                            o = ps[:, V, 128 * h:128 * h + 128]
                            last = mm(o, TT[:, ci, h, :], vb[n % 2][:, h, :], start=True, stop=(n == 0))
                            if n:
                                last = mm(o, N_[:, ci, h, :], s_of(n - 1)[:, h, :], start=False, stop=True)
                        last.then_inc(v_out, 1)
                        pe.wait_ge(vn_ready, base + n + 1)
                        if n < NC - 1:
                            pe.wait_ge(kend_ready, (NC - 1) * (2 * l + d) + n + 1)
                            for h in range(H):
                                last = mm(ps[:, U, 128 * h:128 * h + 128], kend[n % 2][:, h, :], VN[n % 2][:, h, :], start=True, stop=True)
                            last.then_inc(u_out, 1)
                        if ci in chunks_out(l):
                            k = o_count(l, d, n)
                            if k > o_count(l, d, -1) + 2:
                                pe.wait_ge(o_evac, k - 2)
                            for h in range(H):
                                o = ps[:, O, 128 * h:128 * h + 128]
                                if n:
                                    mm(o, s_of(n - 1)[:, h, :], T_[:, ci, h, :], start=True, stop=False)
                                last = mm(o, VN[n % 2][:, h, :], att[:, ci, h, :], start=(n == 0), stop=True)
                            last.then_inc(o_out, 1)
                if l == 0:
                    ada_finish(2 * ADA_GDN - 2, 0)
                    pe.wait_ge(ada_read, 1)
                pe.wait_ge(o_evac, o_count(l, 1, NC - 1))
                for i in range(2):
                    gemm(l, "gate", i, [2 * i, 2 * i + 1], Hm, lo)
                for u in range(4):
                    sum_squares(l, "grms", u, 1, ones, lo)
                for i in range(2):
                    gemm(l, "hq", i, [2 * i, 2 * i + 1], Hm)
                for i in range(4):
                    gemm(l, "hf", i, [2 * i, 2 * i + 1], Hm)
                w = arrived(l, "hi").rearrange("p (k n) -> p k n", k=KB)
                for ci in range(NC):
                    dst = free_pair(l, "hi", ci)
                    for k in range(KB):
                        last = mm(dst[:, 512:768], Hm[:, k, 128 * ci:128 * ci + 128], w[:, k, :], start=(k == 0), stop=(k == KB - 1))
                    last.then_inc(gemm_out, 1)
                gemm(l, "hgate", 0, [0, 1], Hm, lo)
                pe.wait_ge(gemm_evac, number(UNITS, l, "hgate", 1) + 1)

                for d in range(2):
                    lvb = NLV * (2 * l + d)
                    bank = 0
                    if d == 1:
                        pe.wait_ge(ho_evac, o_count(l, 0, NC - 1))
                    pe.wait_ge(k_done, 2 * l + d + 1)
                    for m in range(-2, 16):
                        if m >= 0:
                            pe.wait_ge(m_ready, 16 * (2 * l + d) + m + 1)
                            M = m_piece(d, m).rearrange("p (h t) -> p h t", h=H)
                            if l == 0 and m % 2 == 0:
                                ada_point(2 * ADA_GDN + 8 * d + m // 2, 2 * ADA_GDN)
                        for ci in range(3 * (m % 2), 3 * (m % 2) + 3):
                            cc, mc = slice(128 * ci, 128 * ci + 128), slice(128 * (ci % 3), 128 * (ci % 3) + 128)
                            if bank >= 6:
                                pe.wait_ge(lv_evac, lvb + bank - 5)
                            for h in range(H):
                                o = ps[:, bank % 6, 128 * h:128 * h + 128]
                                if m < 0:
                                    last = mm(o, HK[d][:, h, cc], HQ[:, h, cc], start=True, stop=True)
                                elif m < 14:
                                    last = mm(o, M[:, h, mc], M[:, h, mc], start=True, stop=True)
                                else:
                                    last = tr(o, M[:, h, mc], ident)
                            last.then_inc(lv_out, 1)
                            bank += 1
                    KE = chunks(3 if d == 0 else 5)
                    pe.wait_ge(lv_evac, lvb + NLV)
                    for n, ci in enumerate(order(d)):
                        U, O = n % 2, 2 + n % 2
                        sbase = (NC - 1) * (2 * l + d)
                        if n < NC - 1:
                            if n >= 2:
                                pe.wait_ge(hs_ready, sbase + n - 1)
                            for h in range(H):
                                last = mm(ps[:, U, 64 * h:64 * h + 64], KE[:, ci, h, :], HV[:, ci, 64 * h:64 * h + 64], start=True, stop=True)
                            last.then_inc(hu_out, 1)
                        if ci in chunks_out(l):
                            k = o_count(l, d, n)
                            if k > o_count(l, d, -1) + 2:
                                pe.wait_ge(ho_evac, k - 2)
                            if n:
                                pe.wait_ge(hs_ready, sbase + n)
                            for h in range(H):
                                p0, c0 = 64 * (h % 2), 128 * (h // 2)
                                o = ps[p0:p0 + 64, O, c0:c0 + 128]
                                if n:
                                    mm(o, S[:, (n - 1) % 2, 64 * h:64 * h + 64], HK[d][:, h, 128 * ci:128 * ci + 128], start=True, stop=False)
                                last = mm(o, HV[:, ci, 64 * h:64 * h + 64], HATT[:, ci, h, :], start=(n == 0), stop=True)
                            last.then_inc(ho_out, 1)
                if l == 0:
                    ada_finish(2 * (ADA_GDN + ADA_HGRN) - 2, 2 * ADA_GDN)
                    pe.wait_ge(ada_read, 2)
                pe.wait_ge(ho_evac, o_count(l, 1, NC - 1))
                for u in range(2):
                    sum_squares(l, "hrms", u, 1, bd64, lo)

                gemm(l, "cq", 0, [0, 1], Hm)
                w = arrived(l, "ckv")[:, 0:KB * 160].rearrange("p (k n) -> p k n", k=KB)
                project(free_pair(l, "ckv"), w, Hm, KB, 0, 128).then_inc(gemm_out, 1)
                project(free_pair(l, "kr"), w, Hm, KB, 64, 96).then_inc(gemm_out, 1)
                sum_squares(l, "cqsum", 0, 2, ones)
                sum_squares(l, "ckvsum", 0, 1, ones)
                dst = free_pair(l, "krrot")
                pe.wait_ge(gemm_evac, number(UNITS, l, "kr") + 1)
                mm(dst[0:96, 512:1024], rotp[0:96, 0:96], KR0[0:96, CTX:TOK], start=True, stop=True).then_inc(gemm_out, 1)
                pe.wait_ge(cn_ready, 3 * l + 3)
                w = arrived(l, "uq")[:, 0:768].rearrange("p (k n) -> p k n", k=2)
                for h in range(H):
                    last = project(free_pair(l, "uq", h), w, CQ, 2, 96 * h, 96)
                    last.then_inc(gemm_out, 1)
                for h in range(H):
                    dst = free_pair(l, "qrot", h)
                    pe.wait_ge(gemm_evac, number(UNITS, l, "uq", h) + 1)
                    mm(dst[0:96, 512:1024], rotp[0:96, 0:96], QH[0:96, h, CTX:TOK], start=True, stop=True).then_inc(gemm_out, 1)
                w = arrived(l, "ukv")[:, 0:512].rearrange("p (k n) -> p k n", k=1)
                for h in range(H):
                    project(free_pair(l, "uk", h), w, CKV.unsqueeze(1), 1, 128 * h, 64).then_inc(gemm_out, 1)
                wv = arrived(l, "ukv")[:, 0:512].rearrange("p (h n) -> p h n", h=H)
                for ci in range(NC):
                    dst = free_pair(l, "vt", ci)
                    mm(dst[:, 512:768].rearrange("p (h n) -> p h n", h=H), CKV[:, 128 * ci:128 * ci + 128], wv[:, :, 64:128],
                       start=True, stop=True).then_inc(gemm_out, 1)
                pe.wait_ge(gemm_evac, number(UNITS, l, "vt", NC - 1) + 1)
                pe.wait_ge(rope_done, 5 * (l + 1))
                pe.wait_ge(kr_copied, l + 1)
                steps = att_steps(l)

                def scores(i):
                    qt, h = steps[i]
                    a = ATT0[l] + i
                    if i >= 2:
                        pe.wait_ge(pe_ready, a - 1)
                    dst = ps[:, 2 * (i % 2):2 * (i % 2) + 2, :].rearrange("p a b -> p (a b)")
                    for s0, s1 in ([(0, CTX)] if qt < NCC else [(0, CTX), (CTX, TOK)]):
                        last = mm(dst[:, CTX + s0:CTX + s1], QH[0:96, h, 128 * qt:128 * qt + 128], KH[0:96, h, s0:s1], start=True, stop=True)
                    last.then_inc(sc_out, 1)

                def output(i):
                    qt, h = steps[i]
                    a, nk, p0 = ATT0[l] + i, (NCC if qt < NCC else NC), 64 * (h % 2)
                    pe.wait_ge(pt_ready, a + 1)
                    if i >= 2:
                        pe.wait_ge(pv_evac, a - 1)
                    for ck in range(nk):
                        last = mm(ps[p0:p0 + 64, 6 + i % 2, 0:128], VT[:, ck, 64 * h:64 * h + 64], PT[i % 2][:, 128 * ck:128 * ck + 128],
                                  start=(ck == 0), stop=(ck == nk - 1))
                    last.then_inc(pv_out, 1)

                scores(0)
                scores(1)
                for i, (qt, h) in enumerate(steps):
                    a, nk = ATT0[l] + i, (NCC if qt < NCC else NC)
                    if i + 2 < len(steps):
                        scores(i + 2)
                    pe.wait_ge(p_ready, a + 1)
                    if i >= 1:
                        pe.wait_ge(pt_ready, a)
                    dst = ps[:, 4:6, :].rearrange("p a b -> p (a b)")
                    for ck in range(nk):
                        last = tr(dst[:, CTX + 128 * ck:CTX + 128 * ck + 128], P_[i % 2][:, 128 * ck:128 * ck + 128], ident)
                    last.then_inc(pt_out, 1)
                    if i >= 1:
                        output(i - 1)
                output(len(steps) - 1)
                pe.wait_ge(pv_evac, ATT0[l + 1])
                pe.wait_ge(y_ready, 6 * (l + 1))
                for i in range(4):
                    if i == 0:
                        pe.wait_ge(y_parts_early, 7 * (l + 1))
                    else:
                        pe.wait_ge(out_low_ready, 3 * l + i)
                    high, low = (z.rearrange("p (k n) -> p k n", k=KB) for z in (out_w_high[i], ring_r[:, slot(l, "out", i), :]))
                    for u in (2 * i, 2 * i + 1):
                        dst = free_pair(l, "out", u)
                        m = slice(128 * (u % 2), 128 * (u % 2) + 128)
                        for k in (0, 1, 2, 3, 6, 7, 4, 5):
                            if u == 0 and k in (4, 5):
                                pe.wait_ge(y_parts_late, 2 * l + k - 3)
                            for w, part_of in ((high, "low"), (high, "high"), (low, "high")):
                                r = Y_r[:, k, :] if part_of == "low" else y_high[k]
                                for a, b in streams(lo):
                                    last = mm(dst[:, CTX + a:CTX + b], w[:, k, m], r[:, a:b],
                                              start=(k == 0 and part_of == "low"), stop=(k == 5 and w is low))
                        last.then_inc(gemm_out, 1)
                sum_squares(l, "norm1", 0, KB, ones, lo)
                sum_squares(l, "norm2", 0, KB, ones, lo)
                for j in range(32):
                    what, i = mlp_load(j)
                    pe.wait_ge(w_low_ready, 32 * l + j + 1)
                    high = w_high[j % 2].rearrange("p (k n) -> p k n", k=KB)
                    low = ring_r[:, slot(l, what, i), :].rearrange("p (k n) -> p k n", k=KB)
                    for u in (2 * i, 2 * i + 1):
                        dst = free_pair(l, what, u)
                        m = slice(128 * (u % 2), 128 * (u % 2) + 128)
                        for k in range(KB):
                            if j == 0 and u == 0:
                                pe.wait_ge(h_low_ready, 8 * l + k + 1)
                            if what == "mlp2" and u % 8 == 0:
                                pe.wait_ge(hid_ready, FB * l + u + k + 1)
                            r_high, r_low = (Y_r[:, k, :], Hm_r[:, k, :]) if what == "mlp1" else (hid_high[:, k, :], hid_low[:, k, :])
                            for w, r in ((high, r_low), (high, r_high), (low, r_high)):
                                for a, b in streams(lo):
                                    last = mm(dst[:, CTX + a:CTX + b], w[:, k, m], r[:, a:b],
                                              start=(k == 0 and r is r_low), stop=(k == KB - 1 and w is low))
                        last.then_inc(gemm_out, 1)
                sum_squares(l, "norm3", 0, KB, ones, lo)
            pe.wait_ge(x_ready, 16 * DEPTH)
            for i in range(2 * SEQ // 128):
                if i >= 4:
                    pe.wait_ge(out_evac, i - 3)
                t0 = CTX + 128 * (i // 2)
                for j in range(4):
                    last = tr(ps[:, i % 4, 128 * j:128 * j + 128], X[:, 4 * (i % 2) + j, t0:t0 + 128], ident)
                last.then_inc(out_tr, 1)

        @block.scalar
        def _(act):
            af = nc.scalar.activation
            count = [0]

            def link(ins):
                count[0] += 1
                ins.then_inc(act_step, 1)
                act.wait_ge(act_step, count[0])

            def finished(l, what, i=0):
                act.wait_ge(gemm_out, out_number(l, what, i))
                return pair(number(UNITS, l, what, i))

            def copied(l, what, i, ins):
                ins.then_inc(gemm_evac, 1)
                assert next_unit[0] == number(UNITS, l, what, i), (what, i)
                next_unit[0] += 1
            next_unit = [0]

            def square(l, what, i, src, lo=0):
                n = number(SQUARES, l, what, i)
                if what[:4] != "norm":
                    act.wait_ge(sq_used, n - 3)
                af(square_buffer(what, i, n)[:, lo:], src, ACT.Square).then_inc(sq_ready, 1)

            def roots_used(n):
                l, k = divmod(n, len(ROOTS))
                what, i = ROOTS[k]
                if what in ("norm0", "norm2"):
                    return xn_ready, 8 * (2 * l + (1 if what == "norm0" else 2))
                if what in ("norm1", "norm3"):
                    return x_ready, 16 * l + (8 if what == "norm1" else 16)
                if what == "l2":
                    return l2_done, 8 * l + i + 1
                if what in ("grms", "hrms"):
                    return y_ready, 6 * l + i + 1 + (4 if what == "hrms" else 0)
                return cn_ready, 3 * l + (2 if what == "cqsum" else 3)

            def inverse_root(l, what, i, width, n, lo=0, bias=None):
                first = number(SQUARES, l, what, i)
                act.wait_ge(sq_used, first + n)
                r, u = number(ROOTS, l, what, i), number(UNITS, l, what, i)
                if r >= 2:
                    act.wait_ge(*roots_used(r - 2))
                o = root_buffer(what, r)[:, lo:]
                copied(l, what, i, af(o, tokens(pair(u), lo), ACT.Ln, bias=eps_col, scale=1.0 / width))
                act.wait_ge(gemm_evac, u + 1)
                af(o, o, ACT.Exp, bias=zero_col if bias is None else bias, scale=-0.5).then_inc(rs_ready, 1)

            def out_high_part(l, i):
                n = LOADS.index((l, "out", i))
                act.wait_ge(w_in_s[n % NSLOT], 16 * (n // NSLOT + 1))
                af(out_w_high[i], ring[:, n % NSLOT, :], ACT.Copy).then_inc(out_high_ready, 1)

            def high_part(l, j):
                n = LOADS.index((l, *mlp_load(j)))
                act.wait_ge(w_in_s[n % NSLOT], 16 * (n // NSLOT + 1))
                if j >= 2:
                    act.wait_ge(*weights_used(LOADS.index((l, *mlp_load(j - 2)))))
                af(w_high[j % 2], ring[:, n % NSLOT, :], ACT.Copy).then_inc(w_high_ready, 1)

            def take_and_square(l, what, norm, lo):
                for b in range(KB + 1):
                    if b < KB:
                        copied(l, what, b, af(Hm[:, b, lo:], tokens(finished(l, what, b), lo), ACT.Copy))
                    if what == "out" and b in (0, 3):
                        out_high_part(l, 2 if b == 0 else 3)
                    if b == KB - 2:
                        high_part(l, 0)
                    if b:
                        act.wait_ge(gemm_evac, number(UNITS, l, what, b - 1) + 1)
                        square(l, norm, b - 1, Hm[:, b - 1, lo:], lo)

            def modulate(l, w, A, B):
                for b in range(KB):
                    act.wait_ge(xn_ready, 8 * (2 * l + w) + b + 1)
                    for a, e, s in segments(0 if w == 0 else lo_of(l)):
                        if w == 1:
                            af(Y_r[:, b, a:e], Hm[:, b, a:e], ACT.Identity, bias=B[:, b, s:s + 1], scale=A[:, b, s:s + 1])
                        last = af(Hm[:, b, a:e], Hm[:, b, a:e], ACT.Identity, bias=B[:, b, s:s + 1], scale=A[:, b, s:s + 1])
                    last.then_inc(h_ready, 1)

            act.wait_ge(rows_clear, 1)
            load_rows(act, 0, rows_in)
            for i in range(2 * NC):
                act.wait_ge(xT_ready, i + 1)
                af(X[:, 4 * (i % 2):4 * (i % 2) + 4, 128 * (i // 2):128 * (i // 2) + 128],
                   ps[:, i % 4, :].rearrange("p (b t) -> p b t", b=4), ACT.Copy).then_inc(xT_evac, 1)
            act.wait_ge(consts_ready, 1)
            act.wait_ge(lb_v, 1)
            af(lbt[:, 0:2, :], lbt[:, 0:2, :], ACT.Exp, bias=zero_col).then_inc(lb_a, 1)
            act.wait_ge(vecs_ready, 1)
            af(cs[:, :, :].rearrange("p k s -> p s k"), vecs[:, 1, V_C:V_C + 16].rearrange("p (s k) -> p s k", s=2),
               ACT.Silu, bias=zero_col).then_inc(cs_ready, 1)
            def ada_rows(g, row, q, bank):
                act.wait_ge(ada_out, g + 1)
                af(row[q:q + 2, 0:512], ps[q:q + 2, bank, :], ACT.Copy).then_inc(ada_row, 1)

            def ada_point(p, first):
                if p % 2 == 0 and p > first:
                    g = ADA_FIRST + p // 2 - 1
                    ada_rows(g, ring[:, LOADS.index((0, "ada", p - 1)) % NSLOT, :], 32 * (g % 2), 6)
            for g in range(ADA_FIRST):
                ada_rows(g, ada_first[:, 2 * g + 1, :], 0, g)
            act.wait_ge(xT_evac, 2 * NC)

            for l in range(DEPTH):
                lo = lo_of(l)
                for b in range(KB):
                    if l:
                        act.wait_ge(x_ready, 16 * l - 8 + b + 1)
                    square(l, "norm0", b, X[:, b, :])
                inverse_root(l, "norm0", 0, D, KB)
                modulate(l, 0, A1, mods[:, l, 0:8, :])
                act.wait_ge(pads_ready, l + 1)

                def padded(u):
                    z = finished(l, "qkv", u)
                    if u >= 2:
                        act.wait_ge(conv_done, 12 * l + u - 1)
                    af(zpad[u % 2][:, 2:2 + CTX], z[:, CTX:2 * CTX], ACT.Copy)
                    copied(l, "qkv", u, af(zpad[u % 2][:, CTX + 4:TOK + 4], z[:, 2 * CTX:CTX + TOK], ACT.Copy))

                def silu(u):
                    act.wait_ge(conv_done, 12 * l + u + 1)
                    dst = (qT, kT, vT)[u // 4][:, u % 4, :]
                    af(dst[:, 0:CTX], cacc[u % 2][:, 0:CTX], ACT.Silu, bias=zero_col)
                    af(dst[:, CTX:TOK], cacc[u % 2][:, CTX + 2:TOK + 2], ACT.Silu, bias=zero_col).then_inc(silu_done, 1)
                for u in range(8):
                    padded(u)
                    if u:
                        silu(u - 1)
                copied(l, "ba", 0, af(ba[:, :, :], finished(l, "ba")[:, 512:608].rearrange("p (c n) -> p c n", c=NC), ACT.Copy))
                silu(7)
                padded(8)
                act.wait_ge(la_v, l + 1)
                act.wait_ge(vec_in, 32 * (l + 1))
                af(gd[:, 0, :].rearrange("p (c n) -> p c n", c=NC), ba[:, :, 0:8], ACT.Exp, bias=zero_col, scale=-1.0)
                link(af(gd[:, 6, :], gd[:, 9, :], ACT.Abs, bias=zero_col))
                link(af(gd[:, 6, :], gd[:, 6, :], ACT.Exp, bias=zero_col, scale=-1.0))
                link(af(gd[:, 6, :], gd[:, 6, :], ACT.Ln, bias=one_col))
                af(alog[:, :], alog[:, :], ACT.Exp, bias=zero_col).then_inc(la_a, 1)
                act.wait_ge(silu_done, 12 * l + 8)
                qk = [(qT, kT)[u // 4][:, u % 4, :] for u in range(8)]
                for u in range(4):
                    square(l, "l2", u, qk[u])
                padded(9)
                silu(8)
                silu(9)
                copied(l, "gcum", 0, af(S[:, 0, 0:144], finished(l, "gcum")[:, 512:656], ACT.Copy))
                act.wait_ge(gs_v, l + 1)
                af(gd[:, 4, :], gd[:, 2, :], ACT.Exp, bias=zero_col)
                af(gd[:, 5, :], gd[:, 3, :], ACT.Exp, bias=zero_col)
                af(gd[:, 6, :], gd[:, 6, :], ACT.Exp, bias=zero_col).then_inc(gs_a, 1)
                for u in range(4):
                    inverse_root(l, "l2", u, 1, 1, bias=lnq_col)
                    square(l, "l2", u + 4, qk[u + 4])
                padded(10)
                padded(11)
                silu(10)
                silu(11)
                for u in range(4, 8):
                    inverse_root(l, "l2", u, 1, 1)
                for what, dst in (("ktr", ktok), ("vtr", vtok)):
                    for ci in range(NC):
                        src = finished(l, what, ci)[:, 512:1024].rearrange("p (h d) -> p h d", h=H)
                        copied(l, what, ci, af(dst[:, ci], src, ACT.Copy))
                for d in range(2):
                    base = NC * (2 * l + d)
                    for ci in range(NC):
                        if l == 0:
                            ada_point(2 * NC * d + ci, 0)
                        act.wait_ge(p1_exp_in, base + ci + 1)
                        af(T_[:, ci % 2], T_[:, ci % 2], ACT.Exp, bias=zero_col)
                        af(TT[:, ci % 2], TT[:, ci % 2], ACT.Exp, bias=zero_col).then_inc(p1_exp, 1)
                    bb, cb = 7 * NC * (2 * l + d), 6 * NC * (2 * l + d)
                    for j in range(6 * NC):
                        act.wait_ge(c_out, cb + j + 1)
                        if j >= 2:
                            act.wait_ge(b_out, bb + NC + j - 1)
                        af(Csb[j % 2], ps[:, j % 2, :].rearrange("p (h d) -> p h d", h=H), ACT.Copy).then_inc(c_evac, 1)
                    for ci in range(NC):
                        act.wait_ge(w_out_s, base + ci + 1)
                        G, W = 2 * (ci % 2), 2 * (ci % 2) + 1
                        af(T_[:, ci], ps[:, G, :].rearrange("p (h d) -> p h d", h=H), ACT.Exp, bias=zero_col).then_inc(eg_exp, 1)
                        af(N_[:, ci], ps[:, W, :].rearrange("p (h d) -> p h d", h=H), ACT.Copy, scale=-1.0).then_inc(wt_ready, 1)
                    for n in range(NC):
                        if l == 0:
                            ada_point(2 * NC * d + NC + n, 0)
                        act.wait_ge(v_out, base + n + 1)
                        af(VN[n % 2], ps[:, n % 2, :].rearrange("p (h d) -> p h d", h=H), ACT.Copy).then_inc(vn_ready, 1)
                if l == 0:
                    ada_point(2 * ADA_GDN, 0)
                for u in range(4):
                    copied(l, "gate", u, af(GT[:, u, lo:], tokens(finished(l, "gate", u), lo), ACT.Silu, bias=zero_col))
                act.wait_ge(o_evac, o_count(l, 1, NC - 1))
                for u in range(4):
                    square(l, "grms", u, Y[:, u, lo:], lo)
                for u in range(4):
                    inverse_root(l, "grms", u, 128, 1, lo)
                for u in range(4):
                    copied(l, "hq", u, af(HQ[:, u, :], tokens(finished(l, "hq", u)), ACT.Copy, scale=128 ** -0.5))
                for u in range(4):
                    copied(l, "hf", u, af(HK[0][:, u, :], tokens(finished(l, "hf", u)), ACT.Copy))
                act.wait_ge(gemm_evac, number(UNITS, l, "hf", 3) + 1)
                af(HB[0], HK[0], ACT.Exp, bias=zero_col, scale=-1.0).then_inc(f_exp, 1)
                for u in range(4, 8):
                    copied(l, "hf", u, af(HK[1][:, u - 4, :], tokens(finished(l, "hf", u)), ACT.Copy))
                act.wait_ge(k_done, 2 * l + 1)
                af(HB[0], HB[0], ACT.Ln, bias=tiny_col).then_inc(lf_done, 1)
                act.wait_ge(gemm_evac, number(UNITS, l, "hf", 7) + 1)
                act.wait_ge(y_ready, 6 * l + 4)
                af(HB[1], HK[1], ACT.Exp, bias=zero_col, scale=-1.0).then_inc(f_exp, 1)
                for ci in range(NC):
                    copied(l, "hi", ci, af(HV[:, ci, :], finished(l, "hi", ci)[:, 512:768], ACT.Copy))
                for u in range(2):
                    copied(l, "hgate", u, af(HGT[:, u, lo:], tokens(finished(l, "hgate", u), lo), ACT.Silu, bias=zero_col))
                act.wait_ge(k_done, 2 * l + 2)
                af(HB[1], HB[1], ACT.Ln, bias=tiny_col).then_inc(lf_done, 1)
                for d in range(2):
                    for m in range(16):
                        act.wait_ge(md_ready, 16 * (2 * l + d) + m + 1)
                        M, wide = m_piece(d, m), level(d, m)[0]
                        if m < 14:
                            v = M.rearrange("p (n e s) -> p n e s", e=2, s=wide // 2)
                            low = -1.0 if d == 0 else 1.0
                            af(v[:, :, 0, :], v[:, :, 0, :], ACT.Exp, bias=zero_col, scale=low)
                            af(v[:, :, 1, :], v[:, :, 1, :], ACT.Exp, bias=zero_col, scale=-low).then_inc(me_ready, 1)
                        else:
                            af(M, M, ACT.Exp, bias=zero_col, scale=-1.0).then_inc(me_ready, 1)
                        if l == 0 and m % 2 == 1:
                            ada_point(2 * ADA_GDN + 8 * d + m // 2, 2 * ADA_GDN)
                    b4 = HB[d].rearrange("p h (c t) -> p h c t", t=128)
                    link(af(ebl[:, :, :], b4[:, :, :, 127 if d == 0 else 0], ACT.Exp, bias=zero_col))
                    af(HB[d], HB[d], ACT.Exp, bias=zero_col).then_inc(eb_ready, 1)
                if l == 0:
                    ada_point(2 * (ADA_GDN + ADA_HGRN), 2 * ADA_GDN)
                act.wait_ge(ho_evac, o_count(l, 1, NC - 1))
                for u in range(2):
                    square(l, "hrms", u, Y[:, 6 + u, lo:], lo)
                for u in range(2):
                    inverse_root(l, "hrms", u, 64, 1, lo)
                act.wait_ge(y_ready, 6 * l + 6)
                for u in range(2):
                    copied(l, "cq", u, af(CQ[:, u, :], tokens(finished(l, "cq", u)), ACT.Copy))
                copied(l, "ckv", 0, af(CKV, tokens(finished(l, "ckv")), ACT.Copy))
                copied(l, "kr", 0, af(KR0[0:96], tokens(finished(l, "kr"))[0:96], ACT.Copy))
                act.wait_ge(gemm_evac, number(UNITS, l, "kr") + 1)
                for u in range(2):
                    square(l, "cqsum", u, CQ[:, u, :])
                square(l, "ckvsum", 0, CKV)
                inverse_root(l, "cqsum", 0, 256, 2)
                inverse_root(l, "ckvsum", 0, 128, 1)
                copied(l, "krrot", 0, af(KROT[0:96], finished(l, "krrot")[0:96, 512:1024], ACT.Copy))
                for h in range(H):
                    copied(l, "uq", h, af(QH[0:96, h, :], tokens(finished(l, "uq", h))[0:96], ACT.Copy))
                for h in range(H):
                    copied(l, "qrot", h, af(ROT[0:96, h, 0:SEQ], finished(l, "qrot", h)[0:96, 512:1024], ACT.Copy))
                for h in range(H):
                    copied(l, "uk", h, af(KH[0:64, h, :], tokens(finished(l, "uk", h))[0:64], ACT.Copy))
                for ci in range(NC):
                    copied(l, "vt", ci, af(VT[:, ci, :], finished(l, "vt", ci)[:, 512:768], ACT.Copy))
                act.wait_ge(rope_done, 5 * (l + 1))
                out_high_part(l, 0)
                steps = att_steps(l)

                def keys_of(i):
                    return CTX if steps[i][0] < NCC else TOK

                def probabilities(i):
                    a = ATT0[l] + i
                    act.wait_ge(mx_ready, a + 1)
                    if i >= 2:
                        act.wait_ge(pt_out, a - 1)
                    s = ps[:, 2 * (i % 2):2 * (i % 2) + 2, :].rearrange("p a b -> p (a b)")
                    af(P_[i % 2][:, 0:keys_of(i)], s[:, CTX:CTX + keys_of(i)], ACT.Exp, bias=sm[:, i % 2:i % 2 + 1], scale=96 ** -0.5,
                       accum_out=sm[:, 2 + i % 2:3 + i % 2]).then_inc(pe_ready, 1)

                def take_output(i):
                    qt, h = steps[i]
                    a, p0 = ATT0[l] + i, 64 * (h % 2)
                    act.wait_ge(pv_out, a + 1)
                    af(Y[p0:p0 + 64, 4 + h // 2, 128 * qt:128 * qt + 128], ps[p0:p0 + 64, 6 + i % 2, 0:128], ACT.Copy).then_inc(pv_evac, 1)

                probabilities(0)
                for i in range(len(steps)):
                    a = ATT0[l] + i
                    if i + 1 < len(steps):
                        probabilities(i + 1)
                    act.wait_ge(pt_out, a + 1)
                    if i >= 2:
                        act.wait_ge(pv_out, a - 1)
                    t = ps[:, 4:6, :].rearrange("p a b -> p (a b)")
                    af(PT[i % 2][:, 0:keys_of(i)], t[:, CTX:CTX + keys_of(i)], ACT.Copy).then_inc(pt_ready, 1)
                    if i:
                        take_output(i - 1)
                take_output(len(steps) - 1)
                act.wait_ge(pt_ready, ATT0[l + 1])
                act.wait_ge(pv_out, ATT0[l + 1])
                out_high_part(l, 1)
                take_and_square(l, "out", "norm1", lo)
                inverse_root(l, "norm1", 0, D, KB, lo)
                high_part(l, 1)
                for b in range(KB):
                    act.wait_ge(x_ready, 16 * l + b + 1)
                    square(l, "norm2", b, X[:, b, lo:], lo)
                inverse_root(l, "norm2", 0, D, KB, lo)
                modulate(l, 1, A2, mods[:, l, 24:32, :])
                for j in range(32):
                    what, i = mlp_load(j)
                    for u in (2 * i, 2 * i + 1):
                        src, b = tokens(finished(l, what, u), lo), u % 8
                        if what == "mlp1":
                            copied(l, what, u, af(hid[:, b, lo:], src, ACT.Relu, bias=zero_col))
                        elif u < 8:
                            copied(l, what, u, af(total[:, b, lo:], src, ACT.Copy))
                        else:
                            if u >= 10:
                                act.wait_ge(sum_ready, 24 * l + u - 9)
                            copied(l, what, u, af(partial[:, b % 2, lo:], src, ACT.Copy))
                    if j + 2 < 32:
                        high_part(l, j + 2)
                    if j >= 29:
                        for b in (2 * (j - 29), 2 * (j - 29) + 1):
                            act.wait_ge(sum_ready, 24 * l + 16 + b + 1)
                            square(l, "norm3", b, Hm[:, b, lo:], lo)
                for b in (6, 7):
                    act.wait_ge(sum_ready, 24 * l + 16 + b + 1)
                    square(l, "norm3", b, Hm[:, b, lo:], lo)
                inverse_root(l, "norm3", 0, D, KB, lo)

        @block.vector
        def _(dve):
            v = nc.vector
            count = [0]

            def link(ins):
                count[0] += 1
                ins.then_inc(dve_step, 1)
                dve.wait_ge(dve_step, count[0])

            def roots(l, what, i=0):
                r = number(ROOTS, l, what, i)
                dve.wait_ge(rs_ready, r + 1)
                return root_buffer(what, r)

            def over_heads(ap):
                return ap.unsqueeze(1).to_broadcast([128, H, 128])

            def norm_input(l, what, lo):
                rs = roots(l, what)
                for b in range(KB):
                    v.tensor_tensor(Hm[:, b, lo:], X[:, b, lo:], rs[:, lo:], ALU.mult).then_inc(xn_ready, 1)

            def low_part(l, j):
                at = slot(l, *mlp_load(j))
                dve.wait_ge(w_high_ready, 32 * l + j + 1)
                v.tensor_tensor(ring_r[:, at, :], ring[:, at, :], w_high[j % 2], ALU.subtract).then_inc(w_low_ready, 1)

            def add_normed(l, what, lo, G):
                rs = roots(l, what)
                for b in range(KB):
                    link(v.tensor_tensor(Hm[:, b, lo:], Hm[:, b, lo:], rs[:, lo:], ALU.mult))
                    for a, e, s in segments(lo):
                        last = v.scalar_tensor_tensor(X[:, b, a:e], Hm[:, b, a:e], G[:, b, s:s + 1], X[:, b, a:e], ALU.mult, ALU.add)
                    last.then_inc(x_ready, 1)

            v.memset(rows, 0.0).then_inc(rows_clear, 1)
            for i, val in enumerate((EPS, 1.0, -0.5 * float(np.log(128.0)), 1e-19, 0.0)):
                last = v.memset(cst[:, i:i + 1], val)
            last.then_inc(consts_ready, 1)
            dve.wait_ge(mask_in, 16)
            v.tensor_copy(masks[:, :, :], R[:, 1, 0:15 * 128].rearrange("p (a b) -> p a b", b=128))
            dve.wait_ge(vT_ready, 1)
            v.tensor_copy(vecs[:, 0:2, :], ps[:, 5, 0:256].rearrange("p (a b) -> p a b", a=2)).then_inc(vecs_ready, 1)
            dve.wait_ge(vT1_ready, 1)
            v.tensor_copy(vecs[:, 2:4, :], ps[:, 6, 0:256].rearrange("p (a b) -> p a b", a=2)).then_inc(vecs_ready, 1)
            dve.wait_ge(vecs_ready, 2)
            l0, l1 = vecs[:, 1, V_LB:V_LB + 8], vecs[:, 1, V_LB + 8:V_LB + 16]
            link(v.tensor_tensor(lbt[:, 2, :], l0, l1, ALU.max))
            link(v.tensor_tensor(lbt[:, 0, :], l0, lbt[:, 2, :], ALU.subtract))
            v.tensor_tensor(lbt[:, 1, :], l1, lbt[:, 2, :], ALU.subtract).then_inc(lb_v, 1)
            v.memset(lb[:, 0, 0, :], 0.0)
            v.memset(lb[:, 0, 1, :], 1.0)
            dve.wait_ge(lb_a, 1)
            link(v.tensor_tensor(lbt[:, 2, :], lbt[:, 0, :], lbt[:, 1, :], ALU.add))
            link(v.reciprocal(lbt[:, 2, :], lbt[:, 2, :]))
            link(v.tensor_tensor(lb[:, 1, 0, :], lbt[:, 1, :], lbt[:, 2, :], ALU.mult))
            link(v.tensor_tensor(lb[:, 1, 1, :], lbt[:, 0, :], lbt[:, 2, :], ALU.mult))

            def add_bias(l, b0, b1, columns):
                link(v.tensor_tensor(mods[:, l, b0:b1, :], columns.rearrange("p (b s) -> p b s", s=2),
                                     vecs[:, 2 * l, b0:b1].unsqueeze(2).to_broadcast([128, b1 - b0, 2]), ALU.add))

            for l in range(DEPTH):
                lo = lo_of(l)

                def gain(dst, b0, at, plus_one):
                    g = vecs[:, 2 * l, at:at + 8].unsqueeze(2).to_broadcast([128, 8, 2])
                    m = mods[:, l, b0:b0 + 8, :]
                    return (v.scalar_tensor_tensor(dst[:, :, :], m, 1.0, g, ALU.add, ALU.mult) if plus_one
                            else v.tensor_tensor(dst[:, :, :], m, g, ALU.mult))
                if l == 0:
                    dve.wait_ge(ada_tr, ADA_FIRST)
                    add_bias(0, 0, 16, ps[:, 7, 0:32])
                gain(A1, 8, V_MIXPRE, True).then_inc(mods_ready, 1)
                norm_input(l, "norm0", 0)
                for i in range(2):
                    v.memset(zpad[i][:, 0:2], 0.0)
                    v.memset(zpad[i][:, CTX + 2:CTX + 4], 0.0)
                    last = v.memset(zpad[i][:, TOK + 4:TOK + 6], 0.0)
                last.then_inc(pads_ready, 1)

                def convolve(u):
                    dve.wait_ge(gemm_evac, number(UNITS, l, "qkv", u) + 1)
                    if u >= 2:
                        dve.wait_ge(silu_done, 12 * l + u - 1)
                    for j in range(CONV_W):
                        w = vecs[:, 2 * l + 1, V_CONV + 12 * j + u:V_CONV + 12 * j + u + 1]
                        z = zpad[u % 2][:, j:j + 770]
                        if j == 0:
                            link(v.tensor_scalar(cacc[u % 2], z, w, None, ALU.mult))
                        elif j < CONV_W - 1:
                            link(v.scalar_tensor_tensor(cacc[u % 2], z, w, cacc[u % 2], ALU.mult, ALU.add))
                        else:
                            v.scalar_tensor_tensor(cacc[u % 2], z, w, cacc[u % 2], ALU.mult, ALU.add).then_inc(conv_done, 1)

                def unit_length(u):
                    rs = roots(l, "l2", u)
                    t = (qT, kT)[u // 4][:, u % 4, :]
                    v.tensor_tensor(t, t, rs, ALU.mult).then_inc(l2_done, 1)
                for u in range(8):
                    convolve(u)
                dve.wait_ge(gemm_evac, number(UNITS, l, "ba") + 1)
                dve.wait_ge(vec_in, 32 * (l + 1))
                v.tensor_tensor(gd[:, 9, :].rearrange("p (c n) -> p c n", c=NC), ba[:, :, 8:16],
                                dtb[:, :].unsqueeze(1).to_broadcast([128, NC, 8]), ALU.add).then_inc(la_v, 1)
                convolve(8)
                dve.wait_ge(la_a, l + 1)
                link(v.tensor_scalar(gd[:, 0, :], gd[:, 0, :], 1.0, None, ALU.add))
                link(v.reciprocal(gd[:, 0, :], gd[:, 0, :]))
                link(v.scalar_tensor_tensor(gd[:, 6, :], gd[:, 9, :], 0.0, gd[:, 6, :], ALU.max, ALU.add))
                v.scalar_tensor_tensor(gd[:, 1, :].rearrange("p (c n) -> p c n", c=NC), gd[:, 6, :].rearrange("p (c n) -> p c n", c=NC),
                                       -1.0, alog[:, :].unsqueeze(1).to_broadcast([128, NC, 8]), ALU.mult, ALU.mult).then_inc(la_ready, 1)
                convolve(9)
                dve.wait_ge(gemm_evac, number(UNITS, l, "gcum") + 1)
                raw = S[:, 0, 0:144].rearrange("p (k c d h) -> p k c d h", k=3, c=NC, d=2)
                v.tensor_copy(g_[:, :, 0, :], raw[:, 0, :, 0, :])
                v.tensor_copy(g_[:, :, 1, :], raw[:, 1, :, 1, :])
                link(v.tensor_copy(gd[:, 3, :], S[:, 0, 96:144]))
                v.tensor_scalar(gd[:, 8, :], gd[:, 0, :], -1.0, None, ALU.mult)
                v.tensor_scalar(gd[:, 9, :], gd[:, 2, :], -1.0, None, ALU.mult)
                v.tensor_tensor(gd[:, 6, :], gd[:, 3, :], gd[:, 2, :], ALU.subtract).then_inc(gs_v, 1)
                dve.wait_ge(gs_a, l + 1)
                v.tensor_tensor(gd[:, 7, :], gd[:, 0, :], gd[:, 4, :], ALU.mult).then_inc(gs_ready, 1)
                for u in range(4):
                    unit_length(u)
                convolve(10)
                convolve(11)
                for u in range(4, 8):
                    unit_length(u)
                for d in range(2):
                    base = NC * (2 * l + d)

                    def exponents(ci):
                        dve.wait_ge(p1_out, base + ci + 1)
                        G = ps[:, 3 * (ci % 2), :].rearrange("p (h d) -> p h d", h=H)
                        dve.wait_ge(gmask_ready, base + ci + 1)
                        v.tensor_tensor(T_[:, ci % 2], T_[:, 2 + ci % 2], G, ALU.subtract)
                        v.tensor_tensor(TT[:, ci % 2], G, TT[:, 2 + ci % 2], ALU.add).then_inc(p1_exp_in, 1)

                    def matrices(ci):
                        dve.wait_ge(p1_exp, base + ci + 1)
                        KK, QK = 3 * (ci % 2) + 1, 3 * (ci % 2) + 2
                        for h in range(H):
                            v.scalar_tensor_tensor(N_[:, ci, h, :], ps[:, KK, 128 * h:128 * h + 128], nbeta[:, ci, d, h:h + 1],
                                                   T_[:, ci % 2, h, :], ALU.mult, ALU.mult)
                        v.tensor_tensor(att[:, ci], ps[:, QK, :].rearrange("p (h d) -> p h d", h=H), TT[:, ci % 2], ALU.mult).then_inc(p1_done, 1)
                    for ci in range(NC):
                        exponents(ci)
                        if ci:
                            matrices(ci - 1)
                    matrices(NC - 1)
                    dve.wait_ge(p1_done, base + NC)
                    eye = ident.unsqueeze(1).to_broadcast([128, NC * H, 128])
                    v.tensor_copy(R[:, 5, :].rearrange("p (n d) -> p n d", d=128), eye)
                    link(v.tensor_copy(R[:, 6, :].rearrange("p (n d) -> p n d", d=128), eye))
                    bb = 7 * NC * (2 * l + d)
                    for i in range(7 * NC):
                        lv, ci = divmod(i, NC)
                        dve.wait_ge(b_out, bb + i + 1)
                        B, BT = 2 + 2 * (i % 2), 3 + 2 * (i % 2)
                        mT = over_heads(masks[:, lv + (0 if d == 0 else 7), :])
                        mTT = over_heads(masks[:, lv + (7 if d == 0 else 0), :])
                        if lv == 0:
                            v.copy_predicated(T_[:, ci], mT, N_[:, ci])
                        elif lv < 6:
                            v.copy_predicated(T_[:, ci], mT, ps[:, B, :].rearrange("p (h d) -> p h d", h=H))
                        v.copy_predicated(TT[:, ci], mTT, ps[:, BT, :].rearrange("p (h d) -> p h d", h=H)).then_inc(t_ready, 1)
                    for n, ci in enumerate(order(d)):
                        if n < NC - 1:
                            k = (NC - 1) * (2 * l + d) + n
                            dve.wait_ge(u_out, k + 1)
                            U = ps[:, 2 + n % 2, :].rearrange("p (h d) -> p h d", h=H)
                            if n == 0:
                                v.tensor_copy(s_of(0), U).then_inc(s_ready, 1)
                            else:
                                dve.wait_ge(s_ready, k)
                                for h in range(H):
                                    last = v.scalar_tensor_tensor(s_of(n)[:, h, :], s_of(n - 1)[:, h, :], egl[:, ci, d, h:h + 1], U[:, h, :], ALU.mult, ALU.add)
                                last.then_inc(s_ready, 1)
                        if ci in chunks_out(l):
                            dve.wait_ge(o_out, o_count(l, d, n))
                            O = ps[:, 4 + n % 2, :].rearrange("p (h d) -> p h d", h=H)
                            y = Y[:, 0:4, 128 * ci:128 * ci + 128]
                            if d == 0:
                                v.tensor_copy(y, O).then_inc(o_evac, 1)
                            else:
                                v.tensor_tensor(y, y, O, ALU.add).then_inc(o_evac, 1)

                def gated(what, u, y, gain, gate):
                    rs = roots(l, what, u)
                    link(v.tensor_tensor(y, y, rs[:, lo:], ALU.mult))
                    v.scalar_tensor_tensor(y, y, gain, gate, ALU.mult, ALU.mult).then_inc(y_ready, 1)
                if l == 0:
                    dve.wait_ge(ada_tr, ADA_FIRST + ADA_GDN)
                    add_bias(0, 16, 48, ps[:, 7, 0:64])
                    add_bias(1, 0, 16, ps[:, 7, 64:96])
                    v.tensor_copy(cst[:, 5:6], mods[:, 1, 15, 0:1]).then_inc(ada_read, 1)
                gain(A2, 32, V_MLPPRE, True)
                gain(G1, 16, V_MIXPOST, False)
                link(gain(G2, 40, V_MLPPOST, False))
                dve.wait_ge(gemm_evac, number(UNITS, l, "gate", 3) + 1)
                for u in range(4):
                    gated("grms", u, Y[:, u, lo:], vecs[:, 2 * l + 1, V_GN:V_GN + 1], GT[:, u, lo:])
                for d in range(2):
                    dve.wait_ge(f_exp, 2 * l + d + 1)
                    link(v.tensor_scalar(HB[d], HB[d], 1.0, None, ALU.add))
                    link(v.reciprocal(HB[d], HB[d]))
                    for h in range(H):
                        q = 4 * d + h
                        last = v.tensor_scalar(HB[d][:, h, :], HB[d][:, h, :], lb[:, l, 1, q:q + 1], lb[:, l, 0, q:q + 1], ALU.mult, ALU.add)
                    link(last)
                    v.tensor_scalar(HK[d], HB[d], -1.0, 1.0, ALU.mult, ALU.add).then_inc(k_done, 1)
                    dve.wait_ge(lf_done, 2 * l + d + 1)
                    for h in range(H):
                        for ci in range(NC):
                            a = HB[d][:, h, 128 * ci:128 * ci + 128]
                            if d == 1:
                                a = a[:, ::-1]
                            last = v.tensor_tensor_scan(a, ones, a, 0.0, ALU.mult, ALU.add)
                    last.then_inc(b_done, 1)

                def queries_keys(d, m):
                    wide = level(d, m)[0]
                    dve.wait_ge(me_ready, 16 * (2 * l + d) + m + 1)
                    kk, qq = part(HK[d], m), part(HQ, m)
                    if m < 14:
                        m5 = m_piece(d, m).rearrange("p (h n e s) -> p h n e s", h=H, e=2, s=wide // 2)
                        k5, q5 = (z.rearrange("p h (n e s) -> p h n e s", e=2, s=wide // 2) for z in (kk, qq))
                        low, high = (k5, q5) if d == 0 else (q5, k5)
                        v.tensor_tensor(m5[:, :, :, 0, :], m5[:, :, :, 0, :], low[:, :, :, 0, :], ALU.mult)
                        v.tensor_tensor(m5[:, :, :, 1, :], m5[:, :, :, 1, :], high[:, :, :, 1, :], ALU.mult).then_inc(m_ready, 1)
                    else:
                        M = m_piece(d, m).rearrange("p (h t) -> p h t", h=H)
                        v.tensor_tensor(M, M, kk, ALU.mult).then_inc(m_ready, 1)

                queries_keys(0, 0)
                queries_keys(0, 1)
                for d in range(2):
                    lvb = NLV * (2 * l + d)
                    bank = 0
                    KE = chunks(3 if d == 0 else 5)
                    for m in range(-2, 16):
                        if 0 <= m < 14:
                            queries_keys(d, m + 2)
                        if m == 14:
                            dve.wait_ge(eb_ready, 2 * l + d + 1)
                            dve.wait_ge(m_ready, 16 * (2 * l + d) + 16)
                            v.tensor_tensor(HK[d], HQ, HB[d], ALU.mult).then_inc(hqd_ready, 1)
                            dve.wait_ge(hqd_ready, 2 * l + d + 1)
                        for ci in range(3 * (m % 2), 3 * (m % 2) + 3):
                            dve.wait_ge(lv_out, lvb + bank + 1)
                            o = ps[:, bank % 6, :].rearrange("p (h d) -> p h d", h=H)
                            if m < 0:
                                v.tensor_tensor(HATT[:, ci], o, over_heads(ident), ALU.mult).then_inc(lv_evac, 1)
                            elif m < 14:
                                dve.wait_ge(lv_evac, lvb + bank - NC + 1)
                                mask = over_heads(masks[:, m // 2 + (7 if d == 0 else 0), :])
                                v.copy_predicated(HATT[:, ci], mask, o).then_inc(lv_evac, 1)
                            else:
                                v.tensor_copy(KE[:, ci], o).then_inc(lv_evac, 1)
                            bank += 1
                    if d == 0:
                        queries_keys(1, 0)
                        queries_keys(1, 1)
                    for n, ci in enumerate(order(d)):
                        if n < NC - 1:
                            k = (NC - 1) * (2 * l + d) + n
                            dve.wait_ge(hu_out, k + 1)
                            U = ps[:, n % 2, 0:256]
                            if n == 0:
                                v.tensor_copy(S[:, 0, 0:256], U).then_inc(hs_ready, 1)
                            else:
                                dve.wait_ge(hs_ready, k)
                                if n >= 2 and o_count(l, d, n - 1) > o_count(l, d, -1):
                                    dve.wait_ge(ho_out, o_count(l, d, n - 1))
                                for h in range(H):
                                    e = slice(64 * h, 64 * h + 64)
                                    last = v.scalar_tensor_tensor(S[:, n % 2, e], S[:, (n - 1) % 2, e], ebl[:, h, ci:ci + 1], U[:, e], ALU.mult, ALU.add)
                                last.then_inc(hs_ready, 1)
                        if ci in chunks_out(l):
                            dve.wait_ge(ho_out, o_count(l, d, n))
                            O = ps[:, 2 + n % 2, 0:256].rearrange("p (b t) -> p b t", b=2)
                            y = Y[:, 6:8, 128 * ci:128 * ci + 128]
                            if d == 0:
                                v.tensor_copy(y, O).then_inc(ho_evac, 1)
                            else:
                                v.tensor_tensor(y, y, O, ALU.add).then_inc(ho_evac, 1)
                if l == 0:
                    dve.wait_ge(ada_tr, GROUPS)
                    add_bias(1, 16, 48, ps[:, 7, 0:64])
                    v.tensor_copy(cst[:, 5:6], mods[:, 1, 47, 0:1]).then_inc(ada_read, 1)
                for u in range(2):
                    gated("hrms", u, Y[:, 6 + u, lo:], vecs[:, 2 * l + 1, V_HN:V_HN + 1], HGT[:, u, lo:])
                rs = roots(l, "cqsum")
                for u in range(2):
                    v.scalar_tensor_tensor(CQ[:, u, :], CQ[:, u, :], vecs[:, 2 * l + 1, V_QN + u:V_QN + u + 1], rs, ALU.mult, ALU.mult).then_inc(cn_ready, 1)
                rs = roots(l, "ckvsum")
                v.scalar_tensor_tensor(CKV, CKV, vecs[:, 2 * l + 1, V_KVN:V_KVN + 1], rs, ALU.mult, ALU.mult).then_inc(cn_ready, 1)
                dve.wait_ge(rope_in, 16 * (l + 1))
                cos, sin = COS[64:96], SIN[64:96]

                def rotate(dst, src, rot):
                    link(v.tensor_tensor(rot, rot, sin, ALU.mult))
                    link(v.tensor_tensor(dst, src, cos, ALU.mult))
                    v.tensor_tensor(dst, dst, rot, ALU.add).then_inc(rope_done, 1)
                dve.wait_ge(gemm_evac, number(UNITS, l, "krrot") + 1)
                v.tensor_copy(KR[64:96, 0:CTX], KR0[64:96, 0:CTX])
                rotate(KR[64:96, CTX:TOK], KR0[64:96, CTX:TOK], KROT[64:96])
                for h in range(H):
                    dve.wait_ge(gemm_evac, number(UNITS, l, "qrot", h) + 1)
                    q = QH[64:96, h, CTX:TOK]
                    rotate(q, q, ROT[64:96, h, 0:SEQ])
                steps = att_steps(l)

                def maximum(i):
                    a = ATT0[l] + i
                    nk = CTX if steps[i][0] < NCC else TOK
                    dve.wait_ge(sc_out, a + 1)
                    s = ps[:, 2 * (i % 2):2 * (i % 2) + 2, :].rearrange("p a b -> p (a b)")
                    link(v.reduce_max(sm[:, 4 + i % 2:5 + i % 2], s[:, CTX:CTX + nk], axis=AX.X))
                    v.tensor_scalar(sm[:, i % 2:i % 2 + 1], sm[:, 4 + i % 2:5 + i % 2], -(96 ** -0.5), None, ALU.mult).then_inc(mx_ready, 1)
                maximum(0)
                for i in range(len(steps)):
                    a = ATT0[l] + i
                    nk = CTX if steps[i][0] < NCC else TOK
                    if i + 1 < len(steps):
                        maximum(i + 1)
                    dve.wait_ge(pe_ready, a + 1)
                    link(v.reciprocal(sm[:, 6 + i % 2:7 + i % 2], sm[:, 2 + i % 2:3 + i % 2]))
                    p = P_[i % 2][:, 0:nk]
                    v.tensor_scalar(p, p, sm[:, 6 + i % 2:7 + i % 2], None, ALU.mult).then_inc(p_ready, 1)
                dve.wait_ge(pv_evac, ATT0[l + 1])
                for b in (4, 5):
                    link(v.tensor_copy(y_high[b][:, lo:], Y[:, b, lo:]))
                    v.tensor_tensor(Y_r[:, b, lo:], Y[:, b, lo:], y_high[b][:, lo:], ALU.subtract).then_inc(y_parts_late, 1)
                for i in (1, 2, 3):
                    at = slot(l, "out", i)
                    dve.wait_ge(out_high_ready, 4 * l + i + 1)
                    v.tensor_tensor(ring_r[:, at, :], ring[:, at, :], out_w_high[i], ALU.subtract).then_inc(out_low_ready, 1)
                low_part(l, 0)
                add_normed(l, "norm1", lo, G1)
                dve.wait_ge(x_ready, 16 * l + 8)
                rs = roots(l, "norm2")
                for b in range(KB + 2):
                    if b < KB:
                        v.tensor_tensor(Hm[:, b, lo:], X[:, b, lo:], rs[:, lo:], ALU.mult).then_inc(xn_ready, 1)
                    if b >= 2:
                        dve.wait_ge(h_ready, 8 * (2 * l + 1) + b - 1)
                        v.tensor_tensor(Hm_r[:, b - 2, lo:], Hm[:, b - 2, lo:], Y_r[:, b - 2, lo:], ALU.subtract).then_inc(h_low_ready, 1)
                low_part(l, 1)
                for j in range(32):
                    what, i = mlp_load(j)
                    for u in (2 * i, 2 * i + 1):
                        b = u % 8
                        if what == "mlp2" and u < 8:
                            continue
                        dve.wait_ge(gemm_evac, number(UNITS, l, what, u) + 1)
                        if what == "mlp1":
                            z = hid[:, b, lo:]
                            v.tensor_tensor(hid_high[:, b, lo:], z, z, ALU.mult)
                            link(v.tensor_tensor(z, z, z, ALU.mult))
                            v.tensor_tensor(hid_low[:, b, lo:], z, hid_high[:, b, lo:], ALU.subtract).then_inc(hid_ready, 1)
                        else:
                            if u >= 16:
                                dve.wait_ge(sum_ready, 24 * l + u - 15)
                            dst = (Hm if u >= 24 else total)[:, b, lo:]
                            v.tensor_tensor(dst, total[:, b, lo:], partial[:, b % 2, lo:], ALU.add).then_inc(sum_ready, 1)
                    if j + 2 < 32:
                        low_part(l, j + 2)
                add_normed(l, "norm3", lo, G2)
                dve.wait_ge(x_ready, 16 * l + 16)
            ot = R[:, 0:2, :].rearrange("p a b -> p (a b)")
            for i in range(2 * SEQ // 128):
                dve.wait_ge(out_tr, i + 1)
                v.tensor_copy(ot[:, 512 * i:512 * i + 512], ps[:, i % 4, :]).then_inc(out_evac, 1)


def constants():
    p, f = np.arange(128)[:, None], np.arange(128)[None, :]
    tri_f, tri_b = (p <= f).astype(np.float32), (p >= f).astype(np.float32)
    rot = np.zeros((128, 128), np.float32)
    for i in range(16):
        rot[64 + 16 + i, 64 + i] = -1.0
        rot[64 + i, 64 + 16 + i] = 1.0
    k_f32 = np.stack([np.eye(128), np.ones((128, 128)), (p // 64 == f // 64), rot, tri_f, tri_b,
                      NEG * (tri_f - 1), NEG * (tri_b - 1)], axis=1).astype(np.float32).reshape(128, -1)
    low = [((p // (2 * s) == f // (2 * s)) & ((p // s) % 2 == 1) & ((f // s) % 2 == 0)) for s in LEVELS]
    k_mask = np.stack(low + [m.T for m in low] + [p == f], axis=1).astype(np.float32).reshape(128, -1)
    inv = 10000.0 ** (-np.arange(0, 16, 2, dtype=np.float32) / np.float32(16))
    t = np.arange(SEQ)
    ang = np.concatenate([(t // 64)[:, None] * inv, (t % 64)[:, None] * inv], axis=1).astype(np.float32).T
    k_rope = np.concatenate([np.tile(np.cos(ang), (2, 1)), np.tile(np.sin(ang), (2, 1))], axis=1).astype(np.float32)
    return {"k_f32": k_f32, "k_mask": k_mask, "k_rope": k_rope}


_INS = ["x", "ctx", "c", "c_ctx", "w_ada", "b_ada", "norm_mix_pre", "norm_mix_post", "norm_mlp_pre", "norm_mlp_post",
        "w_in", "w_out", "gdn_conv", "gdn_a_log", "gdn_dt_bias", "gdn_norm", "mla_q_norm", "mla_kv_norm",
        "mla_w_uq", "mla_w_ukv", "hgrn_lb_logits", "hgrn_norm", "w_mlp1", "w_mlp2"]


def kernel(**inputs):
    import concourse.bacc as bacc
    from concourse.bass_utils import run_bass_kernel_spmd

    nc = bacc.Bacc("TRN2", target_bir_lowering=False, num_devices=1)
    arrays, args = {}, []
    for name, a in [(n, inputs[n]) for n in _INS] + list(constants().items()):
        a = np.ascontiguousarray(a)
        arrays[f"in_{name}"] = a
        args.append(nc.dram_tensor(f"in_{name}", a.shape, mybir.dt.from_np(a.dtype), kind="ExternalInput").ap())
    args.append(nc.dram_tensor("out_0", (1, SEQ, D), mybir.dt.float32, kind="ExternalOutput").ap())
    trunk_program(nc, *args)
    r = run_bass_kernel_spmd(nc, [arrays], core_ids=[0])
    return r.results[0]["out_0"]
```
